# Optimizing a Trainium2 kernel written in Bass

```python
import jax, jax.numpy as jnp
from jax import lax
import numpy as np
import math

D_MODEL = 1024
BATCH = 1
SEQ = 512
DEPTH = 2

GRID_W = 64
CTX_LEN = 256
D_MIX = D_MODEL
HEAD_DIM = 64
POOL_GROUPS = 4
POOL_WINDOWS = (2, 4, 8, 16)
POOL_DIM = D_MIX // 4
POOL_GROUP_DIM = POOL_DIM // POOL_GROUPS
NA_HEADS = (D_MIX - POOL_DIM) // 2 // HEAD_DIM
NA_DIM = NA_HEADS * HEAD_DIM
NA_KH = 8
NA_KW = 16
RET_HEADS = (D_MIX - POOL_DIM - NA_DIM) // HEAD_DIM
RET_DIM = RET_HEADS * HEAD_DIM
RET_CHUNK = 128
D_FF = 2816
CONV_W = 3
ROPE_BASE = 10000.0
ROT_QUARTER = HEAD_DIM // 4
EPS = 1e-6
NEG_INF = -1e30
IN_SIZES = (POOL_DIM, NA_DIM, NA_DIM, NA_DIM, RET_DIM, RET_DIM, RET_DIM, RET_DIM)
IN_DIM = sum(IN_SIZES)
SPLIT_POINTS = tuple(int(s) for s in np.cumsum(IN_SIZES)[:-1])


def rmsnorm(t, g):
    tf = t.astype(jnp.float32)
    y = tf * lax.rsqrt(jnp.mean(tf * tf, axis=-1, keepdims=True) + EPS) * g.astype(jnp.float32)
    return y.astype(t.dtype)

def modulate(t, shift, scale):
    return t * (1 + scale) + shift

def heads(t, n):
    return t.reshape(t.shape[0], t.shape[1], n, HEAD_DIM)

def pool_mixer(p, w_grp, scale):
    B, L, _ = p.shape
    pf = p.astype(jnp.float32).reshape(B, L, POOL_GROUPS, POOL_GROUP_DIM)
    csum = jnp.concatenate([jnp.zeros_like(pf[:, :1]), jnp.cumsum(pf, axis=1)], axis=1)
    t = jnp.arange(L)[:, None]
    win = jnp.asarray(POOL_WINDOWS, dtype=jnp.int32)[None, :]
    lo = jnp.clip(t - win // 2, 0, L)
    hi = jnp.clip(t - win // 2 + win, 0, L)
    g = jnp.arange(POOL_GROUPS)[None, :]
    total = csum[:, hi, g] - csum[:, lo, g]
    mean = total / (hi - lo).astype(jnp.float32)[None, :, :, None]
    y = jnp.einsum('blgc,gcd->blgd', mean - pf, w_grp.astype(jnp.float32))
    return (y.reshape(B, L, POOL_DIM) * scale.astype(jnp.float32)).astype(p.dtype)

def neighborhood_attention(q, k, v, kc, vc, rpb, rows):
    B, L, H, dh = q.shape
    kh = min(NA_KH, rows)
    span = 2 * NA_KW
    n_cb = GRID_W // NA_KW
    qg = (q * dh ** -0.5).reshape(B, rows, GRID_W, H, dh)
    kg = k.reshape(B, rows, GRID_W, H, dh)
    vg = v.reshape(B, rows, GRID_W, H, dh)
    qcol = np.arange(GRID_W).reshape(n_cb, NA_KW)
    win_start = np.clip(qcol - NA_KW // 2, 0, GRID_W - NA_KW)
    col_start = np.clip(np.arange(n_cb) * NA_KW - NA_KW // 2, 0, GRID_W - span)
    kcol = col_start[:, None] + np.arange(span)
    col_valid = (kcol[:, None, :] >= win_start[:, :, None]) & (kcol[:, None, :] < win_start[:, :, None] + NA_KW)
    dc_idx = np.clip(kcol[:, None, :] - qcol[:, :, None] + NA_KW - 1, 0, 2 * NA_KW - 2)
    rpb_c = rpb.astype(jnp.float32)[:, :, dc_idx]
    valid = jnp.asarray(col_valid)[:, :, None, :]

    def one_row(r):
        rs = jnp.clip(r - kh // 2, 0, rows - kh)
        qr = lax.dynamic_index_in_dim(qg, r, axis=1, keepdims=False)
        kr = lax.dynamic_slice_in_dim(kg, rs, kh, axis=1)
        vr = lax.dynamic_slice_in_dim(vg, rs, kh, axis=1)
        kb = kr[:, :, kcol]
        vb = vr[:, :, kcol]
        qb = qr.reshape(B, n_cb, NA_KW, H, dh)
        dr_idx = rs + jnp.arange(kh) - r + NA_KH - 1
        bias = rpb_c[:, dr_idx].transpose(0, 2, 3, 1, 4)
        s_loc = jnp.einsum('bnqhd,binshd->bhnqis', qb, kb).astype(jnp.float32)
        s_loc = jnp.where(valid, s_loc + bias, NEG_INF)
        s_ctx = jnp.einsum('bnqhd,bkhd->bhnqk', qb, kc).astype(jnp.float32)
        s = jnp.concatenate([s_loc.reshape(B, H, n_cb, NA_KW, kh * span), s_ctx], axis=-1)
        p = jax.nn.softmax(s, axis=-1).astype(v.dtype)
        p_loc = p[..., :kh * span].reshape(B, H, n_cb, NA_KW, kh, span)
        p_ctx = p[..., kh * span:]
        o = jnp.einsum('bhnqis,binshd->bnqhd', p_loc, vb) + jnp.einsum('bhnqk,bkhd->bnqhd', p_ctx, vc)
        return o.reshape(B, GRID_W, H, dh)

    out = lax.map(one_row, jnp.arange(rows))
    return out.transpose(1, 0, 2, 3, 4).reshape(B, L, H, dh)

def context_attention(q, k, v):
    s = jnp.einsum('bqhd,bkhd->bhqk', q * HEAD_DIM ** -0.5, k).astype(jnp.float32)
    p = jax.nn.softmax(s, axis=-1).astype(v.dtype)
    return jnp.einsum('bhqk,bkhd->bqhd', p, v)

def axial_rotary(t, cos_r, sin_r, cos_c, sin_c):
    def rot(u, cos, sin):
        u1, u2 = jnp.split(u, 2, axis=-1)
        cos = cos[None, :, None, :]
        sin = sin[None, :, None, :]
        return jnp.concatenate([u1 * cos - u2 * sin, u1 * sin + u2 * cos], axis=-1)
    tr, tc = jnp.split(t, 2, axis=-1)
    return jnp.concatenate([rot(tr, cos_r, sin_r), rot(tc, cos_c, sin_c)], axis=-1)

def retention_chunks(q, k, v, log_gamma, state, with_outputs):
    B, L, H, _ = q.shape
    n = L // RET_CHUNK
    lg = log_gamma.astype(jnp.float32)
    idx = jnp.arange(RET_CHUNK, dtype=jnp.float32)
    diff = idx[:, None] - idx[None, :]
    intra = jnp.exp(jnp.where(diff[None] >= 0, diff[None] * lg[:, None, None], -jnp.inf))
    q_dec = jnp.exp((idx + 1)[None, :] * lg[:, None])
    k_dec = jnp.exp((RET_CHUNK - 1 - idx)[None, :] * lg[:, None])
    c_dec = jnp.exp(RET_CHUNK * lg)

    def to_chunks(t):
        return t.reshape(B, n, RET_CHUNK, H, t.shape[-1]).transpose(1, 0, 3, 2, 4)

    def step(s, blk):
        qb, kb, vb = blk
        s_new = s * c_dec[None, :, None, None] + jnp.einsum('bhcd,bhce->bhde', kb * k_dec[None, :, :, None], vb)
        if not with_outputs:
            return s_new, None
        a = jnp.einsum('bhid,bhjd->bhij', qb, kb) * intra[None]
        y = jnp.einsum('bhij,bhje->bhie', a, vb) + jnp.einsum('bhid,bhde->bhie', qb, s) * q_dec[None, :, :, None]
        return s_new, y

    s_fin, ys = lax.scan(step, state, (to_chunks(q), to_chunks(k), to_chunks(v)))
    if not with_outputs:
        return None, s_fin
    return ys.transpose(1, 0, 3, 2, 4).reshape(B, L, H, v.shape[-1]), s_fin

def bidirectional_retention(q, k, v, qc, kc, vc, dec_f, dec_b, need_ctx):
    B = q.shape[0]
    s0 = jnp.zeros((B, RET_HEADS, HEAD_DIM, HEAD_DIM), jnp.float32)
    rev = lambda t: jnp.flip(t, axis=1)
    yc_f, s_f = retention_chunks(qc, kc, vc, dec_f, s0, need_ctx)
    yx_f, _ = retention_chunks(q, k, v, dec_f, s_f, True)
    yc_b, s_b = retention_chunks(rev(qc), rev(kc), rev(vc), dec_b, s0, need_ctx)
    yx_b, _ = retention_chunks(rev(q), rev(k), rev(v), dec_b, s_b, True)
    yc = yc_f + rev(yc_b) if need_ctx else None
    return yx_f + rev(yx_b), yc

def retention_output(y, gate, gn_g):
    B, L = y.shape[:2]
    mu = jnp.mean(y, axis=-1, keepdims=True)
    var = jnp.mean((y - mu) ** 2, axis=-1, keepdims=True)
    yn = ((y - mu) * lax.rsqrt(var + EPS)).reshape(B, L, RET_DIM) * gn_g.astype(jnp.float32)
    return (jax.nn.silu(gate.astype(jnp.float32)) * yn).astype(gate.dtype)

def mixing_layer(px, pc, pool_w, pool_scale, na_rpb, dec_f, dec_b, gn_g, rope, rows, need_ctx):
    B, L, _ = px.shape
    xs = jnp.split(px, SPLIT_POINTS, axis=-1)
    cs = jnp.split(pc, SPLIT_POINTS, axis=-1)
    f32 = jnp.float32
    pool_x = pool_mixer(xs[0], pool_w, pool_scale)
    na_q, na_k, na_v = [heads(t, NA_HEADS) for t in xs[1:4]]
    nc_q, nc_k, nc_v = [heads(t, NA_HEADS) for t in cs[1:4]]
    na_x = neighborhood_attention(na_q, na_k, na_v, nc_k, nc_v, na_rpb, rows).reshape(B, L, NA_DIM)
    rq = axial_rotary(heads(xs[4], RET_HEADS).astype(f32), *rope)
    rk = axial_rotary(heads(xs[5], RET_HEADS).astype(f32), *rope) * HEAD_DIM ** -0.5
    rv = heads(xs[6], RET_HEADS).astype(f32)
    cq = heads(cs[4], RET_HEADS).astype(f32)
    ck = heads(cs[5], RET_HEADS).astype(f32) * HEAD_DIM ** -0.5
    cv = heads(cs[6], RET_HEADS).astype(f32)
    ret_x, ret_c = bidirectional_retention(rq, rk, rv, cq, ck, cv, dec_f, dec_b, need_ctx)
    ret_x = retention_output(ret_x, xs[7], gn_g)
    yx = jnp.concatenate([pool_x, na_x.astype(px.dtype), ret_x.astype(px.dtype)], axis=-1)
    if not need_ctx:
        return yx, None
    pool_c = pool_mixer(cs[0], pool_w, pool_scale)
    na_c = context_attention(nc_q, nc_k, nc_v).reshape(B, pc.shape[1], NA_DIM)
    ret_c = retention_output(ret_c, cs[7], gn_g)
    yc = jnp.concatenate([pool_c, na_c.astype(pc.dtype), ret_c.astype(pc.dtype)], axis=-1)
    return yx, yc

def conv_ffn(h, w_up, conv_w, conv_b, w_down):
    u = h @ w_up
    up = jnp.pad(u, ((0, 0), (1, 1), (0, 0)))
    u = up[:, :-2] * conv_w[0] + up[:, 1:-1] * conv_w[1] + up[:, 2:] * conv_w[2] + conv_b
    a, b = jnp.split(u, 2, axis=-1)
    return (jax.nn.silu(a) * b) @ w_down

def first_inputs(seed: int = 0) -> dict:
    key = jax.random.key(seed)
    ks = jax.random.split(key, 24)
    f32 = jnp.float32
    nrm = lambda k, shape, s: jax.random.normal(k, shape, f32) * s
    exps_f = 5.0 + jnp.arange(RET_HEADS, dtype=f32)[None, :] + 0.25 * jax.random.uniform(ks[11], (DEPTH, RET_HEADS), f32)
    exps_b = 5.0 + jnp.arange(RET_HEADS, dtype=f32)[None, :] + 0.25 * jax.random.uniform(ks[12], (DEPTH, RET_HEADS), f32)
    return {
        "x": nrm(ks[0], (BATCH, SEQ, D_MODEL), 1.0),
        "c": nrm(ks[1], (BATCH, D_MODEL), 1.0),
        "ctx": nrm(ks[2], (BATCH, CTX_LEN, D_MODEL), 1.0),
        "c_ctx": nrm(ks[3], (D_MODEL,), 1.0),
        "w_mod": nrm(ks[4], (DEPTH, D_MODEL, 6 * D_MODEL), 0.5 * D_MODEL ** -0.5),
        "b_mod": nrm(ks[5], (DEPTH, 6 * D_MODEL), 0.02),
        "norm1_g": 1.0 + nrm(ks[6], (DEPTH, D_MODEL), 0.02),
        "w_in": nrm(ks[7], (DEPTH, D_MODEL, IN_DIM), D_MODEL ** -0.5),
        "pool_w": nrm(ks[8], (DEPTH, POOL_GROUPS, POOL_GROUP_DIM, POOL_GROUP_DIM), POOL_GROUP_DIM ** -0.5),
        "pool_scale": 1.0 + nrm(ks[9], (DEPTH, POOL_DIM), 0.1),
        "na_rpb": nrm(ks[10], (DEPTH, NA_HEADS, 2 * NA_KH - 1, 2 * NA_KW - 1), 0.1),
        "ret_decay_fwd": jnp.log1p(-jnp.exp2(-exps_f)),
        "ret_decay_bwd": jnp.log1p(-jnp.exp2(-exps_b)),
        "ret_gn_g": 1.0 + nrm(ks[13], (DEPTH, RET_DIM), 0.02),
        "w_out": nrm(ks[14], (DEPTH, D_MIX, D_MODEL), D_MIX ** -0.5),
        "norm2_g": 1.0 + nrm(ks[15], (DEPTH, D_MODEL), 0.02),
        "w_up": nrm(ks[16], (DEPTH, D_MODEL, 2 * D_FF), D_MODEL ** -0.5),
        "conv_w": nrm(ks[17], (DEPTH, CONV_W, 2 * D_FF), CONV_W ** -0.5),
        "conv_b": nrm(ks[18], (DEPTH, 2 * D_FF), 0.02),
        "w_down": nrm(ks[19], (DEPTH, D_FF, D_MODEL), D_FF ** -0.5),
        "final_g": 1.0 + nrm(ks[20], (D_MODEL,), 0.02),
    }

def first_block(x, c, ctx, c_ctx, w_mod, b_mod, norm1_g, w_in, pool_w, pool_scale, na_rpb, ret_decay_fwd, ret_decay_bwd, ret_gn_g, w_out, norm2_g, w_up, conv_w, conv_b, w_down, final_g):
    B, L, _ = x.shape
    rows = L // GRID_W
    pos = jnp.arange(L)
    inv = ROPE_BASE ** (-jnp.arange(ROT_QUARTER, dtype=jnp.float32) / ROT_QUARTER)
    ang_r = (pos // GRID_W).astype(jnp.float32)[:, None] * inv[None, :]
    ang_c = (pos % GRID_W).astype(jnp.float32)[:, None] * inv[None, :]
    rope = (jnp.cos(ang_r), jnp.sin(ang_r), jnp.cos(ang_c), jnp.sin(ang_c))
    silu_c = jax.nn.silu(c)[:, None, :]
    silu_cc = jax.nn.silu(c_ctx)
    h = x
    hc = ctx
    for l in range(DEPTH):
        need_ctx = l < DEPTH - 1
        mx = jnp.split(silu_c @ w_mod[l] + b_mod[l], 6, axis=-1)
        mc = jnp.split(silu_cc @ w_mod[l] + b_mod[l], 6, axis=-1)
        ax = modulate(rmsnorm(h, norm1_g[l]), mx[0], mx[1])
        ac = modulate(rmsnorm(hc, norm1_g[l]), mc[0], mc[1])
        yx, yc = mixing_layer(ax @ w_in[l], ac @ w_in[l], pool_w[l], pool_scale[l], na_rpb[l],
                              ret_decay_fwd[l], ret_decay_bwd[l], ret_gn_g[l], rope, rows, need_ctx)
        h = h + mx[2] * (yx @ w_out[l])
        h = h + mx[5] * conv_ffn(modulate(rmsnorm(h, norm2_g[l]), mx[3], mx[4]), w_up[l], conv_w[l], conv_b[l], w_down[l])
        if need_ctx:
            hc = hc + mc[2] * (yc @ w_out[l])
            hc = hc + mc[5] * conv_ffn(modulate(rmsnorm(hc, norm2_g[l]), mc[3], mc[4]), w_up[l], conv_w[l], conv_b[l], w_down[l])
    return rmsnorm(h, final_g)


DEPTH_2 = 1

MEM_TOKENS = 256
MLA_HEADS = 8
MLA_NOPE = 64
MLA_ROPE = 32
MLA_V = 64
MLA_Q_RANK = 256
MLA_KV_RANK = 128
Q_BLOCK = 128
HY_WIDTH = D_MODEL - MLA_HEADS * MLA_V
HY_ORDER = 2
HY_DIRS = 2
HY_BANDS = 16
HY_EMB = 1 + 2 * HY_BANDS
HY_FFN = 64
HY_TARGET = 1e-2
HY_FAST_PCT = 0.3
HY_SLOW_PCT = 1.5
OFF_Q = 0
OFF_KV = OFF_Q + MLA_Q_RANK
OFF_KR = OFF_KV + MLA_KV_RANK
OFF_HY = OFF_KR + MLA_ROPE
IN_COLS = OFF_HY + 3 * HY_WIDTH
MEM_HEADS = 4
MEM_HEAD_DIM = D_MODEL // MEM_HEADS
N_GROUPS = 4
EXPERTS_PER_GROUP = 8
TOP_K_IN_GROUP = 2
D_EXPERT = 256


def _rms(x, g):
    xf = x.astype(jnp.float32)
    y = xf * lax.rsqrt(jnp.mean(xf * xf, axis=-1, keepdims=True) + EPS)
    return (y * g.astype(jnp.float32)).astype(x.dtype)

def _rope(x, cos, sin):
    x1, x2 = jnp.split(x.astype(jnp.float32), 2, axis=-1)
    return jnp.concatenate([x1 * cos - x2 * sin, x1 * sin + x2 * cos], axis=-1).astype(x.dtype)

def _mla(h_q, h_kv, h_kr, q_norm_g, kv_norm_g, w_uq, w_ukv):
    B, S, _ = h_q.shape
    q = (_rms(h_q, q_norm_g) @ w_uq).reshape(B, S, MLA_HEADS, MLA_NOPE + MLA_ROPE)
    q_nope, q_rot = q[..., :MLA_NOPE], q[..., MLA_NOPE:]
    kv = (_rms(h_kv, kv_norm_g) @ w_ukv).reshape(B, S, MLA_HEADS, MLA_NOPE + MLA_V)
    k_nope, v = kv[..., :MLA_NOPE], kv[..., MLA_NOPE:]
    pos = jnp.arange(S, dtype=jnp.float32)
    half = MLA_ROPE // 2
    inv = ROPE_BASE ** (-jnp.arange(half, dtype=jnp.float32) / half)
    ang = pos[:, None] * inv[None, :]
    cos, sin = jnp.cos(ang), jnp.sin(ang)
    q_rot = _rope(q_rot, cos[:, None, :], sin[:, None, :])
    k_rot = _rope(h_kr, cos, sin)
    scale = (MLA_NOPE + MLA_ROPE) ** -0.5
    nb = S // Q_BLOCK

    def to_blocks(t):
        return jnp.moveaxis(t.reshape(B, nb, Q_BLOCK, *t.shape[2:]), 1, 0)

    def attend(blk):
        qn, qr = blk
        s = (jnp.einsum('bqhd,bkhd->bhqk', qn, k_nope)
             + jnp.einsum('bqhr,bkr->bhqk', qr, k_rot)).astype(jnp.float32) * scale
        p = jax.nn.softmax(s, axis=-1).astype(v.dtype)
        return jnp.einsum('bhqk,bkhd->bqhd', p, v)

    o = lax.map(attend, (to_blocks(q_nope), to_blocks(q_rot)))
    return jnp.moveaxis(o, 0, 1).reshape(B, S, MLA_HEADS * MLA_V)

def _hyena_filters(L, w1, b1, freq, w2, b2, w3, b3, decay):
    f32 = jnp.float32
    t = jnp.arange(L, dtype=f32)
    t01 = t / L
    bands = jnp.linspace(1e-4, HY_BANDS - 1, HY_BANDS, dtype=f32)
    ang = 2.0 * math.pi * t[:, None] * bands[None, :] / L
    z = jnp.concatenate([t01[:, None], jnp.cos(ang), -jnp.sin(ang)], axis=-1)
    fr = freq.astype(f32)
    h = jnp.sin(fr[0] * (z @ w1.astype(f32) + b1.astype(f32)))
    h = jnp.sin(fr[1] * (h @ w2.astype(f32) + b2.astype(f32)))
    h = h @ w3.astype(f32) + b3.astype(f32)
    h = h * jnp.exp(-t01[:, None] * jnp.abs(decay.astype(f32))[None, :])
    h = h.reshape(L, HY_ORDER, HY_DIRS, HY_WIDTH)
    fwd, bwd = h[:, :, 0], h[:, :, 1]
    k = jnp.concatenate([fwd, jnp.zeros((1, HY_ORDER, HY_WIDTH), f32), bwd[:0:-1]], axis=0)
    return jnp.fft.rfft(k, axis=0)

def _hyena(u, conv_w, conv_b, kf, skip):
    B, S, _ = u.shape
    up = jnp.pad(u, ((0, 0), (1, 1), (0, 0)))
    u = up[:, :-2] * conv_w[0] + up[:, 1:-1] * conv_w[1] + up[:, 2:] * conv_w[2] + conv_b
    x1, x2, v = jnp.split(u, 3, axis=-1)
    gates = (x1, x2)
    z = v.astype(jnp.float32)
    for n in range(HY_ORDER):
        zf = jnp.fft.rfft(z, n=2 * S, axis=1)
        conv = jnp.fft.irfft(zf * kf[None, :, n], n=2 * S, axis=1)[:, :S]
        z = gates[n].astype(jnp.float32) * (conv + skip[n].astype(jnp.float32) * z)
    return z.astype(u.dtype)

def _mem_xattn(hx, hm, w_mq, w_mkv, w_mo):
    B, S, _ = hx.shape
    M = hm.shape[1]
    q = (hx @ w_mq).reshape(B, S, MEM_HEADS, MEM_HEAD_DIM)
    k, v = jnp.split(hm @ w_mkv, 2, axis=-1)
    k = k.reshape(B, M, MEM_HEADS, MEM_HEAD_DIM)
    v = v.reshape(B, M, MEM_HEADS, MEM_HEAD_DIM)
    s = jnp.einsum('bshd,bmhd->bhsm', q, k).astype(jnp.float32) * MEM_HEAD_DIM ** -0.5
    p = jax.nn.softmax(s, axis=-1).astype(v.dtype)
    o = jnp.einsum('bhsm,bmhd->bshd', p, v).reshape(B, S, MEM_HEADS * MEM_HEAD_DIM)
    return o @ w_mo

def _hier_moe(h, w_rg, b_rg, w_re, b_re, w_gate, w_up, w_down):
    B, S, D = h.shape
    t = h.reshape(B * S, D)
    g_logits = (t @ w_rg).astype(jnp.float32) + b_rg.astype(jnp.float32)
    g_prob = jax.nn.softmax(g_logits, axis=-1)
    _, g_idx = lax.top_k(g_logits, 1)
    p_group = jnp.take_along_axis(g_prob, g_idx, axis=1)
    e_logits = ((t @ w_re).astype(jnp.float32) + b_re.astype(jnp.float32)).reshape(-1, N_GROUPS, EXPERTS_PER_GROUP)
    e_in = jnp.take_along_axis(e_logits, g_idx[:, :, None], axis=1)[:, 0]
    top_v, top_i = lax.top_k(e_in, TOP_K_IN_GROUP)
    p_exp = jax.nn.softmax(top_v, axis=-1)
    w_e = jnp.sum(jax.nn.one_hot(top_i, EXPERTS_PER_GROUP, dtype=jnp.float32) * p_exp[..., None], axis=1)
    combine = ((p_group * w_e)[:, None, :]
               * jax.nn.one_hot(g_idx[:, 0], N_GROUPS, dtype=jnp.float32)[:, :, None]).astype(t.dtype)
    y = jnp.zeros_like(t)
    for g in range(N_GROUPS):
        a = jnp.einsum('td,edf->tef', t, w_gate[g])
        b = jnp.einsum('td,edf->tef', t, w_up[g])
        m = jax.nn.silu(a) * b * combine[:, g, :, None]
        y = y + jnp.einsum('tef,efd->td', m, w_down[g])
    return y.reshape(B, S, D)

def second_inputs(seed: int = 0) -> dict:
    key = jax.random.key(seed)
    ks = iter(jax.random.split(key, 40))
    f32 = jnp.float32
    L_ = DEPTH_2

    def nrm(shape, fan_in, scale=1.0):
        return jax.random.normal(next(ks), shape, f32) * (scale * fan_in ** -0.5)

    def gain(shape):
        return 1.0 + 0.02 * jax.random.normal(next(ks), shape, f32)

    def small(shape, s=0.02):
        return s * jax.random.normal(next(ks), shape, f32)

    G, E, F = N_GROUPS, EXPERTS_PER_GROUP, D_EXPERT
    d_min = math.log(1.0 / HY_TARGET) / HY_SLOW_PCT
    d_max = math.log(1.0 / HY_TARGET) / HY_FAST_PCT
    return {
        "x": jax.random.normal(next(ks), (BATCH, SEQ, D_MODEL), f32),
        "mem": jax.random.normal(next(ks), (BATCH, MEM_TOKENS, D_MODEL), f32),
        "mix_norm_g": gain((L_, D_MODEL)),
        "w_in": nrm((L_, D_MODEL, IN_COLS), D_MODEL),
        "q_norm_g": gain((L_, MLA_Q_RANK)),
        "kv_norm_g": gain((L_, MLA_KV_RANK)),
        "w_uq": nrm((L_, MLA_Q_RANK, MLA_HEADS * (MLA_NOPE + MLA_ROPE)), MLA_Q_RANK),
        "w_ukv": nrm((L_, MLA_KV_RANK, MLA_HEADS * (MLA_NOPE + MLA_V)), MLA_KV_RANK),
        "hy_conv_w": nrm((L_, 3, 3 * HY_WIDTH), 3),
        "hy_conv_b": small((L_, 3 * HY_WIDTH)),
        "hy_w1": nrm((L_, HY_EMB, HY_FFN), HY_EMB),
        "hy_b1": small((L_, HY_FFN), 0.1),
        "hy_freq": gain((L_, 2, HY_FFN)),
        "hy_w2": nrm((L_, HY_FFN, HY_FFN), HY_FFN),
        "hy_b2": small((L_, HY_FFN), 0.1),
        "hy_w3": nrm((L_, HY_FFN, HY_ORDER * HY_DIRS * HY_WIDTH), HY_FFN, 0.1),
        "hy_b3": small((L_, HY_ORDER * HY_DIRS * HY_WIDTH), 0.01),
        "hy_decay": jax.random.uniform(next(ks), (L_, HY_ORDER * HY_DIRS * HY_WIDTH), f32, d_min, d_max),
        "hy_skip": jax.random.normal(next(ks), (L_, HY_ORDER, HY_WIDTH), f32),
        "attn_out_g": gain((L_, MLA_HEADS * MLA_V)),
        "hy_out_g": gain((L_, HY_WIDTH)),
        "w_out": nrm((L_, D_MODEL, D_MODEL), D_MODEL),
        "cross_norm_g": gain((L_, D_MODEL)),
        "mem_norm_g": gain((L_, D_MODEL)),
        "w_mq": nrm((L_, D_MODEL, MEM_HEADS * MEM_HEAD_DIM), D_MODEL),
        "w_mkv": nrm((L_, D_MODEL, 2 * MEM_HEADS * MEM_HEAD_DIM), D_MODEL),
        "w_mo": nrm((L_, MEM_HEADS * MEM_HEAD_DIM, D_MODEL), MEM_HEADS * MEM_HEAD_DIM),
        "ffn_norm_g": gain((L_, D_MODEL)),
        "w_route_group": nrm((L_, D_MODEL, G), D_MODEL),
        "b_route_group": small((L_, G), 0.01),
        "w_route_expert": nrm((L_, D_MODEL, G * E), D_MODEL),
        "b_route_expert": small((L_, G * E), 0.01),
        "w_gate": nrm((L_, G, E, D_MODEL, F), D_MODEL),
        "w_up": nrm((L_, G, E, D_MODEL, F), D_MODEL),
        "w_down": nrm((L_, G, E, F, D_MODEL), F),
        "final_norm_g": gain((D_MODEL,)),
    }

def second_block(x, mem, mix_norm_g, w_in, q_norm_g, kv_norm_g, w_uq, w_ukv, hy_conv_w, hy_conv_b,
              hy_w1, hy_b1, hy_freq, hy_w2, hy_b2, hy_w3, hy_b3, hy_decay, hy_skip, attn_out_g, hy_out_g,
              w_out, cross_norm_g, mem_norm_g, w_mq, w_mkv, w_mo, ffn_norm_g, w_route_group, b_route_group,
              w_route_expert, b_route_expert, w_gate, w_up, w_down, final_norm_g):
    S = x.shape[1]
    for l in range(DEPTH_2):
        h = _rms(x, mix_norm_g[l])
        p = h @ w_in[l]
        a_out = _mla(p[..., OFF_Q:OFF_KV], p[..., OFF_KV:OFF_KR], p[..., OFF_KR:OFF_HY],
                     q_norm_g[l], kv_norm_g[l], w_uq[l], w_ukv[l])
        kf = _hyena_filters(S, hy_w1[l], hy_b1[l], hy_freq[l], hy_w2[l], hy_b2[l], hy_w3[l], hy_b3[l], hy_decay[l])
        h_out = _hyena(p[..., OFF_HY:], hy_conv_w[l], hy_conv_b[l], kf, hy_skip[l])
        mixed = jnp.concatenate([_rms(a_out, attn_out_g[l]), _rms(h_out, hy_out_g[l])], axis=-1)
        x = x + mixed @ w_out[l]
        x = x + _mem_xattn(_rms(x, cross_norm_g[l]), _rms(mem, mem_norm_g[l]), w_mq[l], w_mkv[l], w_mo[l])
        x = x + _hier_moe(_rms(x, ffn_norm_g[l]), w_route_group[l], b_route_group[l], w_route_expert[l],
                          b_route_expert[l], w_gate[l], w_up[l], w_down[l])
    return _rms(x, final_norm_g)


def setup_inputs(seed=0):
    out = dict(first_inputs(seed))
    for name, value in second_inputs(seed + 1).items():
        if name != "x":
            out[name + "_2"] = value
    return out


def reference(
    x, c, ctx, c_ctx, w_mod, b_mod, norm1_g, w_in, pool_w, pool_scale, na_rpb, ret_decay_fwd,
    ret_decay_bwd, ret_gn_g, w_out, norm2_g, w_up, conv_w, conv_b, w_down, final_g, mem_2,
    mix_norm_g_2, w_in_2, q_norm_g_2, kv_norm_g_2, w_uq_2, w_ukv_2, hy_conv_w_2, hy_conv_b_2,
    hy_w1_2, hy_b1_2, hy_freq_2, hy_w2_2, hy_b2_2, hy_w3_2, hy_b3_2, hy_decay_2, hy_skip_2,
    attn_out_g_2, hy_out_g_2, w_out_2, cross_norm_g_2, mem_norm_g_2, w_mq_2, w_mkv_2, w_mo_2,
    ffn_norm_g_2, w_route_group_2, b_route_group_2, w_route_expert_2, b_route_expert_2,
    w_gate_2, w_up_2, w_down_2, final_norm_g_2,
):
    x = first_block(
        x, c, ctx, c_ctx, w_mod, b_mod, norm1_g, w_in, pool_w, pool_scale, na_rpb,
        ret_decay_fwd, ret_decay_bwd, ret_gn_g, w_out, norm2_g, w_up, conv_w, conv_b, w_down,
        final_g,
    )
    return second_block(
        x, mem_2, mix_norm_g_2, w_in_2, q_norm_g_2, kv_norm_g_2, w_uq_2, w_ukv_2, hy_conv_w_2,
        hy_conv_b_2, hy_w1_2, hy_b1_2, hy_freq_2, hy_w2_2, hy_b2_2, hy_w3_2, hy_b3_2,
        hy_decay_2, hy_skip_2, attn_out_g_2, hy_out_g_2, w_out_2, cross_norm_g_2, mem_norm_g_2,
        w_mq_2, w_mkv_2, w_mo_2, ffn_norm_g_2, w_route_group_2, b_route_group_2,
        w_route_expert_2, b_route_expert_2, w_gate_2, w_up_2, w_down_2, final_norm_g_2,
    )


_drawn_inputs = setup_inputs


def setup_inputs(seed=0):
    import zlib

    import numpy as np

    out = dict(_drawn_inputs(seed))
    spreads = {}
    factors = {'norm1_g': 3.088,
     'na_rpb': 8.0,
     'ret_gn_g': 7.065,
     'norm2_g': 2.959,
     'conv_b': 2.903,
     'q_norm_g_2': 3.444,
     'hy_freq_2': 5.769,
     'attn_out_g_2': 3.779,
     'hy_out_g_2': 3.539,
     'cross_norm_g_2': 8.0,
     'mem_norm_g_2': 8.0,
     'ffn_norm_g_2': 2.827,
     'b_route_group_2': 23.953,
     'b_route_expert_2': 14.23,
     'final_norm_g_2': 7.795}
    for name, (base, spread) in spreads.items():
        noise = np.random.default_rng([zlib.crc32(name.encode()), seed]).standard_normal(out[name].shape)
        drawn = base * np.exp(spread * noise) if base else spread * noise
        out[name] = __import__('jax').numpy.asarray(drawn.astype(out[name].dtype))
    for name, factor in factors.items():
        out[name] = (out[name] * factor).astype(out[name].dtype)
    return out
```

```python
import contextlib
import math

import numpy as np

import concourse.bass as bass
from concourse import mybir
from concourse.alu_op_type import AluOpType as ALU

F32 = mybir.dt.float32
ACT = mybir.ActivationFunctionType
AX = mybir.AxisListType.X

P = 128
D = 1024
KT = D // P
S = 512
CTX = 256
T = S + CTX
DEPTH = 2
GRID_W = 64
NEG_INF = -1e30
EPS = 1e-6
HEAD = 64
HEADS = 6
WINDOWS = (2, 4, 8, 16)
D_FF = 2816
FT = D_FF // P
STRIP = 2048
RING = 5
MLA_HEADS = 8
MEM_HEADS = 4
EXPERTS = 32
GROUPS = 4
PER_GROUP = EXPERTS // GROUPS
NFFT = 2 * S

POOL, NAQ, NAK, RQ, RK, GATE, NPX = 0, 2, 5, 8, 11, 14, 17
MQ, MKV, MKR, HY = 0, 2, 3, 4




def strip_plan():
    plan = []
    r = np.arange
    off = np.cumsum([0, 256, 384, 384, 384, 384, 384, 384, 384])
    feature = np.concatenate([r(off[i], off[i + 1]) for i in (0, 1, 2, 4, 5, 7)])
    token = np.concatenate([r(off[3], off[4]), r(off[6], off[7])])
    for l in range(DEPTH):
        for c in range(0, 6 * D, 512):
            for half in range(2):
                plan.append((("w_mod", l), r(half * 512, half * 512 + 512), r(c, c + 512)))
    for l in range(DEPTH):
        for c in range(0, NPX * P, 256):
            plan.append((("w_in", l), r(D), feature[c:c + 256]))
        for c in range(0, 768, 256):
            plan.append((("w_in", l), r(D), token[c:c + 256]))
        for c in range(0, D, 256):
            plan.append((("w_out", l), r(D), r(c, c + 256)))
        for m in range(FT):
            plan.append((("w_up", l), r(D), np.concatenate([r(m * P, m * P + P), D_FF + r(m * P, m * P + P)])))
        for c in range(0, D, P):
            for half in range(2):
                plan.append((("w_down", l), r(half * 1408, half * 1408 + 1408), r(c, c + P)))
    plan.append((("w_in_2", 0), r(D), r(0, 256)))
    plan.append((("w_in_2", 0), r(D), r(256, 416)))
    for c in range(0, 1536, 256):
        plan.append((("w_in_2", 0), r(D), 416 + r(c, c + 256)))
    plan.append((("w_uq_2", 0), r(256), r(768)))
    nope = np.concatenate([h * 128 + r(64) for h in range(MLA_HEADS)])
    plan.append((("w_ukv_2", 0), r(128), np.concatenate([nope, nope + 64])))
    for name, cols in (("w_out_2", D), ("w_mkv_2", 2 * D), ("w_mq_2", D), ("w_mo_2", D)):
        for c in range(0, cols, 256):
            plan.append(((name, 0), r(D), r(c, c + 256)))
    return plan


PLAN = strip_plan()
STRIPS = len(PLAN)
WIDTH = [len(rows) // P * len(cols) for _, rows, cols in PLAN]


def pack_strip(matrix, rows, cols):
    a = matrix[rows][:, cols]
    a = a.reshape(len(rows) // P, P, len(cols)).transpose(1, 0, 2).reshape(P, -1)
    return a


class Columns:

    def __init__(self):
        self.at, self.n = {}, 0

    def add(self, name, count):
        self.at[name] = self.n
        self.n += count

    def __getitem__(self, name):
        return self.at[name]


VEC = Columns()
for _l in range(DEPTH):
    for _name, _count in (("b_mod", 48), ("norm1_g", KT), ("norm2_g", KT), ("conv_w", 6 * FT), ("conv_b", 2 * FT),
                          ("pool_scale", 2), ("ret_gn_g", 3), ("decay_f", HEADS), ("decay_b", HEADS), ("pool_w", 128)):
        VEC.add((_name, _l), _count)
for _name, _count in (("c", 2 * KT), ("final_g", KT), ("mix_g", KT), ("q_g", 2), ("kv_g", 1), ("hy_cw", 36),
                      ("hy_cb", 12), ("attn_g", 4), ("hyout_g", 4), ("cross_g", KT), ("mem_g", KT), ("ffn_g", KT),
                      ("last_g", KT), ("hy_f", 4), ("w1", 64), ("w2", 64), ("route_b", 4 * 36)):
    VEC.add(_name, _count)


def tiles_of(v):
    return np.reshape(v, (-1, P)).T


def pack_vectors(x):
    out = np.zeros((P, VEC.n), np.float32)

    def put(name, a):
        out[:a.shape[0], VEC[name]:VEC[name] + a.shape[1]] = a

    for l in range(DEPTH):
        for name in ("b_mod", "norm1_g", "norm2_g", "conv_b", "pool_scale", "ret_gn_g"):
            put((name, l), tiles_of(x[name][l]))
        put(("conv_w", l), tiles_of(x["conv_w"][l]))
        put(("decay_f", l), np.broadcast_to(x["ret_decay_fwd"][l], (P, HEADS)))
        put(("decay_b", l), np.broadcast_to(x["ret_decay_bwd"][l], (P, HEADS)))
        w = x["pool_w"][l].reshape(2, 2, 64, 64)
        put(("pool_w", l), w.transpose(1, 2, 0, 3).reshape(P, 128))
    put("c", np.stack([tiles_of(x["c"][0]), tiles_of(x["c_ctx"])], axis=2).reshape(P, 2 * KT))
    for name, key in (("final_g", "final_g"), ("mix_g", "mix_norm_g_2"), ("q_g", "q_norm_g_2"),
                      ("kv_g", "kv_norm_g_2"), ("hy_cw", "hy_conv_w_2"), ("hy_cb", "hy_conv_b_2"),
                      ("attn_g", "attn_out_g_2"), ("hyout_g", "hy_out_g_2"), ("cross_g", "cross_norm_g_2"),
                      ("mem_g", "mem_norm_g_2"), ("ffn_g", "ffn_norm_g_2"), ("last_g", "final_norm_g_2")):
        put(name, tiles_of(x[key]))
    put("hy_f", np.stack([x["hy_b1_2"][0], x["hy_b2_2"][0], x["hy_freq_2"][0, 0], x["hy_freq_2"][0, 1]], axis=1))
    put("w1", x["hy_w1_2"][0])
    put("w2", x["hy_w2_2"][0])
    bias = np.concatenate([x["b_route_group_2"][0], x["b_route_expert_2"][0]])
    put("route_b", np.broadcast_to(np.tile(bias, 4), (P, 144)))
    return out


def constants():
    f = np.float64
    p = np.arange(P)[:, None]
    t = np.arange(S)[None, :]
    out = {}
    inv = np.zeros((P, 2, T), f)
    for g, w in enumerate(WINDOWS):
        for a, n in ((0, S), (S, CTX)):
            i = np.arange(n)
            inv[64 * (g % 2):64 * (g % 2) + 64, g // 2, a:a + n] = 1.0 / (np.clip(i - w // 2 + w, 0, n) - np.clip(i - w // 2, 0, n))
    out["pool"] = inv.reshape(P, -1)
    freq = 10000.0 ** (-np.arange(16) / 16.0)
    freq = freq.astype(np.float32)
    pos = np.arange(S)
    ang = np.stack([(pos // GRID_W).astype(np.float32)[None, :] * freq[:, None],
                    (pos % GRID_W).astype(np.float32)[None, :] * freq[:, None]]).astype(np.float32)
    within = np.arange(P) % 64
    axis, i = within // 32, within % 16
    a = ang[axis, i]
    swap = np.zeros((P, P), f)
    for q in range(P):
        first = q % 32 < 16
        swap[q + 16 if first else q - 16, q] = -1.0 if first else 1.0
    out["rope"] = np.concatenate([np.cos(a), np.sin(a), swap], axis=1)
    x = np.arange(896)[None, :] - 384 - p
    y = np.arange(896)[None, :] - 128 - p
    out["ramp"] = np.concatenate([np.maximum(x, 0), np.maximum(-x, 0), (x == 0), 256 + y[:, :640], 512 - y[:, :640]], axis=1)
    ang = (pos.astype(np.float32)[None, :] * freq[:, None]).astype(np.float32)
    ang = ang[np.arange(32) % 16]
    c96 = np.ones((P, S), f)
    s96 = np.zeros((P, S), f)
    c96[64:96], s96[64:96] = np.cos(ang), np.sin(ang)
    swap = np.zeros((P, P), f)
    for q in range(64, 96):
        first = q < 80
        swap[q + 16 if first else q - 16, q] = -1.0 if first else 1.0
    out["rope96"] = np.concatenate([c96, s96, swap], axis=1)
    n, k = np.arange(S)[:, None], np.arange(S)[None, :]
    cos = np.cos(2 * np.pi * (n * k % NFFT) / NFFT)
    sin = np.sin(2 * np.pi * (n * k % NFFT) / NFFT)
    sin[:, 0] = 1.0 - 2.0 * (np.arange(S) % 2)
    def tiled(m):
        return m.reshape(4, P, S).transpose(1, 0, 2).reshape(P, 4 * S)
    out["dft"] = np.concatenate([tiled(cos), tiled(sin), tiled(sin.T)], axis=1)
    tt = np.arange(S).astype(np.float32)
    t01 = tt / np.float32(S)
    bands = np.linspace(1e-4, 15, 16, dtype=np.float32)
    ang = (np.float32(2.0 * math.pi) * tt[:, None] * bands[None, :] / np.float32(S)).astype(np.float32)
    z = np.concatenate([t01[:, None], np.cos(ang), -np.sin(ang)], axis=1).T
    feats = np.zeros((P, 2 * S), f)
    feats[:33, :S] = z
    feats[0, S:] = -t01
    out["hyena"] = feats
    group = np.zeros((P, P))
    group[:64, :64] = group[64:, 64:] = 1.0 / 64
    w = np.full((P, 2), 2.0 / NFFT)
    w[0, 0] = 1.0 / NFFT
    rank = np.broadcast_to(np.arange(8, 0, -1)[None, :], (P, 8))
    out["base"] = np.concatenate([np.eye(P), np.ones((P, P)), group, w, rank], axis=1)
    return {k: np.ascontiguousarray(v.astype(np.float32)) for k, v in out.items()}


BASE_COLS = 3 * P + 10


def pack_bias(rpb):
    qc = np.arange(GRID_W)
    start = np.clip(qc - 8, 0, GRID_W - 16)
    kc = np.arange(GRID_W)
    valid = (kc[None, :] >= start[:, None]) & (kc[None, :] < start[:, None] + 16)
    dc = np.clip(kc[None, :] - qc[:, None] + 15, 0, 30)
    out = np.full((DEPTH, HEADS, 2, GRID_W, 15, GRID_W), NEG_INF, np.float32)
    for a in range(2):
        for s in range(1, 15):
            picked = rpb[:, :, s - a][:, :, dc]
            out[:, :, a, :, s, :] = np.where(valid, picked, np.float32(NEG_INF))
    return out.reshape(DEPTH * HEADS, P, 15 * GRID_W)


def lay_out(x):
    x = {k: np.asarray(v) for k, v in x.items()}
    out = dict(constants())
    stream = np.zeros((STRIPS, P, STRIP), np.float32)
    for i, ((name, l), rows, cols) in enumerate(PLAN):
        stream[i, :, :WIDTH[i]] = pack_strip(x[name][l], rows, cols)
    out["stream"] = stream
    experts = np.empty((EXPERTS, 3, P, STRIP), np.float32)
    for j, name in enumerate(("w_gate_2", "w_up_2")):
        w = x[name][0].reshape(EXPERTS, KT, P, 256)
        experts[:, j] = w.transpose(0, 2, 1, 3).reshape(EXPERTS, P, STRIP)
    experts[:, 2] = x["w_down_2"][0].reshape(EXPERTS, 2, P, D).transpose(0, 2, 1, 3).reshape(EXPERTS, P, STRIP)
    out["experts"] = experts
    out["vectors"] = pack_vectors(x)
    out["bias"] = pack_bias(x["na_rpb"])
    out["tokens"] = np.concatenate([x["x"][0].T.reshape(KT, P, S), x["ctx"][0].T.reshape(KT, P, CTX)], axis=2).transpose(1, 0, 2)
    out["memory"] = x["mem_2"][0].T.reshape(KT, P, 256).transpose(1, 0, 2)
    route = np.concatenate([x["w_route_group_2"][0], x["w_route_expert_2"][0]], axis=1)
    out["route"] = route.reshape(KT, P, 36).transpose(1, 0, 2)
    out["filter"] = np.concatenate([x["hy_w3_2"][0], x["hy_b3_2"]], axis=0)
    out["decay"] = x["hy_decay_2"]
    out["skip"] = np.broadcast_to(x["hy_skip_2"].reshape(1, 2 * S), (P, 2 * S))
    return {"in_" + k: np.ascontiguousarray(v) for k, v in out.items()}




class Signal:

    def __init__(self, nc, name):
        self.sem = nc.alloc_semaphore(name)
        self.base = self.n = 0

    def up(self, by=1):
        self.n += by
        return self.sem

    def at(self, k):
        return self.base + k

    def now(self):
        return self.base + self.n

    def close(self):
        self.base += self.n
        self.n = 0


def settle(engine, instruction, signal):
    instruction.then_inc(signal.up(), 1)
    engine.wait_ge(signal.sem, signal.now())


def pieces(width):
    return [(a, min(a + 512, width)) for a in range(0, width, 512)]


class Builder:
    def __init__(self, nc, t, out):
        self.nc, self.t, self.out = nc, t, out
        self.signals = {}
        alloc = lambda name, cols: nc.alloc_sbuf_tensor(name, [P, cols], F32)[:, :]
        self.h = alloc("h", KT * T).rearrange("p (k t) -> p k t", k=KT)
        self.xn = alloc("xn", KT * T)
        self.big = alloc("big", 17664)
        self.ring = alloc("ring", RING * STRIP)
        self.vec = alloc("vec", VEC.n)
        self.base = alloc("base", BASE_COLS)
        self.mods = alloc("mods", DEPTH * 2 * 48).rearrange("p (l s m) -> p l s m", l=DEPTH, s=2)
        self.gains = alloc("gains", DEPTH * 2 * 2 * KT).rearrange("p (l s n k) -> p l s n k", l=DEPTH, s=2, n=2)
        self.small = alloc("small", 128)
        self.work = alloc("work", 10900)
        self.ps = nc.alloc_psum_tensor("ps", [P, 4096], F32)[:, :]
        self.ident = self.base[:, 0:P]
        self.ones = self.base[:, P:2 * P]
        self.group = self.base[:, 2 * P:3 * P]
        self.freq_w = self.base[:, 3 * P:3 * P + 2]
        self.rank = self.base[:, 3 * P + 2:3 * P + 10]
        self.x = self.h[:, :, 0:S]
        self.issued = 0
        self.freed_at = []
        self.landed = [nc.alloc_semaphore(f"strip_landed_{i}") for i in range(RING)]
        self.done = self.sig("product_done")

    def sig(self, name):
        if name not in self.signals:
            self.signals[name] = Signal(self.nc, name)
        return self.signals[name]

    @contextlib.contextmanager
    def stage(self):
        with self.nc.Block(no_gpsimd_drain=True) as block:
            yield block
        for s in self.signals.values():
            s.close()

    def v(self, name, i=0, n=1):
        a = VEC[name] + i
        return self.vec[:, a:a + n]

    def bank(self, b, width=512, rows=P, first=0):
        return self.ps[first:first + rows, b * 512:b * 512 + width]


    def load_strips(self, sp):
        until = min(len(self.freed_at) + RING, STRIPS)
        for i in range(self.issued, until):
            if i >= RING:
                sp.wait_ge(self.done.sem, self.freed_at[i - RING])
            slot = i % RING
            sp.dma_start(self.ring[:, slot * STRIP:slot * STRIP + WIDTH[i]],
                         self.t["stream"][i, :, 0:WIDTH[i]]).then_inc(self.landed[slot], 16)
        self.issued = until

    def strip(self, pe, i):
        pe.wait_ge(self.landed[i % RING], 16 * (i // RING + 1))
        a = (i % RING) * STRIP
        return self.ring[:, a:a + WIDTH[i]]

    def drain_loads(self):
        with self.stage() as block:
            @block.sync
            def _(sp):
                for i in range(RING):
                    sp.wait_ge(self.landed[i], 16 * ((self.issued - 1 - i) // RING + 1))

    def strips_freed(self, count):
        self.freed_at += [self.done.now()] * count


    def load(self, items):
        landed = self.sig("inputs_landed")
        with self.stage() as block:
            @block.scalar
            def _(act):
                for dst, src in items:
                    act.dma_start(dst, src).then_inc(landed.up(16), 16)
                act.wait_ge(landed.sem, landed.now())

    def norm(self, dst, src, kt, width, segments, tmp, load=()):
        squared, summed, rooted = self.sig("squared"), self.sig("summed"), self.sig("rooted")
        scaled, shifted, vstep = self.sig("scaled"), self.sig("shifted"), self.sig("vector_step")
        landed = self.sig("inputs_landed")
        sq = [tmp[:, i * width:(i + 1) * width] for i in range(2)]
        rstd = tmp[:, 2 * width:3 * width]
        mean = self.ps[:, 0:width]
        with self.stage() as block:
            @block.scalar
            def _(act):
                for a, b in load:
                    act.dma_start(a, b).then_inc(landed.up(16), 16)
                for k in range(kt):
                    if k >= 2:
                        act.wait_ge(summed.sem, summed.at(k - 1))
                    act.activation(sq[k % 2], src(k), ACT.Square).then_inc(squared.up(), 1)
                act.wait_ge(summed.sem, summed.at(kt))
                act.activation(rstd, mean, ACT.Sqrt, scale=1.0 / (kt * P), bias=EPS).then_inc(rooted.up(), 1)
                done = 0
                for k in range(kt):
                    for a, b, gain, shift in segments:
                        done += 1
                        if shift is not None:
                            act.wait_ge(scaled.sem, scaled.at(done))
                            act.activation(dst(k)[:, a:b], dst(k)[:, a:b], ACT.Identity, bias=shift(k)).then_inc(shifted.up(), 1)
                if load:
                    act.wait_ge(landed.sem, landed.now())

            @block.tensor
            def _(pe):
                for k in range(kt):
                    pe.wait_ge(squared.sem, squared.at(k + 1))
                    for a, b in pieces(width):
                        mm = pe.matmul(mean[:, a:b], self.ones, sq[k % 2][:, a:b], start=k == 0, stop=k == kt - 1)
                    mm.then_inc(summed.up(), 1)

            @block.vector
            def _(dve):
                dve.wait_ge(rooted.sem, rooted.at(1))
                settle(dve, dve.reciprocal(rstd, rstd), vstep)
                for k in range(kt):
                    for a, b, gain, shift in segments:
                        dve.scalar_tensor_tensor(out=dst(k)[:, a:b], in0=src(k)[:, a:b], scalar=gain(k), in1=rstd[:, a:b],
                                                 op0=ALU.mult, op1=ALU.mult).then_inc(scaled.up(), 1)

    def project(self, units, strips, finish, banks_each=1, act_every=0):
        first = len(self.freed_at)
        done, taken_v, taken_a = self.done, self.sig("taken_by_vector"), self.sig("taken_by_scalar")
        slots = 8 // banks_each
        on_act = [act_every and i % act_every == act_every - 1 for i in range(len(units))]

        def freed(pe, i):
            j = i - slots
            if j >= 0:
                if on_act[j]:
                    pe.wait_ge(taken_a.sem, taken_a.at(sum(on_act[:j + 1])))
                else:
                    pe.wait_ge(taken_v.sem, taken_v.at(j + 1 - sum(on_act[:j + 1])))

        def place(i):
            rows0, rows, width = units[i][2]
            a = (i % slots) * banks_each * 512
            return self.ps[rows0:rows0 + rows, a:a + width]

        with self.stage() as block:
            @block.tensor
            def _(pe):
                for i, (need, pairs, _) in enumerate(units):
                    freed(pe, i)
                    w = [self.strip(pe, first + s) for s in need]
                    out = place(i)
                    for (a, b), terms in pairs(w):
                        for j, (lhs, rhs) in enumerate(terms):
                            mm = pe.matmul(out[:, a:b], lhs, rhs, start=j == 0, stop=j == len(terms) - 1)
                    mm.then_inc(done.up(), 1)
                    upto = strips if i == len(units) - 1 else min(units[i + 1][0])
                    self.strips_freed(first + upto - len(self.freed_at))

            @block.sync
            def _(sp):
                self.load_strips(sp)

            @block.vector
            def _(dve):
                for i in range(len(units)):
                    if not on_act[i]:
                        dve.wait_ge(done.sem, done.at(i + 1))
                        finish(dve, i, place(i)).then_inc(taken_v.up(), 1)

            @block.scalar
            def _(act):
                for i in range(len(units)):
                    if on_act[i]:
                        act.wait_ge(done.sem, done.at(i + 1))
                        finish(act, i, place(i)).then_inc(taken_a.up(), 1)

    def attention(self, heads, nq, width, depth, q, k, bias, v, outs, scale, tmp):
        nk = width // P
        sbanks = (width + 511) // 512
        scored, tk, biased = self.sig("scored"), self.sig("max_taken"), self.sig("biased")
        exped, normed, turned = self.sig("exponentials"), self.sig("normalised"), self.sig("turned")
        copied, valued, stored = self.sig("turned_copied"), self.sig("valued"), self.sig("stored")
        vstep, bias_in = self.sig("vector_step"), self.sig("bias_landed")
        n_out = len(outs(0))
        pbuf = [tmp[:, i * width:(i + 1) * width] for i in range(2)]
        at = 2 * width
        pt = [tmp[:, at + i * nk * nq * P:at + (i + 1) * nk * nq * P].rearrange("p (k q) -> p k q", k=nk) for i in range(2)]
        at += 2 * nk * nq * P
        gt = [tmp[:, at + i * 960:at + (i + 1) * 960] for i in range(2)]
        stat = self.small[:, 0:16].rearrange("p (a b) -> p a b", a=4)
        units = heads * nq
        spsum = [self.ps[:, i * 1024:i * 1024 + width] for i in range(2)]
        tpsum = self.ps[:, 2048:2048 + width]
        opsum = [self.ps[:, 3072 + i * 512:3072 + (i + 1) * 512] for i in range(2)]
        with self.stage() as block:
            if bias:
                @block.sync
                def _(sp):
                    for h in range(heads):
                        if h >= 2:
                            sp.wait_ge(tk.sem, tk.at((h - 1) * nq))
                        sp.dma_start(gt[h % 2], bias(h)).then_inc(bias_in.up(16), 16)
                        sp.wait_ge(bias_in.sem, bias_in.now())

            @block.tensor
            def _(pe):
                def scores(u):
                    h, i = divmod(u, nq)
                    if u >= 2:
                        pe.wait_ge(exped.sem, exped.at(u - 1))
                    for d in range(depth):
                        for a, b, keys in k(h)[d]:
                            mm = pe.matmul(spsum[u % 2][:, a:b], q(h, i)[d], keys, start=d == 0, stop=d == depth - 1)
                    mm.then_inc(scored.up(), 1)

                def values(h):
                    pe.wait_ge(copied.sem, copied.at((h + 1) * nq))
                    for n in range(n_out):
                        m = h * n_out + n
                        if m >= 2:
                            pe.wait_ge(stored.sem, stored.at(m - 1))
                        dst = outs(h)[n]
                        r0, rows = dst.base_partition(), dst.shape[0]
                        for j in range(nk):
                            mm = pe.matmul(opsum[m % 2][r0:r0 + rows, 0:nq * P], v(h, j, n), pt[h % 2][:, j, :],
                                           start=j == 0, stop=j == nk - 1)
                        mm.then_inc(valued.up(), 1)

                scores(0)
                for u in range(units):
                    if u + 1 < units:
                        scores(u + 1)
                    pe.wait_ge(normed.sem, normed.at(u + 1))
                    if u >= 1:
                        pe.wait_ge(copied.sem, copied.at(u))
                    for j in range(nk):
                        mm = pe.transpose(tpsum[:, j * P:(j + 1) * P], pbuf[u % 2][:, j * P:(j + 1) * P], self.ident)
                    mm.then_inc(turned.up(), 1)
                    if u % nq == 0 and u >= nq:
                        values(u // nq - 1)
                values(heads - 1)

            @block.vector
            def _(dve):
                def top(u):
                    h, i = divmod(u, nq)
                    b = u % 2
                    dve.wait_ge(scored.sem, scored.at(u + 1))
                    src, s = spsum[b], scale
                    if bias:
                        if i == 0:
                            dve.wait_ge(bias_in.sem, bias_in.at(16 * (h + 1)))
                        if u >= 2:
                            dve.wait_ge(turned.sem, turned.at(u - 1))
                        a = (7 - 2 * i) * GRID_W
                        dve.tensor_scalar(pbuf[b][:, 512:width], spsum[b][:, 512:width], scale, None, ALU.mult)
                        settle(dve, dve.scalar_tensor_tensor(out=pbuf[b][:, 0:512], in0=spsum[b][:, 0:512], scalar=scale,
                                                             in1=gt[h % 2][:, a:a + 512], op0=ALU.mult, op1=ALU.add), vstep)
                        src, s = pbuf[b], 1.0
                    settle(dve, dve.reduce_max(stat[:, 0, b:b + 1], src, AX), vstep)
                    dve.tensor_scalar(stat[:, 1, b:b + 1], stat[:, 0, b:b + 1], -s, None, ALU.mult).then_inc(tk.up(), 1)

                def normalise(u):
                    b = u % 2
                    dve.wait_ge(exped.sem, exped.at(u + 1))
                    settle(dve, dve.reciprocal(stat[:, 3, b:b + 1], stat[:, 2, b:b + 1]), vstep)
                    dve.tensor_scalar(pbuf[b], pbuf[b], stat[:, 3, b:b + 1], None, ALU.mult).then_inc(normed.up(), 1)

                def store(h):
                    for n in range(n_out):
                        m = h * n_out + n
                        dve.wait_ge(valued.sem, valued.at(m + 1))
                        dst = outs(h)[n]
                        r0, rows = dst.base_partition(), dst.shape[0]
                        dve.tensor_copy(dst, opsum[m % 2][r0:r0 + rows, 0:nq * P]).then_inc(stored.up(), 1)

                top(0)
                for u in range(units):
                    if u + 1 < units:
                        top(u + 1)
                    normalise(u)
                    if u % nq == min(1, nq - 1) and u >= nq:
                        store(u // nq - 1)
                store(heads - 1)

            @block.scalar
            def _(act):
                for u in range(units):
                    b = u % 2
                    act.wait_ge(tk.sem, tk.at(u + 1))
                    if not bias and u >= 2:
                        act.wait_ge(turned.sem, turned.at(u - 1))
                    src, s = (pbuf[b], 1.0) if bias else (spsum[b], scale)
                    act.activation(pbuf[b], src, ACT.Exp, bias=stat[:, 1, b:b + 1], scale=s,
                                   accum_out=stat[:, 2, b:b + 1]).then_inc(exped.up(), 1)
                    if u >= 1:
                        self._turn_copy(act, u - 1, nq, nk, turned, copied, valued, n_out, pt, tpsum)
                self._turn_copy(act, units - 1, nq, nk, turned, copied, valued, n_out, pt, tpsum)

    def _turn_copy(self, act, u, nq, nk, turned, copied, valued, n_out, pt, tpsum):
        h, i = divmod(u, nq)
        if i == 0 and h >= 2:
            act.wait_ge(valued.sem, valued.at((h - 1) * n_out))
        act.wait_ge(turned.sem, turned.at(u + 1))
        act.activation(pt[h % 2][:, :, i * P:(i + 1) * P], tpsum.rearrange("p (k q) -> p k q", k=nk), ACT.Copy).then_inc(copied.up(), 1)


    def start(self):
        landed, done = self.sig("inputs_landed"), self.sig("conditioned")
        self.cond = self.small[:, 16:32]
        with self.stage() as block:
            @block.sync
            def _(sp):
                self.load_strips(sp)

            @block.scalar
            def _(act):
                for dst, src in ((self.vec, self.t["vectors"]), (self.base, self.t["base"]), (self.h, self.t["tokens"])):
                    act.dma_start(dst, src).then_inc(landed.up(16), 16)
                act.wait_ge(landed.sem, landed.now())
                act.activation(self.cond, self.v("c", 0, 16), ACT.Silu).then_inc(done.up(), 1)
                act.wait_ge(done.sem, done.now())

    def modulation(self):
        rows = self.big[0:2, 0:DEPTH * 6 * D]
        cond = self.cond.rearrange("p (k s) -> p k s", s=2)
        units = []
        for c in range(DEPTH * 12):
            def pairs(w, c=c):
                return [((0, 512), [(cond[:, k, :], w[k // 4][:, (k % 4) * 512:(k % 4 + 1) * 512]) for k in range(KT)])]
            units.append(([2 * c, 2 * c + 1], pairs, (0, 2, 512)))

        def finish(eng, i, ps):
            return eng.tensor_copy(rows[:, i * 512:(i + 1) * 512], ps)

        self.project(units, DEPTH * 24, finish)
        turned, vstep = self.sig("turned"), self.sig("vector_step")
        n = DEPTH * 48
        ps = self.ps[:, 0:2 * n].rearrange("p (l m s) -> p l m s", l=DEPTH, s=2)
        with self.stage() as block:
            @block.tensor
            def _(pe):
                for j in range(n):
                    mm = pe.transpose(self.ps[:, 2 * j:2 * j + 2], rows[:, j * P:(j + 1) * P], self.ident[0:2, 0:2])
                mm.then_inc(turned.up(), 1)

            @block.vector
            def _(dve):
                dve.wait_ge(turned.sem, turned.at(1))
                for l in range(DEPTH):
                    for s in range(2):
                        settle(dve, dve.tensor_tensor(self.mods[:, l, s, :], ps[:, l, :, s], self.v(("b_mod", l), 0, 48), ALU.add), vstep)
                        for which, name, m in ((0, "norm1_g", 1), (1, "norm2_g", 4)):
                            dve.scalar_tensor_tensor(out=self.gains[:, l, s, which, :], in0=self.mods[:, l, s, m * KT:(m + 1) * KT],
                                                     scalar=1.0, in1=self.v((name, l), 0, KT), op0=ALU.add, op1=ALU.mult)

    def segments(self, l, which, need_ctx=True):
        shift = 0 if which == 0 else 3
        def seg(a, b, s):
            return (a, b, lambda k: self.gains[:, l, s, which, k:k + 1],
                    lambda k: self.mods[:, l, s, shift * KT + k:shift * KT + k + 1])
        return [seg(0, S, 0)] + ([seg(S, T, 1)] if need_ctx else [])

    def input_projection(self, l, need_ctx):
        xn = self.xn.rearrange("p (k t) -> p k t", k=KT)
        px = self.big[:, 0:NPX * T].rearrange("p (n t) -> p n t", n=NPX)
        pv = self.big[:, NPX * T:NPX * T + 6 * 768].rearrange("p (n c) -> p n c", n=6)
        self.px, self.pv = px, pv
        units, dst = [], []
        for m in range(NPX):
            width = T if need_ctx or NAK <= m < RQ or RK <= m < GATE else S
            def pairs(w, m=m, width=width):
                ws = w[0].rearrange("p (k c) -> p k c", k=KT)
                o = (m % 2) * P
                return [((a, b), [(ws[:, k, o:o + P], xn[:, k, a:b]) for k in range(KT)]) for a, b in pieces(width)]
            units.append(([m // 2], pairs, (0, P, width)))
            dst.append(px[:, m, 0:width])
        for c in range(3):
            for n in range(6):
                def pairs(w, n=n):
                    ws = w[0].rearrange("p (k c) -> p k c", k=KT)
                    return [((0, 256), [(xn[:, k, n * P:(n + 1) * P], ws[:, k, :]) for k in range(KT)])]
                units.append(([9 + c], pairs, (0, P, 256)))
                dst.append(pv[:, n, c * 256:(c + 1) * 256])
        def finish(eng, i, ps):
            if eng is self.nc.scalar:
                return eng.activation(dst[i], ps, ACT.Copy)
            return eng.tensor_copy(dst[i], ps)

        self.project(units, 12, finish, banks_each=2)

    def pooling(self, l, need_ctx):
        px, y = self.px, self.xn.rearrange("p (k t) -> p k t", k=KT)
        w = self.work
        inv = w[:, 0:2 * T].rearrange("p (n t) -> p n t", n=2)
        lead, gap = 8, 16
        width = lead + S + gap + CTX + lead
        buf = [[w[:, 2 * T + (5 * n + j) * width:2 * T + (5 * n + j + 1) * width] for j in range(5)] for n in range(2)]
        runs = [(0, S, lead), (S, T, lead + S + gap)] if need_ctx else [(0, S, lead)]
        landed, vstep, ready = self.sig("inputs_landed"), self.sig("vector_step"), self.sig("pooled")
        done = self.sig("product_done")
        with self.stage() as block:
            @block.sync
            def _(sp):
                sp.dma_start(inv, self.t["pool"].rearrange("p (n t) -> p n t", n=2)).then_inc(landed.up(16), 16)

            @block.vector
            def _(dve):
                dve.wait_ge(landed.sem, landed.at(16))
                for n in range(2):
                    settle(dve, dve.memset(buf[n][0], 0.0), vstep)
                    for a, b, o in runs:
                        settle(dve, dve.tensor_copy(buf[n][0][:, o:o + b - a], px[:, n, a:b]), vstep)
                    lo, hi = 1, width
                    settle(dve, dve.tensor_tensor(buf[n][1][:, 1:width], buf[n][0][:, 0:width - 1], buf[n][0][:, 1:width], ALU.add), vstep)
                    for level in range(2 + 2 * n):
                        dst = buf[n][(level + 1) % 4]
                        if level > 0:
                            src, half = buf[n][level % 4], 2 ** (level - 1)
                            settle(dve, dve.tensor_tensor(dst[:, lo + half:hi - half], src[:, lo:hi - 2 * half],
                                                          src[:, lo + 2 * half:hi], ALU.add), vstep)
                            lo, hi = lo + half, hi - half
                        group = level - 2 * n
                        if group >= 0:
                            r = slice(64 * group, 64 * group + 64)
                            for a, b, o in runs:
                                settle(dve, dve.tensor_tensor(buf[n][4][r, a:b], dst[r, o:o + b - a], inv[r, n, a:b], ALU.mult), vstep)
                    for a, b, o in runs:
                        dve.tensor_tensor(buf[n][4][:, a:b], buf[n][4][:, a:b], px[:, n, a:b], ALU.subtract).then_inc(ready.up(), 1)
                for n in range(2):
                    dve.wait_ge(done.sem, done.at(n + 1))
                    for a, b, o in runs:
                        dve.tensor_scalar(y[:, n, a:b], self.ps[:, n * 1024 + a:n * 1024 + b], self.v(("pool_scale", l), n), None, ALU.mult)

            @block.tensor
            def _(pe):
                for n in range(2):
                    pe.wait_ge(ready.sem, ready.at(len(runs) * (n + 1)))
                    for half in range(2):
                        r = slice(64 * half, 64 * half + 64)
                        for a, b, o in runs:
                            mm = pe.matmul(self.ps[r, n * 1024 + a:n * 1024 + b], self.v(("pool_w", l), 64 * n, 64)[r, :],
                                           buf[n][4][r, a:b], start=True, stop=True)
                    mm.then_inc(done.up(), 1)

    def rotate(self):
        px = self.px
        cos, sin, swap = self.work[:, 0:S], self.work[:, S:2 * S], self.work[:, 2 * S:2 * S + P]
        tmp = [self.work[:, 1152 + i * S:1152 + (i + 1) * S] for i in range(2)]
        tiles = [RQ, RQ + 1, RQ + 2, RK, RK + 1, RK + 2]
        self._rotate([px[:, m, 0:S] for m in tiles], 0, P, cos, sin, swap, tmp, self.t["rope"], self.work[:, 0:1152])

    def _rotate(self, tiles, row0, rows, cos, sin, swap, tmp, table, table_at):
        r = slice(row0, row0 + rows)
        landed, vstep, done = self.sig("inputs_landed"), self.sig("vector_step"), self.sig("product_done")
        with self.stage() as block:
            @block.sync
            def _(sp):
                sp.dma_start(table_at, table).then_inc(landed.up(16), 16)

            @block.tensor
            def _(pe):
                pe.wait_ge(landed.sem, landed.at(16))
                for i, t in enumerate(tiles):
                    pe.matmul(self.ps[r, i % 8 * 512:i % 8 * 512 + S], swap[r, r], t, start=True, stop=True).then_inc(done.up(), 1)

            @block.vector
            def _(dve):
                dve.wait_ge(landed.sem, landed.at(16))
                for i, t in enumerate(tiles):
                    dve.wait_ge(done.sem, done.at(i + 1))
                    dve.tensor_tensor(tmp[i % 2][r, :], self.ps[r, i % 8 * 512:i % 8 * 512 + S], sin[r, :], ALU.mult)
                    settle(dve, dve.tensor_tensor(t, t, cos[r, :], ALU.mult), vstep)
                    settle(dve, dve.tensor_tensor(t, t, tmp[i % 2][r, :], ALU.add), vstep)

    def neighbourhood(self, l):
        px, pv, y = self.px, self.pv, self.xn.rearrange("p (k t) -> p k t", k=KT)
        def rows(h):
            return slice(64 * (h % 2), 64 * (h % 2) + 64)
        self.attention(
            HEADS, 4, T, 1,
            q=lambda h, i: [px[rows(h), NAQ + h // 2, i * P:(i + 1) * P]],
            k=lambda h: [[(a, b, px[rows(h), NAK + h // 2, a:b]) for a, b in pieces(T)]],
            bias=lambda h: self.t["bias"][l * HEADS + h],
            v=lambda h, j, n: pv[:, j, h * 64:(h + 1) * 64],
            outs=lambda h: [y[rows(h), 2 + h // 2, 0:S]],
            scale=HEAD ** -0.5, tmp=self.work)

    def context_attention(self):
        px, pv, y = self.px, self.pv, self.xn.rearrange("p (k t) -> p k t", k=KT)
        def rows(h):
            return slice(64 * (h % 2), 64 * (h % 2) + 64)
        self.attention(
            HEADS, 2, CTX, 1,
            q=lambda h, i: [px[rows(h), NAQ + h // 2, S + i * P:S + (i + 1) * P]],
            k=lambda h: [[(0, CTX, px[rows(h), NAK + h // 2, S:T])]],
            bias=None,
            v=lambda h, j, n: pv[:, 4 + j, h * 64:(h + 1) * 64],
            outs=lambda h: [y[rows(h), 2 + h // 2, S:T]],
            scale=HEAD ** -0.5, tmp=self.work)

    def retention(self, l, need_ctx):
        px, pv, y = self.px, self.pv, self.xn.rearrange("p (k t) -> p k t", k=KT)
        w = self.work
        ramps = w[:, 0:3968]
        fwd, bwd, diag = (w[:, i * 896:(i + 1) * 896] for i in range(3))
        cfwd, cbwd = w[:, 2688:3328], w[:, 3328:3968]
        mask = [w[:, 3968 + i * 896:3968 + (i + 1) * 896] for i in range(2)]
        cmask = [w[:, 5760 + i * 640:5760 + (i + 1) * 640] for i in range(2)]
        arg, carg = w[:, 7040:7936], w[:, 7936:8576]
        aw = [w[:, 8576 + i * T:8576 + (i + 1) * T] for i in range(3)]
        qw = T if need_ctx else S
        keys = [(4, qw), (5, qw)] + [(j, S) for j in range(4)]
        n = len(keys)
        landed, vstep, argued = self.sig("inputs_landed"), self.sig("vector_step"), self.sig("argued")
        powered, masked, scored = self.sig("powered"), self.sig("masked"), self.sig("scored")
        weighed, valued, stored = self.sig("weighed"), self.sig("valued"), self.sig("stored")
        astep, carg_done = self.sig("scalar_step"), self.sig("context_powered")
        def rows(h):
            return slice(64 * (h % 2), 64 * (h % 2) + 64)
        sps = [self.ps[:, i * 1024:i * 1024 + T] for i in range(2)]
        yps = [self.ps[:, 2048 + i * 1024:2048 + i * 1024 + T] for i in range(2)]
        with self.stage() as block:
            @block.sync
            def _(sp):
                sp.dma_start(ramps, self.t["ramp"]).then_inc(landed.up(16), 16)

            @block.tensor
            def _(pe):
                def scores(u):
                    h, j = divmod(u, n)
                    tile, width = keys[j]
                    if u >= 2:
                        pe.wait_ge(weighed.sem, weighed.at(u - 1))
                    a0 = tile * P
                    for a, b in pieces(width):
                        mm = pe.matmul(sps[u % 2][:, a:b], px[rows(h), RK + h // 2, a0:a0 + P], px[rows(h), RQ + h // 2, a:b],
                                       start=True, stop=True)
                    mm.then_inc(scored.up(), 1)

                scores(0)
                for u in range(HEADS * n):
                    h, j = divmod(u, n)
                    if u + 1 < HEADS * n:
                        scores(u + 1)
                    if j == 0 and h >= 2:
                        pe.wait_ge(stored.sem, stored.at(h - 1))
                    pe.wait_ge(weighed.sem, weighed.at(u + 1))
                    tile, width = keys[j]
                    for a, b in pieces(width):
                        mm = pe.matmul(yps[h % 2][rows(h), a:b], pv[:, tile, 384 + h * 64:384 + (h + 1) * 64], aw[u % 3][:, a:b],
                                       start=j == 0, stop=j == (n - 1 if a == 0 else 1))
                    mm.then_inc(valued.up(), 1)

            @block.scalar
            def _(act):
                act.wait_ge(landed.sem, landed.at(16))
                for h in range(HEADS):
                    if h >= 2:
                        act.wait_ge(weighed.sem, weighed.at(n * (h - 1)))
                    if h >= 1:
                        act.wait_ge(masked.sem, masked.at(h))
                    act.activation(cmask[h % 2], cfwd, ACT.Exp, scale=self.v(("decay_f", l), h)).then_inc(powered.up(), 1)
                    act.activation(carg, cbwd, ACT.Exp, scale=self.v(("decay_b", l), h)).then_inc(powered.up(), 1)
                    act.wait_ge(argued.sem, argued.at(h + 1))
                    act.activation(mask[h % 2], arg, ACT.Exp).then_inc(powered.up(), 1)

            @block.vector
            def _(dve):
                dve.wait_ge(landed.sem, landed.at(16))

                def masks(h):
                    if h >= 1:
                        dve.wait_ge(powered.sem, powered.at(3 * h))
                    settle(dve, dve.tensor_scalar(arg, fwd, self.v(("decay_f", l), h), None, ALU.mult), vstep)
                    dve.scalar_tensor_tensor(out=arg, in0=bwd, scalar=self.v(("decay_b", l), h), in1=arg,
                                             op0=ALU.mult, op1=ALU.add).then_inc(argued.up(), 1)
                    dve.wait_ge(powered.sem, powered.at(3 * h + 3))
                    dve.tensor_tensor(cmask[h % 2], cmask[h % 2], carg, ALU.add)
                    dve.tensor_tensor(mask[h % 2], mask[h % 2], diag, ALU.add).then_inc(masked.up(), 1)
                    dve.wait_ge(masked.sem, masked.at(h + 1))

                def store(h):
                    dve.wait_ge(valued.sem, valued.at(n * (h + 1)))
                    dve.tensor_copy(y[rows(h), 5 + h // 2, 0:qw], yps[h % 2][rows(h), 0:qw]).then_inc(stored.up(), 1)

                masks(0)
                for u in range(HEADS * n):
                    h, j = divmod(u, n)
                    tile, width = keys[j]
                    dve.wait_ge(scored.sem, scored.at(u + 1))
                    if u >= 3:
                        dve.wait_ge(valued.sem, valued.at(u - 2))
                    if j < 2:
                        m = cmask[h % 2][:, 128 - 128 * j:128 - 128 * j + S]
                    else:
                        m = mask[h % 2][:, 384 - 128 * tile:384 - 128 * tile + S]
                    ins = dve.scalar_tensor_tensor(out=aw[u % 3][:, 0:S], in0=sps[u % 2][:, 0:S], scalar=HEAD ** -0.5, in1=m,
                                                   op0=ALU.mult, op1=ALU.mult)
                    if width > S:
                        m = mask[h % 2][:, 384 - 128 * j:384 - 128 * j + CTX]
                        ins = dve.scalar_tensor_tensor(out=aw[u % 3][:, S:T], in0=sps[u % 2][:, S:T], scalar=HEAD ** -0.5, in1=m,
                                                       op0=ALU.mult, op1=ALU.mult)
                    ins.then_inc(weighed.up(), 1)
                    if j == 3 and h + 1 < HEADS:
                        masks(h + 1)
                    if j == 1 and h >= 1:
                        store(h - 1)
                store(HEADS - 1)

    def retention_output(self, l, need_ctx):
        px, y = self.px, self.xn.rearrange("p (k t) -> p k t", k=KT)
        width = T if need_ctx else S
        w = self.work
        sq = [w[:, i * T:i * T + width] for i in range(3)]
        rstd = [w[:, (3 + i) * T:(3 + i) * T + width] for i in range(3)]
        ga = [w[:, (6 + i) * T:(6 + i) * T + width] for i in range(3)]
        meant, centred, squared = self.sig("summed"), self.sig("centred"), self.sig("squared")
        varied, rooted, vstep, gated = self.sig("varied"), self.sig("rooted"), self.sig("vector_step"), self.sig("gated")
        with self.stage() as block:
            @block.tensor
            def _(pe):
                for i in range(3):
                    for a, b in pieces(width):
                        mm = pe.matmul(self.ps[:, i * 1024 + a:i * 1024 + b], self.group, y[:, 5 + i, a:b], start=True, stop=True)
                    mm.then_inc(meant.up(), 1)
                for i in range(3):
                    pe.wait_ge(squared.sem, squared.at(i + 1))
                    for a, b in pieces(width):
                        mm = pe.matmul(self.ps[:, i * 1024 + a:i * 1024 + b], self.group, sq[i][:, a:b], start=True, stop=True)
                    mm.then_inc(varied.up(), 1)

            @block.scalar
            def _(act):
                for i in range(3):
                    act.activation(ga[i], px[:, GATE + i, 0:width], ACT.Silu).then_inc(gated.up(), 1)
                for i in range(3):
                    act.wait_ge(centred.sem, centred.at(i + 1))
                    act.activation(sq[i], y[:, 5 + i, 0:width], ACT.Square).then_inc(squared.up(), 1)
                for i in range(3):
                    act.wait_ge(varied.sem, varied.at(i + 1))
                    act.activation(rstd[i], self.ps[:, i * 1024:i * 1024 + width], ACT.Sqrt, bias=EPS).then_inc(rooted.up(), 1)

            @block.vector
            def _(dve):
                for i in range(3):
                    dve.wait_ge(meant.sem, meant.at(i + 1))
                    dve.tensor_tensor(y[:, 5 + i, 0:width], y[:, 5 + i, 0:width], self.ps[:, i * 1024:i * 1024 + width],
                                      ALU.subtract).then_inc(centred.up(), 1)
                for i in range(3):
                    t = y[:, 5 + i, 0:width]
                    dve.wait_ge(rooted.sem, rooted.at(i + 1))
                    settle(dve, dve.reciprocal(rstd[i], rstd[i]), vstep)
                    settle(dve, dve.scalar_tensor_tensor(out=t, in0=t, scalar=self.v(("ret_gn_g", l), i), in1=rstd[i],
                                                         op0=ALU.mult, op1=ALU.mult), vstep)
                    dve.wait_ge(gated.sem, gated.at(i + 1))
                    settle(dve, dve.tensor_tensor(t, t, ga[i], ALU.mult), vstep)

    def output_projection(self, src, segments, residual):
        width = segments[-1][1]
        units = []
        for m in range(KT):
            def pairs(w, m=m):
                ws = w[0].rearrange("p (k c) -> p k c", k=KT)
                o = (m % 2) * P
                return [((a, b), [(ws[:, k, o:o + P], src(k)[:, a:b]) for k in range(KT)]) for a, b in pieces(width)]
            units.append(([m // 2], pairs, (0, P, width)))

        def finish(eng, i, ps):
            for a, b, gate in segments:
                if gate is None:
                    ins = eng.tensor_tensor(residual(i)[:, a:b], ps[:, a:b], residual(i)[:, a:b], ALU.add)
                else:
                    ins = eng.scalar_tensor_tensor(out=residual(i)[:, a:b], in0=ps[:, a:b], scalar=gate(i), in1=residual(i)[:, a:b],
                                                   op0=ALU.mult, op1=ALU.add)
            return ins

        self.project(units, 4, finish, banks_each=2)

    def gates(self, l, which, need_ctx):
        def seg(a, b, s):
            return (a, b, lambda k: self.mods[:, l, s, which * KT + k:which * KT + k + 1])
        return [seg(0, S, 0)] + ([seg(S, T, 1)] if need_ctx else [])

    def ffn_up(self, l, need_ctx):
        xn = self.xn.rearrange("p (k t) -> p k t", k=KT)
        width = T if need_ctx else S
        g = self.big[:, 0:FT * width].rearrange("p (m t) -> p m t", m=FT)
        self.g = g
        padded = S + 2 + (CTX + 1 if need_ctx else 0)
        n = padded - 2
        w = self.work
        u = w[:, 0:4 * 772].rearrange("p (b c t) -> p b c t", b=2, c=2)
        cv = w[:, 3088:3088 + 4 * 772].rearrange("p (b c t) -> p b c t", b=2, c=2)
        runs = [(0, S, 1)] + ([(S, T, S + 2)] if need_ctx else [])
        done, copied, convolved = self.sig("product_done"), self.sig("copied"), self.sig("convolved")
        silued, zeroed, vstep, gated = self.sig("silued"), self.sig("zeroed"), self.sig("vector_step"), self.sig("gated")
        first = len(self.freed_at)
        cw = lambda j, t: self.v(("conv_w", l), j * 2 * FT + t)
        with self.stage() as block:
            @block.gpsimd
            def _(pool):
                pool.memset(w[:, 0:4 * 772], 0.0).then_inc(zeroed.up(), 1)

            @block.tensor
            def _(pe):
                for i in range(FT):
                    ws = self.strip(pe, first + i).rearrange("p (k c) -> p k c", k=KT)
                    for c in range(2):
                        if i >= 2:
                            pe.wait_ge(copied.sem, copied.at(2 * (i - 2) + c + 1))
                        out = self.ps[:, (i % 2) * 2048 + c * 1024:(i % 2) * 2048 + c * 1024 + width]
                        for a, b in pieces(width):
                            for k in range(KT):
                                mm = pe.matmul(out[:, a:b], ws[:, k, c * P:(c + 1) * P], xn[:, k, a:b], start=k == 0, stop=k == KT - 1)
                        mm.then_inc(done.up(), 1)
                    self.strips_freed(1)

            @block.sync
            def _(sp):
                self.load_strips(sp)

            @block.scalar
            def _(act):
                act.wait_ge(zeroed.sem, zeroed.at(1))

                def silu(i):
                    act.wait_ge(convolved.sem, convolved.at(2 * i + 1))
                    act.activation(cv[:, i % 2, 0, 0:n], cv[:, i % 2, 0, 0:n], ACT.Silu).then_inc(silued.up(), 1)

                for i in range(FT):
                    for c in range(2):
                        act.wait_ge(done.sem, done.at(2 * i + c + 1))
                        if i >= 2:
                            act.wait_ge(convolved.sem, convolved.at(2 * (i - 2) + c + 1))
                        for a, b, o in runs:
                            ps = self.ps[:, (i % 2) * 2048 + c * 1024 + a:(i % 2) * 2048 + c * 1024 + b]
                            ins = act.activation(u[:, i % 2, c, o:o + b - a], ps, ACT.Copy)
                        ins.then_inc(copied.up(), 1)
                    if i >= 1:
                        silu(i - 1)
                silu(FT - 1)

            @block.vector
            def _(dve):
                def gate(i):
                    dve.wait_ge(silued.sem, silued.at(i + 1))
                    dve.wait_ge(convolved.sem, convolved.at(2 * i + 2))
                    for a, b, o in runs:
                        o -= 1
                        dve.tensor_tensor(g[:, i, a:b], cv[:, i % 2, 0, o:o + b - a], cv[:, i % 2, 1, o:o + b - a], ALU.mult).then_inc(gated.up(), 1)

                for i in range(FT):
                    for c in range(2):
                        t = i + c * FT
                        uu, cc = u[:, i % 2, c, :], cv[:, i % 2, c, 0:n]
                        dve.wait_ge(copied.sem, copied.at(2 * i + c + 1))
                        if i >= 2:
                            dve.wait_ge(gated.sem, gated.at(len(runs) * (i - 1)))
                        settle(dve, dve.tensor_scalar(cc, uu[:, 1:1 + n], cw(1, t), self.v(("conv_b", l), t), ALU.mult, ALU.add), vstep)
                        settle(dve, dve.scalar_tensor_tensor(out=cc, in0=uu[:, 0:n], scalar=cw(0, t), in1=cc, op0=ALU.mult, op1=ALU.add), vstep)
                        dve.scalar_tensor_tensor(out=cc, in0=uu[:, 2:2 + n], scalar=cw(2, t), in1=cc, op0=ALU.mult, op1=ALU.add).then_inc(convolved.up(), 1)
                    if i >= 1:
                        gate(i - 1)
                gate(FT - 1)

    def ffn_down(self, l, need_ctx):
        width = T if need_ctx else S
        g, segments = self.g, self.gates(l, 5, need_ctx)
        units = []
        for m in range(KT):
            def pairs(w):
                ws = [a.rearrange("p (k c) -> p k c", k=FT // 2) for a in w]
                return [((a, b), [(ws[k // 11][:, k % 11, :], g[:, k, a:b]) for k in range(FT)]) for a, b in pieces(width)]
            units.append(([2 * m, 2 * m + 1], pairs, (0, P, width)))

        def finish(eng, i, ps):
            for a, b, gate in segments:
                ins = eng.scalar_tensor_tensor(out=self.h[:, i, a:b], in0=ps[:, a:b], scalar=gate(i), in1=self.h[:, i, a:b],
                                               op0=ALU.mult, op1=ALU.add)
            return ins

        self.project(units, 2 * KT, finish, banks_each=2)

    def layer(self, l):
        need_ctx = l < DEPTH - 1
        xn = self.xn.rearrange("p (k t) -> p k t", k=KT)
        self.norm(lambda k: xn[:, k, :], lambda k: self.h[:, k, :], KT, T, self.segments(l, 0), self.work)
        self.input_projection(l, need_ctx)
        self.pooling(l, need_ctx)
        self.rotate()
        self.neighbourhood(l)
        if need_ctx:
            self.context_attention()
        self.retention(l, need_ctx)
        self.retention_output(l, need_ctx)
        self.output_projection(lambda k: xn[:, k, :], self.gates(l, 2, need_ctx), lambda m: self.h[:, m, :])
        width = T if need_ctx else S
        self.norm(lambda k: xn[:, k, 0:width], lambda k: self.h[:, k, 0:width], KT, width, self.segments(l, 1, need_ctx), self.work)
        self.ffn_up(l, need_ctx)
        self.ffn_down(l, need_ctx)


    def bigs(self, col, n, width):
        return self.big[:, col:col + n * width].rearrange("p (n t) -> p n t", n=n)

    def xns(self, n, width, col=0):
        return self.xn[:, col:col + n * width].rearrange("p (n t) -> p n t", n=n)

    def sine(self, eng, arg, k, vstep):
        two_pi_hi = 6.28125
        two_pi_lo = 2 * math.pi - two_pi_hi
        magic = 1.5 * 2.0 ** 23
        settle(eng, eng.tensor_scalar(k, arg, 1.0 / (2 * math.pi), magic, ALU.mult, ALU.add), vstep)
        settle(eng, eng.tensor_scalar(k, k, magic, None, ALU.subtract), vstep)
        settle(eng, eng.scalar_tensor_tensor(out=arg, in0=k, scalar=-two_pi_hi, in1=arg, op0=ALU.mult, op1=ALU.add), vstep)
        settle(eng, eng.scalar_tensor_tensor(out=arg, in0=k, scalar=-two_pi_lo, in1=arg, op0=ALU.mult, op1=ALU.add), vstep)
        top = float(np.nextafter(np.float32(math.pi), np.float32(0)))
        return eng.tensor_scalar(arg, arg, top, -top, ALU.min, ALU.max)

    def hyena_filters(self):
        taps = self.bigs(0, 4, 4 * S)
        spectra = self.big[:, 8192:8192 + 9216].rearrange("p (o n c) -> p o n c", o=2, n=9)
        self.spectra = spectra
        self.dft = self.work[:, 0:6144].rearrange("p (m k f) -> p m k f", m=3, k=4)
        cos, sin = self.dft[:, 0], self.dft[:, 1]
        feats = self.xn[:, 0:2 * S]
        filt = self.xn[:, 1024:3072]
        decay = self.xn[:, 3072:5120]
        h = [self.work[:, 6144 + i * S:6144 + (i + 1) * S] for i in range(2)]
        k = self.work[:, 7168:7168 + S]
        ex = [self.work[:, 7680 + i * S:7680 + (i + 1) * S] for i in range(2)]
        f = lambda i: self.v("hy_f", i)
        self.load([(feats, self.t["hyena"]), (filt[0:65, :], self.t["filter"]), (decay[0:1, :], self.t["decay"]),
                   (self.work[:, 0:6144], self.t["dft"])])
        done, vstep, ready, sined = self.sig("product_done"), self.sig("vector_step"), self.sig("reduced"), self.sig("sined")
        with self.stage() as block:
            @block.tensor
            def _(pe):
                pe.matmul(self.ps[0:64, 0:S], self.v("w1", 0, 64)[0:33, :], feats[0:33, 0:S], start=True, stop=True).then_inc(done.up(), 1)
                pe.wait_ge(sined.sem, sined.at(2))
                pe.matmul(self.ps[0:64, 512:512 + S], self.v("w2", 0, 64)[0:64, :], h[0][0:64, :], start=True, stop=True).then_inc(done.up(), 1)

            @block.vector
            def _(dve):
                dve.memset(h[1][64:65, :], 1.0)
                for i in range(2):
                    r = slice(0, 64)
                    dve.wait_ge(done.sem, done.at(i + 1))
                    settle(dve, dve.tensor_scalar(h[i][r, :], self.ps[r, i * 512:i * 512 + S], f(i)[r, :], f(2 + i)[r, :], ALU.add, ALU.mult), vstep)
                    self.sine(dve, h[i][r, :], k[r, :], vstep).then_inc(ready.up(), 1)

            @block.scalar
            def _(act):
                act.activation(decay[0:1, :], decay[0:1, :], ACT.Abs).then_inc(sined.up(), 1)
                for i in range(2):
                    act.wait_ge(ready.sem, ready.at(i + 1))
                    act.activation(h[i][0:64, :], h[i][0:64, :], ACT.Sin).then_inc(sined.up(), 1)

        exped, multiplied = self.sig("exponentials"), self.sig("multiplied")
        units = [(t, c) for t in range(4) for c in range(4)]
        with self.stage() as block:
            @block.tensor
            def _(pe):
                for u, (t, c) in enumerate(units):
                    if u >= 4:
                        pe.wait_ge(multiplied.sem, multiplied.at(u - 3))
                    b = 2 * (u % 4)
                    pe.matmul(self.bank(b + 1), feats[0:1, S + t * P:S + (t + 1) * P], decay[0:1, c * S:(c + 1) * S], start=True, stop=True)
                    pe.matmul(self.bank(b), h[1][0:65, t * P:(t + 1) * P], filt[0:65, c * S:(c + 1) * S], start=True, stop=True).then_inc(done.up(), 1)

            @block.scalar
            def _(act):
                for u, (t, c) in enumerate(units):
                    act.wait_ge(done.sem, done.at(u + 1))
                    if u >= 2:
                        act.wait_ge(multiplied.sem, multiplied.at(u - 1))
                    act.activation(ex[u % 2], self.bank(2 * (u % 4) + 1), ACT.Exp).then_inc(exped.up(), 1)

            @block.vector
            def _(dve):
                for u, (t, c) in enumerate(units):
                    dve.wait_ge(exped.sem, exped.at(u + 1))
                    dve.tensor_tensor(taps[:, t, c * S:(c + 1) * S], self.bank(2 * (u % 4)), ex[u % 2], ALU.mult).then_inc(multiplied.up(), 1)

        combined, taken = self.sig("combined"), self.sig("taken_by_vector")
        with self.stage() as block:
            @block.vector
            def _(dve):
                for o in range(2):
                    settle(dve, dve.memset(taps[0:1, 0, (2 * o + 1) * S:(2 * o + 2) * S], 0.0), vstep)
                    for t in range(4):
                        fw, bw = taps[:, t, 2 * o * S:(2 * o + 1) * S], taps[:, t, (2 * o + 1) * S:(2 * o + 2) * S]
                        settle(dve, dve.tensor_tensor(fw, fw, bw, ALU.add), vstep)
                        dve.scalar_tensor_tensor(out=bw, in0=bw, scalar=-2.0, in1=fw, op0=ALU.mult, op1=ALU.add).then_inc(combined.up(), 1)
                for o in range(2):
                    for n in range(9):
                        u = 9 * o + n
                        dve.wait_ge(done.sem, done.at(u + 1))
                        first = 0 if n % 4 == 0 else 1
                        if n == 0:
                            settle(dve, dve.tensor_scalar(spectra[:, o, 8, :], self.bank(u % 8), self.freq_w[:, 0:1], None, ALU.mult), vstep)
                        if n == 4:
                            settle(dve, dve.tensor_scalar(spectra[:, o, n, :], self.bank(u % 8), self.freq_w[:, first:first + 1], None, ALU.mult), vstep)
                            ins = dve.memset(spectra[0:1, o, 4, :], 0.0)
                        elif n < 8:
                            ins = dve.tensor_scalar(spectra[:, o, n, :], self.bank(u % 8), self.freq_w[:, first:first + 1], None, ALU.mult)
                        else:
                            ins = dve.tensor_scalar(spectra[0:1, o, 8, :], self.bank(u % 8)[0:1, :], self.freq_w[0:1, 0:1], None, ALU.mult)
                        ins.then_inc(taken.up(), 1)

            @block.tensor
            def _(pe):
                for o in range(2):
                    pe.wait_ge(combined.sem, combined.at(4 * (o + 1)))
                    for n in range(9):
                        u = 9 * o + n
                        if u >= 8:
                            pe.wait_ge(taken.sem, taken.at(u - 7))
                        table, half, m = (cos, 0, n) if n < 4 else (sin, 1, n - 4)
                        for t in range(4):
                            if n < 8:
                                lhs, out = table[:, t, m * P:(m + 1) * P], self.bank(u % 8)
                            else:
                                lhs, out, half = sin[:, t, 0:1], self.bank(u % 8)[0:1, :], 0
                            mm = pe.matmul(out, lhs, taps[:, t, (2 * o + half) * S:(2 * o + half + 1) * S], start=t == 0, stop=t == 3)
                        mm.then_inc(done.up(), 1)

    def second_projection(self):
        xn = self.xns(KT, S)
        p2 = self.bigs(0, 16, S)
        self.p2 = p2
        units = []
        for m in range(16):
            s = m // 2 if m < 2 else (1 if m < 4 else 2 + (m - 4) // 2)
            def pairs(w, m=m, s=s):
                ws = w[0].rearrange("p (k c) -> p k c", k=KT)
                o, n = (128, 32) if m == MKR else ((m % 2) * P if m != MKV else 0, P)
                return [((0, S), [(ws[:, k, o:o + n], xn[:, k, :]) for k in range(KT)])]
            units.append(([0 if m < 2 else s], pairs, (64, 32, S) if m == MKR else (0, P, S)))

        def finish(eng, i, ps):
            dst = p2[64:96, i, :] if i == MKR else p2[:, i, :]
            return eng.tensor_copy(dst, ps)

        self.project(units, 8, finish)

    def hyena(self):
        p2, u = self.p2, self.xns(4, 3 * S)
        free = self.big[:, 2048:8192]
        cos, sin, sint = self.dft[:, 0], self.dft[:, 1], self.dft[:, 2]
        cv = [self.work[:, 6144 + i * S:6144 + (i + 1) * S] for i in range(2)]
        done, vstep, conv, turned = self.sig("product_done"), self.sig("vector_step"), self.sig("convolved"), self.sig("turned")
        copied = self.sig("copied")
        with self.stage() as block:
            @block.vector
            def _(dve):
                for i in range(12):
                    src, c = p2[:, HY + i, :], cv[i % 2]
                    if i >= 2:
                        dve.wait_ge(turned.sem, turned.at(i - 1))
                    settle(dve, dve.tensor_scalar(c, src, self.v("hy_cw", 12 + i), self.v("hy_cb", i), ALU.mult, ALU.add), vstep)
                    settle(dve, dve.scalar_tensor_tensor(out=c[:, 1:S], in0=src[:, 0:S - 1], scalar=self.v("hy_cw", i), in1=c[:, 1:S],
                                                         op0=ALU.mult, op1=ALU.add), vstep)
                    dve.scalar_tensor_tensor(out=c[:, 0:S - 1], in0=src[:, 1:S], scalar=self.v("hy_cw", 24 + i), in1=c[:, 0:S - 1],
                                             op0=ALU.mult, op1=ALU.add).then_inc(conv.up(), 1)

            @block.tensor
            def _(pe):
                for i in range(12):
                    pe.wait_ge(conv.sem, conv.at(i + 1))
                    if i >= 4:
                        pe.wait_ge(copied.sem, copied.at(i - 3))
                    for t in range(4):
                        mm = pe.transpose(self.bank(i % 4)[:, t * P:(t + 1) * P], cv[i % 2][:, t * P:(t + 1) * P], self.ident)
                    mm.then_inc(turned.up(), 1)

            @block.scalar
            def _(act):
                for i in range(12):
                    act.wait_ge(turned.sem, turned.at(i + 1))
                    act.activation(u[:, :, i * P:(i + 1) * P], self.bank(i % 4).rearrange("p (t c) -> p t c", t=4), ACT.Copy).then_inc(copied.up(), 1)

        y = self.bigs(2048, 8, S)
        tmp = [self.work[:, 6144 + i * S:6144 + (i + 1) * S] for i in range(4)]
        skip = self.work[:, 8192:9216]
        self.load([(skip, self.t["skip"])])
        z = [u[:, t, 2 * S:3 * S] for t in range(4)]
        taken, filtered, gated = self.sig("taken_by_vector"), self.sig("filtered"), self.sig("gated")
        for o in range(2):
            sp = self.spectra[:, o]
            with self.stage() as block:
                @block.tensor
                def _(pe):
                    for m in range(4):
                        for half, table in enumerate((cos, sin)):
                            for t in range(4):
                                mm = pe.matmul(self.bank(2 * m + half), table[:, t, m * P:(m + 1) * P], z[t], start=t == 0, stop=t == 3)
                            mm.then_inc(done.up(), 1)
                    for t in range(4):
                        pe.wait_ge(filtered.sem, filtered.at(4))
                        for m in range(4):
                            pe.matmul(self.bank(t), cos[:, m, t * P:(t + 1) * P], y[:, m, :], start=m == 0, stop=False)
                            mm = pe.matmul(self.bank(t), sint[:, m, t * P:(t + 1) * P], y[:, 4 + m, :], start=False, stop=m == 3)
                        mm.then_inc(done.up(), 1)

                @block.vector
                def _(dve):
                    for m in range(4):
                        dve.wait_ge(done.sem, done.at(2 * m + 2))
                        re, im = self.bank(2 * m), self.bank(2 * m + 1)
                        kc, ks, kd = sp[:, m, :], sp[:, 4 + m, :], sp[:, 8 if m == 0 else m, :]
                        a, b = tmp[2 * (m % 2)], tmp[2 * (m % 2) + 1]
                        dve.tensor_tensor(y[:, m, :], re, kc, ALU.mult)
                        dve.tensor_tensor(a, im, ks, ALU.mult)
                        dve.tensor_tensor(y[:, 4 + m, :], re, ks, ALU.mult)
                        settle(dve, dve.tensor_tensor(b, im, kd, ALU.mult), vstep)
                        settle(dve, dve.tensor_tensor(y[:, m, :], y[:, m, :], a, ALU.subtract), vstep)
                        dve.tensor_tensor(y[:, 4 + m, :], y[:, 4 + m, :], b, ALU.add).then_inc(filtered.up(), 1)
                    for t in range(4):
                        if t >= 2:
                            dve.wait_ge(gated.sem, gated.at(t - 1))
                        settle(dve, dve.tensor_tensor(tmp[t % 2], z[t], skip[:, o * S:(o + 1) * S], ALU.mult), vstep)
                        dve.wait_ge(done.sem, done.at(9 + t))
                        settle(dve, dve.tensor_tensor(tmp[t % 2], self.bank(t), tmp[t % 2], ALU.add), vstep)
                        dve.tensor_tensor(z[t], tmp[t % 2], u[:, t, o * S:(o + 1) * S], ALU.mult).then_inc(gated.up(), 1)

        self.mix = self.bigs(8192, 8, S)
        squared, rooted, normed = self.sig("squared"), self.sig("rooted"), self.sig("normalised")
        ss, rs = self.small[:, 0:4], self.small[:, 4:8]
        with self.stage() as block:
            @block.scalar
            def _(act):
                for t in range(4):
                    act.activation(tmp[t], z[t], ACT.Square, accum_out=ss[:, t:t + 1]).then_inc(squared.up(), 1)
                act.wait_ge(squared.sem, squared.at(4))
                act.activation(rs, ss, ACT.Sqrt, scale=1.0 / S, bias=EPS).then_inc(rooted.up(), 1)

            @block.vector
            def _(dve):
                dve.wait_ge(rooted.sem, rooted.at(1))
                settle(dve, dve.reciprocal(rs, rs), vstep)
                for t in range(4):
                    dve.tensor_scalar(z[t], z[t], rs[:, t:t + 1], None, ALU.mult).then_inc(normed.up(), 1)
                for i in range(4):
                    dve.wait_ge(turned.sem, turned.at(i + 1))
                    dve.tensor_scalar(self.mix[:, 4 + i, :], self.bank(i), self.v("hyout_g", i), None, ALU.mult)

            @block.tensor
            def _(pe):
                pe.wait_ge(normed.sem, normed.at(4))
                for i in range(4):
                    for t in range(4):
                        mm = pe.transpose(self.bank(i)[:, t * P:(t + 1) * P], z[t][:, i * P:(i + 1) * P], self.ident)
                    mm.then_inc(turned.up(), 1)

    def latent_attention(self):
        p2, mix = self.p2, self.mix
        whole = lambda gain: [(0, S, gain, None)]
        self.norm(lambda k: p2[:, MQ + k, :], lambda k: p2[:, MQ + k, :], 2, S, whole(lambda k: self.v("q_g", k)), self.work)
        self.norm(lambda k: p2[:, MKV, :], lambda k: p2[:, MKV, :], 1, S, whole(lambda k: self.v("kv_g")), self.work)
        q = self.bigs(12288, MLA_HEADS, S)
        kk = self.xns(MLA_HEADS, S)
        v = self.xns(4, S, 4096)
        units, dst = [], []
        for h in range(MLA_HEADS):
            def pairs(w, h=h):
                ws = w[0].rearrange("p (k c) -> p k c", k=2)
                return [((0, S), [(ws[:, k, h * 96:(h + 1) * 96], p2[:, MQ + k, :]) for k in range(2)])]
            units.append(([0], pairs, (0, 96, S)))
            dst.append(q[0:96, h, :])
        for h in range(MLA_HEADS):
            units.append(([1], lambda w, h=h: [((0, S), [(w[0][:, h * 64:(h + 1) * 64], p2[:, MKV, :])])], (0, 64, S)))
            dst.append(kk[0:64, h, :])
        for t in range(4):
            units.append(([1], lambda w, t=t: [((0, S), [(p2[:, MKV, t * P:(t + 1) * P], w[0][:, 512:1024])])], (0, P, S)))
            dst.append(v[:, t, :])

        def finish(eng, i, ps):
            if eng is self.nc.scalar:
                return eng.activation(dst[i], ps, ACT.Copy)
            return eng.tensor_copy(dst[i], ps)

        self.project(units, 2, finish)
        w = self.work
        tables = (w[:, 0:S], w[:, S:2 * S], w[:, 2 * S:2 * S + P])
        tmp = [w[:, 1152 + i * S:1152 + (i + 1) * S] for i in range(2)]
        self._rotate([q[0:96, h, :] for h in range(MLA_HEADS)], 0, 96, *tables, tmp, self.t["rope96"], w[:, 0:1152])
        self._rotate([p2[64:96, MKR, :]], 64, 32, *tables, tmp, self.t["rope96"], w[:, 0:1152])
        with self.stage() as block:
            @block.vector
            def _(dve):
                for h in range(MLA_HEADS):
                    dve.tensor_copy(kk[64:96, h, :], p2[64:96, MKR, :])
        def rows(h):
            return slice(64 * (h % 2), 64 * (h % 2) + 64)
        self.attention(
            MLA_HEADS, 4, S, 1,
            q=lambda h, i: [q[0:96, h, i * P:(i + 1) * P]],
            k=lambda h: [[(0, S, kk[0:96, h, :])]],
            bias=None,
            v=lambda h, j, n: v[:, j, h * 64:(h + 1) * 64],
            outs=lambda h: [mix[rows(h), h // 2, :]],
            scale=96 ** -0.5, tmp=self.work)
        self.norm(lambda k: mix[:, k, :], lambda k: mix[:, k, :], 4, S, whole(lambda k: self.v("attn_g", k)), self.work)

    def memory_attention(self):
        xn = self.xns(KT, S)
        self.norm(lambda k: xn[:, k, :], lambda k: self.x[:, k, :], KT, S, [(0, S, lambda k: self.v("cross_g", k), None)], self.work,
                  load=[(self.big[:, 0:2048].rearrange("p (k t) -> p k t", k=KT), self.t["memory"])])
        mem, hm = self.bigs(0, KT, 256), self.bigs(2048, KT, 256)
        self.norm(lambda k: hm[:, k, :], lambda k: mem[:, k, :], KT, 256, [(0, 256, lambda k: self.v("mem_g", k), None)], self.work)
        keys, v, q, o = self.bigs(4096, KT, 256), self.bigs(6144, 2, D), self.bigs(8192, KT, S), self.bigs(12288, KT, S)
        units, dst = [], []

        def feature(strip, m, src, width):
            def pairs(w):
                ws = w[0].rearrange("p (k c) -> p k c", k=KT)
                return [((0, width), [(ws[:, k, (m % 2) * P:(m % 2 + 1) * P], src[:, k, :]) for k in range(KT)])]
            units.append(([strip + m // 2], pairs, (0, P, width)))

        for m in range(KT):
            feature(0, m, hm, 256)
            dst.append(keys[:, m, :])
        for c in range(4):
            for t in range(2):
                def pairs(w, t=t):
                    ws = w[0].rearrange("p (k c) -> p k c", k=KT)
                    return [((0, 256), [(hm[:, k, t * P:(t + 1) * P], ws[:, k, :]) for k in range(KT)])]
                units.append(([4 + c], pairs, (0, P, 256)))
                dst.append(v[:, t, c * 256:(c + 1) * 256])
        for m in range(KT):
            feature(8, m, xn, S)
            dst.append(q[:, m, :])
        self.project(units, 12, lambda eng, i, ps: eng.tensor_copy(dst[i], ps))
        self.attention(
            MEM_HEADS, 4, 256, 2,
            q=lambda h, i: [q[:, 2 * h + d, i * P:(i + 1) * P] for d in range(2)],
            k=lambda h: [[(0, 256, keys[:, 2 * h + d, :])] for d in range(2)],
            bias=None,
            v=lambda h, j, n: v[:, j, h * 256 + n * P:h * 256 + (n + 1) * P],
            outs=lambda h: [o[:, 2 * h + n, :] for n in range(2)],
            scale=1.0 / 16, tmp=self.work)
        self.output_projection(lambda k: o[:, k, :], [(0, S, None)], lambda m: self.x[:, m, :])

    def route(self):
        xn = self.xns(KT, S)
        w = self.work[:, 9600:9888].rearrange("p (k c) -> p k c", k=KT)
        tmp = self.work[:, 9888:]
        at = [0]

        def take(*dims):
            n = int(np.prod(dims))
            a = tmp[:, at[0]:at[0] + n]
            at[0] += n
            return a.rearrange("p (a b) -> p a b", a=dims[0]) if len(dims) > 1 else a

        logits = take(4, 36)
        one_g, ex, picked = take(4, 4), take(4, 4), take(4, 32)
        e_in, one_1, one_2, rest, weight = take(4, 8), take(4, 8), take(4, 8), take(4, 8), take(4, 8)
        comb = take(4, 32)
        top, total, v1, v2, p1, p2, m = (take(4) for _ in range(7))
        self.norm(lambda k: xn[:, k, :], lambda k: self.x[:, k, :], KT, S, [(0, S, lambda k: self.v("ffn_g", k), None)], self.work,
                  load=[(w, self.t["route"])])
        done, vstep, exped, ready = self.sig("product_done"), self.sig("vector_step"), self.sig("exponentials"), self.sig("argued")
        turned, copied, stored = self.sig("turned"), self.sig("copied"), self.sig("outputs_stored")
        comb_t = self.work[:, 9088:9600]
        self.comb_dram = self.nc.dram_tensor("combine", [EXPERTS, S], F32, kind="Internal").ap()
        wide = lambda a, n: a.unsqueeze(2).to_broadcast([P, 4, n])
        rank = lambda n: self.rank[:, 8 - n:8].unsqueeze(1).to_broadcast([P, 4, n])
        with self.stage() as block:
            @block.tensor
            def _(pe):
                for t in range(4):
                    for k in range(KT):
                        mm = pe.matmul(self.ps[:, t * 36:(t + 1) * 36], xn[:, k, t * P:(t + 1) * P], w[:, k, :], start=k == 0, stop=k == KT - 1)
                mm.then_inc(done.up(), 1)
                pe.wait_ge(ready.sem, ready.at(3))
                for t in range(4):
                    mm = pe.transpose(self.ps[0:32, 512 + t * P:512 + (t + 1) * P], comb[:, t, :], self.ident)
                mm.then_inc(turned.up(), 1)

            @block.scalar
            def _(act):
                act.wait_ge(ready.sem, ready.at(1))
                act.activation(ex, ex, ACT.Exp).then_inc(exped.up(), 1)
                act.wait_ge(ready.sem, ready.at(2))
                act.activation(p2, p2, ACT.Exp).then_inc(exped.up(), 1)

            @block.vector
            def _(dve):
                def do(ins):
                    settle(dve, ins, vstep)

                def first_best(hot, values, best, n):
                    do(dve.tensor_tensor(hot, values, wide(best, n), ALU.is_equal))
                    do(dve.tensor_tensor(hot, hot, rank(n), ALU.mult))
                    do(dve.reduce_max(m, hot, AX))
                    do(dve.tensor_tensor(hot, hot, wide(m, n), ALU.is_equal))

                dve.wait_ge(done.sem, done.at(1))
                do(dve.tensor_tensor(logits.rearrange("p a b -> p (a b)"), self.ps[:, 0:144], self.v("route_b", 0, 144), ALU.add))
                g, e = logits[:, :, 0:4], logits[:, :, 4:36]
                do(dve.reduce_max(top, g, AX))
                dve.tensor_tensor(ex, g, wide(top, 4), ALU.subtract).then_inc(ready.up(), 1)
                first_best(one_g, g, top, 4)
                for i in range(GROUPS):
                    do(dve.tensor_tensor(picked[:, :, i * 8:(i + 1) * 8], e[:, :, i * 8:(i + 1) * 8], one_g[:, :, i:i + 1].to_broadcast([P, 4, 8]), ALU.mult))
                do(dve.tensor_tensor(e_in, picked[:, :, 0:8], picked[:, :, 8:16], ALU.add))
                do(dve.tensor_tensor(e_in, e_in, picked[:, :, 16:24], ALU.add))
                do(dve.tensor_tensor(e_in, e_in, picked[:, :, 24:32], ALU.add))
                do(dve.reduce_max(v1, e_in, AX))
                first_best(one_1, e_in, v1, 8)
                do(dve.scalar_tensor_tensor(out=rest, in0=one_1, scalar=-3.0e38, in1=e_in, op0=ALU.mult, op1=ALU.add))
                do(dve.reduce_max(v2, rest, AX))
                first_best(one_2, rest, v2, 8)
                dve.tensor_tensor(p2, v2, v1, ALU.subtract).then_inc(ready.up(), 1)
                dve.wait_ge(exped.sem, exped.at(2))
                do(dve.reduce_sum(total, ex, AX))
                do(dve.tensor_scalar(p1, p2, 1.0, None, ALU.add))
                do(dve.tensor_tensor(p1, p1, total, ALU.mult))
                do(dve.reciprocal(p1, p1))
                do(dve.tensor_tensor(p2, p2, p1, ALU.mult))
                do(dve.tensor_tensor(one_1, one_1, wide(p1, 8), ALU.mult))
                do(dve.tensor_tensor(one_2, one_2, wide(p2, 8), ALU.mult))
                do(dve.tensor_tensor(weight, one_1, one_2, ALU.add))
                for i in range(GROUPS):
                    ins = dve.tensor_tensor(comb[:, :, i * 8:(i + 1) * 8], weight, one_g[:, :, i:i + 1].to_broadcast([P, 4, 8]), ALU.mult)
                    if i < GROUPS - 1:
                        do(ins)
                ins.then_inc(ready.up(), 1)
                dve.wait_ge(turned.sem, turned.at(1))
                dve.tensor_copy(comb_t[0:32, :], self.ps[0:32, 512:1024]).then_inc(copied.up(), 1)

            @block.sync
            def _(sp):
                sp.wait_ge(copied.sem, copied.at(1))
                sp.dma_start(self.comb_dram, comb_t[0:32, :]).then_inc(stored.up(16), 16)
                sp.wait_ge(stored.sem, stored.at(16))

    def experts(self):
        nc, turns = self.nc, EXPERTS // 2
        xn = self.xns(KT, S)
        ring = [self.big[:, i * STRIP:(i + 1) * STRIP] for i in range(6)]
        comb = [self.big[:, 12288 + i * S:12288 + (i + 1) * S] for i in range(2)]
        act_t = [self.big[:, 13312 + i * S:13312 + (i + 1) * S] for i in range(2)]
        hidden = [self.work[:, i * S:(i + 1) * S] for i in range(4)]
        landed = [nc.alloc_semaphore(f"expert_strip_landed_{i}") for i in range(6)]
        comb_landed = [nc.alloc_semaphore(f"combine_landed_{i}") for i in range(2)]
        up_done, silued, hidden_done = (nc.alloc_semaphore(n) for n in ("up_done", "silu_done", "hidden_done"))
        down_done, added, weighed = (nc.alloc_semaphore(n) for n in ("down_done", "added", "silu_weighed"))
        with self.stage() as block:
            @block.sync
            def _(sp):
                def load(it, e, strips=(0, 1, 2)):
                    for j in strips:
                        i = 3 * e + j
                        sp.dma_start(ring[i], self.t["experts"][bass.ds(it * 2 + e, 1), j, :, :].rearrange("a p c -> (a p) c"))\
                            .then_inc(landed[i], 16)

                def load_comb(it, e):
                    sp.dma_start(comb[e], self.comb_dram[bass.ds(it * 2 + e, 1), :].to_broadcast([P, S])).then_inc(comb_landed[e], 16)

                for e in range(2):
                    load(0, e)
                    load_comb(0, e)
                with sp.Fori(1, turns) as it:
                    for e in range(2):
                        sp.wait_ge(up_done, it * 8 - 4 + 4 * e)
                        load(it, e, (0, 1))
                        sp.wait_ge(hidden_done, it * 4 - 2 + 2 * e)
                        load_comb(it, e)
                    sp.wait_ge(down_done, it * 8)
                    for e in range(2):
                        load(it, e, (2,))

            @block.tensor
            def _(pe):
                with pe.Fori(0, turns) as it:
                    for e in range(2):
                        for m in range(2):
                            for j in range(2):
                                n = 4 * e + 2 * m + j
                                if m == 0:
                                    pe.wait_ge(landed[3 * e + j], it * 16 + 16)
                                if e == 1:
                                    pe.wait_ge(hidden_done, it * 4 + m + 1)
                                ws = ring[3 * e + j].rearrange("p (k c) -> p k c", k=KT)
                                for k in range(KT):
                                    mm = pe.matmul(self.bank(2 * m + j), ws[:, k, m * P:(m + 1) * P], xn[:, k, :], start=k == 0, stop=k == KT - 1)
                                mm.then_inc(up_done, 1)
                    for half in range(2):
                        for e in range(2):
                            if half == 0:
                                pe.wait_ge(landed[3 * e + 2], it * 16 + 16)
                                pe.wait_ge(hidden_done, it * 4 + 2 + 2 * e)
                            ws = ring[3 * e + 2].rearrange("p (k c) -> p k c", k=2)
                            for d in range(4):
                                if e == 0 and half == 1:
                                    pe.wait_ge(added, it * 8 + d + 1)
                                c = (4 * half + d) * P
                                for k in range(2):
                                    mm = pe.matmul(self.bank(4 + d), ws[:, k, c:c + P], hidden[2 * e + k], start=e == 0 and k == 0, stop=e == 1 and k == 1)
                                if e == 1:
                                    mm.then_inc(down_done, 1)

            @block.scalar
            def _(act):
                with act.Fori(0, turns) as it:
                    for e in range(2):
                        for m in range(2):
                            act.wait_ge(up_done, it * 8 + 4 * e + 2 * m + 1)
                            if e == 1:
                                act.wait_ge(hidden_done, it * 4 + m + 1)
                            act.activation(act_t[m], self.bank(2 * m), ACT.Silu).then_inc(silued, 1)

            @block.vector
            def _(dve):
                with dve.Fori(0, turns) as it:
                    for e in range(2):
                        dve.wait_ge(comb_landed[e], it * 16 + 16)
                        for m in range(2):
                            i = 2 * e + m
                            dve.wait_ge(silued, it * 4 + i + 1)
                            dve.tensor_tensor(act_t[m], act_t[m], comb[e], ALU.mult).then_inc(weighed, 1)
                            dve.wait_ge(weighed, it * 4 + i + 1)
                            dve.wait_ge(up_done, it * 8 + 4 * e + 2 * m + 2)
                            dve.tensor_tensor(hidden[i], self.bank(2 * m + 1), act_t[m], ALU.mult).then_inc(hidden_done, 1)
                    for d in range(8):
                        dve.wait_ge(down_done, it * 8 + d + 1)
                        dve.tensor_tensor(self.x[:, d, :], self.bank(4 + d % 4), self.x[:, d, :], ALU.add).then_inc(added, 1)

    def second(self):
        xn = self.xns(KT, S)
        whole = lambda name: [(0, S, lambda k: self.v(name, k), None)]
        stream = lambda k: self.x[:, k, :]
        for name, step in (
            ("first", lambda: self.norm(stream, stream, KT, S, whole("final_g"), self.work)),
            ("filters", self.hyena_filters),
            ("mixnorm", lambda: self.norm(lambda k: xn[:, k, :], stream, KT, S, whole("mix_g"), self.work[:, 6144:])),
            ("proj", self.second_projection),
            ("hyena", self.hyena),
            ("mla", self.latent_attention),
            ("mixed", lambda: self.output_projection(lambda k: self.mix[:, k, :], [(0, S, None)], stream)),
            ("mem", self.memory_attention),
            ("route", self.route),
            ("experts", self.experts),
            ("last", lambda: self.norm(lambda k: xn[:, k, :], stream, KT, S, whole("last_g"), self.work))):
            step()
            if name == self.until:
                if len(self.freed_at) < STRIPS or self.issued > 0: self.drain_loads()
                return
        stored = self.sig("outputs_stored")
        with self.stage() as block:
            @block.sync
            def _(sp):
                sp.dma_start(self.out, xn).then_inc(stored.up(16), 16)
                sp.wait_ge(stored.sem, stored.at(16))


def build(nc, tables, until=None):
    t = {}
    for name, a in tables.items():
        t[name[3:]] = nc.dram_tensor(name, a.shape, F32, kind="ExternalInput").ap()
    out = nc.dram_tensor("out", [P, KT, S], F32, kind="ExternalOutput").ap()
    b = Builder(nc, t, out)
    b.until = until
    b.start()
    b.modulation()
    for l in range(DEPTH):
        b.layer(l)
        if until == f"layer{l}":
            b.drain_loads()
            return
    b.second()


def kernel(**inputs):
    import concourse.bacc as bacc
    from concourse.bass_utils import run_bass_kernel_spmd

    tables = lay_out(inputs)
    nc = bacc.Bacc("TRN2", target_bir_lowering=False, num_devices=1)
    build(nc, tables)
    r = run_bass_kernel_spmd(nc, [tables], core_ids=[0])
    got = r.results[0]["out"]
    return np.ascontiguousarray(got.transpose(2, 1, 0).reshape(1, S, D))
```

```python
import contextlib
import math

import numpy as np

import concourse.bass as bass
from concourse import mybir
from concourse.alu_op_type import AluOpType as ALU

F32 = mybir.dt.float32
ACT = mybir.ActivationFunctionType
AX = mybir.AxisListType.X

P = 128
D = 1024
KT = D // P
S = 512
CTX = 256
T = S + CTX
DEPTH = 2
GRID_W = 64
NEG_INF = -1e30
EPS = 1e-6
HEAD = 64
HEADS = 6
WINDOWS = (2, 4, 8, 16)
D_FF = 2816
FT = D_FF // P
STRIP = 2048
RING = 5
MLA_HEADS = 8
MEM_HEADS = 4
EXPERTS = 32
GROUPS = 4
SLOTS = 64
PER_GROUP = EXPERTS // GROUPS
NFFT = 2 * S

POOL, NAQ, NAK, RQ, RK, GATE, NPX = 0, 2, 5, 8, 11, 14, 17
MQ, MKV, MKR, HY = 0, 2, 3, 4




def strip_plan():
    plan = []
    r = np.arange
    off = np.cumsum([0, 256, 384, 384, 384, 384, 384, 384, 384])
    feature = np.concatenate([r(off[i], off[i + 1]) for i in (0, 1, 2, 4, 5, 7)])
    token = np.concatenate([r(off[3], off[4]), r(off[6], off[7])])
    for l in range(DEPTH):
        for c in range(0, 6 * D, 512):
            for half in range(2):
                plan.append((("w_mod", l), r(half * 512, half * 512 + 512), r(c, c + 512)))
    for l in range(DEPTH):
        for c in range(0, NPX * P, 256):
            plan.append((("w_in", l), r(D), feature[c:c + 256]))
        for c in range(0, 768, 256):
            plan.append((("w_in", l), r(D), token[c:c + 256]))
        for c in range(0, D, 256):
            plan.append((("w_out", l), r(D), r(c, c + 256)))
        for m in range(FT):
            plan.append((("w_up", l), r(D), np.concatenate([r(m * P, m * P + P), D_FF + r(m * P, m * P + P)])))
        for c in range(0, D, P):
            for half in range(2):
                plan.append((("w_down", l), r(half * 1408, half * 1408 + 1408), r(c, c + P)))
    plan.append((("w_in_2", 0), r(D), r(0, 256)))
    plan.append((("w_in_2", 0), r(D), r(256, 416)))
    for c in range(0, 1536, 256):
        plan.append((("w_in_2", 0), r(D), 416 + r(c, c + 256)))
    plan.append((("w_uq_2", 0), r(256), r(768)))
    nope = np.concatenate([h * 128 + r(64) for h in range(MLA_HEADS)])
    plan.append((("w_ukv_2", 0), r(128), np.concatenate([nope, nope + 64])))
    for name, cols in (("w_out_2", D), ("w_mkv_2", 2 * D), ("w_mq_2", D), ("w_mo_2", D)):
        for c in range(0, cols, 256):
            plan.append(((name, 0), r(D), r(c, c + 256)))
    return plan


PLAN = strip_plan()
STRIPS = len(PLAN)
WIDTH = [len(rows) // P * len(cols) for _, rows, cols in PLAN]


def pack_strip(matrix, rows, cols):
    a = matrix[rows][:, cols]
    a = a.reshape(len(rows) // P, P, len(cols)).transpose(1, 0, 2).reshape(P, -1)
    return a


class Columns:

    def __init__(self):
        self.at, self.n = {}, 0

    def add(self, name, count):
        self.at[name] = self.n
        self.n += count

    def __getitem__(self, name):
        return self.at[name]


VEC = Columns()
for _l in range(DEPTH):
    for _name, _count in (("b_mod", 48), ("norm1_g", KT), ("norm2_g", KT), ("conv_w", 6 * FT), ("conv_b", 2 * FT),
                          ("pool_scale", 2), ("ret_gn_g", 3), ("decay_f", HEADS), ("decay_b", HEADS), ("pool_w", 128)):
        VEC.add((_name, _l), _count)
for _name, _count in (("c", 2 * KT), ("final_g", KT), ("mix_g", KT), ("q_g", 2), ("kv_g", 1), ("hy_cw", 36),
                      ("hy_cb", 12), ("attn_g", 4), ("hyout_g", 4), ("cross_g", KT), ("mem_g", KT), ("ffn_g", KT),
                      ("last_g", KT), ("hy_f", 4), ("w1", 64), ("w2", 64), ("route_b", 4 * 36)):
    VEC.add(_name, _count)


def tiles_of(v):
    return np.reshape(v, (-1, P)).T


def pack_vectors(x):
    out = np.zeros((P, VEC.n), np.float32)

    def put(name, a):
        out[:a.shape[0], VEC[name]:VEC[name] + a.shape[1]] = a

    for l in range(DEPTH):
        for name in ("b_mod", "norm1_g", "norm2_g", "conv_b", "pool_scale", "ret_gn_g"):
            put((name, l), tiles_of(x[name][l]))
        put(("conv_w", l), tiles_of(x["conv_w"][l]))
        put(("decay_f", l), np.broadcast_to(x["ret_decay_fwd"][l], (P, HEADS)))
        put(("decay_b", l), np.broadcast_to(x["ret_decay_bwd"][l], (P, HEADS)))
        w = x["pool_w"][l].reshape(2, 2, 64, 64)
        put(("pool_w", l), w.transpose(1, 2, 0, 3).reshape(P, 128))
    put("c", np.stack([tiles_of(x["c"][0]), tiles_of(x["c_ctx"])], axis=2).reshape(P, 2 * KT))
    for name, key in (("final_g", "final_g"), ("mix_g", "mix_norm_g_2"), ("q_g", "q_norm_g_2"),
                      ("kv_g", "kv_norm_g_2"), ("hy_cw", "hy_conv_w_2"), ("hy_cb", "hy_conv_b_2"),
                      ("attn_g", "attn_out_g_2"), ("hyout_g", "hy_out_g_2"), ("cross_g", "cross_norm_g_2"),
                      ("mem_g", "mem_norm_g_2"), ("ffn_g", "ffn_norm_g_2"), ("last_g", "final_norm_g_2")):
        put(name, tiles_of(x[key]))
    put("hy_f", np.stack([x["hy_b1_2"][0], x["hy_b2_2"][0], x["hy_freq_2"][0, 0], x["hy_freq_2"][0, 1]], axis=1))
    put("w1", x["hy_w1_2"][0])
    put("w2", x["hy_w2_2"][0])
    bias = np.concatenate([x["b_route_group_2"][0], x["b_route_expert_2"][0]])
    put("route_b", np.broadcast_to(np.tile(bias, 4), (P, 144)))
    return out


def constants():
    f = np.float64
    p = np.arange(P)[:, None]
    t = np.arange(S)[None, :]
    out = {}
    inv = np.zeros((P, 2, T), f)
    for g, w in enumerate(WINDOWS):
        for a, n in ((0, S), (S, CTX)):
            i = np.arange(n)
            inv[64 * (g % 2):64 * (g % 2) + 64, g // 2, a:a + n] = 1.0 / (np.clip(i - w // 2 + w, 0, n) - np.clip(i - w // 2, 0, n))
    out["pool"] = inv.reshape(P, -1)
    freq = 10000.0 ** (-np.arange(16) / 16.0)
    freq = freq.astype(np.float32)
    pos = np.arange(S)
    ang = np.stack([(pos // GRID_W).astype(np.float32)[None, :] * freq[:, None],
                    (pos % GRID_W).astype(np.float32)[None, :] * freq[:, None]]).astype(np.float32)
    within = np.arange(P) % 64
    axis, i = within // 32, within % 16
    a = ang[axis, i]
    swap = np.zeros((P, P), f)
    for q in range(P):
        first = q % 32 < 16
        swap[q + 16 if first else q - 16, q] = -1.0 if first else 1.0
    out["rope"] = np.concatenate([np.cos(a), np.sin(a), swap], axis=1)
    x = np.arange(896)[None, :] - 384 - p
    y = np.arange(896)[None, :] - 128 - p
    out["ramp"] = np.concatenate([np.maximum(x, 0), np.maximum(-x, 0), (x == 0), 256 + y[:, :640], 512 - y[:, :640]], axis=1)
    ang = (pos.astype(np.float32)[None, :] * freq[:, None]).astype(np.float32)
    ang = ang[np.arange(32) % 16]
    c96 = np.ones((P, S), f)
    s96 = np.zeros((P, S), f)
    c96[64:96], s96[64:96] = np.cos(ang), np.sin(ang)
    swap = np.zeros((P, P), f)
    for q in range(64, 96):
        first = q < 80
        swap[q + 16 if first else q - 16, q] = -1.0 if first else 1.0
    out["rope96"] = np.concatenate([c96, s96, swap], axis=1)
    n, k = np.arange(S)[:, None], np.arange(S)[None, :]
    cos = np.cos(2 * np.pi * (n * k % NFFT) / NFFT)
    sin = np.sin(2 * np.pi * (n * k % NFFT) / NFFT)
    sin[:, 0] = 1.0 - 2.0 * (np.arange(S) % 2)
    def tiled(m):
        return m.reshape(4, P, S).transpose(1, 0, 2).reshape(P, 4 * S)
    out["dft"] = np.concatenate([tiled(cos), tiled(sin), tiled(sin.T)], axis=1)
    tt = np.arange(S).astype(np.float32)
    t01 = tt / np.float32(S)
    bands = np.linspace(1e-4, 15, 16, dtype=np.float32)
    ang = (np.float32(2.0 * math.pi) * tt[:, None] * bands[None, :] / np.float32(S)).astype(np.float32)
    z = np.concatenate([t01[:, None], np.cos(ang), -np.sin(ang)], axis=1).T
    feats = np.zeros((P, 2 * S), f)
    feats[:33, :S] = z
    feats[0, S:] = -t01
    out["hyena"] = feats
    group = np.zeros((P, P))
    group[:64, :64] = group[64:, 64:] = 1.0 / 64
    w = np.full((P, 2), 2.0 / NFFT)
    w[0, 0] = 1.0 / NFFT
    rank = np.broadcast_to(np.arange(8, 0, -1)[None, :], (P, 8))
    earlier = p < np.arange(P)[None, :]
    slot = np.broadcast_to(SLOTS * np.arange(EXPERTS)[None, :], (P, EXPERTS))
    out["base"] = np.concatenate([np.eye(P), np.ones((P, P)), group, w, rank, earlier, slot, p + P * np.arange(4)[None, :]], axis=1)
    return {k: np.ascontiguousarray(v.astype(np.float32)) for k, v in out.items()}


BASE_COLS = 4 * P + 46


def pack_bias(rpb):
    qc = np.arange(GRID_W)
    start = np.clip(qc - 8, 0, GRID_W - 16)
    kc = np.arange(GRID_W)
    valid = (kc[None, :] >= start[:, None]) & (kc[None, :] < start[:, None] + 16)
    dc = np.clip(kc[None, :] - qc[:, None] + 15, 0, 30)
    out = np.full((DEPTH, HEADS, 2, GRID_W, 15, GRID_W), NEG_INF, np.float32)
    for a in range(2):
        for s in range(1, 15):
            picked = rpb[:, :, s - a][:, :, dc]
            out[:, :, a, :, s, :] = np.where(valid, picked, np.float32(NEG_INF))
    return out.reshape(DEPTH * HEADS, P, 15 * GRID_W)


def lay_out(x):
    x = {k: np.asarray(v) for k, v in x.items()}
    out = dict(constants())
    stream = np.zeros((STRIPS, P, STRIP), np.float32)
    for i, ((name, l), rows, cols) in enumerate(PLAN):
        stream[i, :, :WIDTH[i]] = pack_strip(x[name][l], rows, cols)
    out["stream"] = stream
    experts = np.empty((EXPERTS, P, 3 * STRIP), np.float32)
    both = np.concatenate([x[name][0].reshape(EXPERTS, KT, P, 256) for name in ("w_gate_2", "w_up_2")], axis=3)
    experts[:, :, :2 * STRIP] = both.transpose(0, 2, 1, 3).reshape(EXPERTS, P, 2 * STRIP)
    experts[:, :, 2 * STRIP:] = x["w_down_2"][0].reshape(EXPERTS, 2, P, D).transpose(0, 2, 1, 3).reshape(EXPERTS, P, STRIP)
    out["experts"] = experts
    out["last_gain"] = np.broadcast_to(x["final_norm_g_2"], (P, D))
    out["vectors"] = pack_vectors(x)
    out["bias"] = pack_bias(x["na_rpb"])
    out["tokens"] = np.concatenate([x["x"][0].T.reshape(KT, P, S), x["ctx"][0].T.reshape(KT, P, CTX)], axis=2).transpose(1, 0, 2)
    out["memory"] = x["mem_2"][0].T.reshape(KT, P, 256).transpose(1, 0, 2)
    route = np.concatenate([x["w_route_group_2"][0], x["w_route_expert_2"][0]], axis=1)
    out["route"] = route.reshape(KT, P, 36).transpose(1, 0, 2)
    out["filter"] = np.concatenate([x["hy_w3_2"][0], x["hy_b3_2"]], axis=0)
    out["decay"] = x["hy_decay_2"]
    out["skip"] = np.broadcast_to(x["hy_skip_2"].reshape(1, 2 * S), (P, 2 * S))
    return {"in_" + k: np.ascontiguousarray(v) for k, v in out.items()}




class Signal:

    def __init__(self, nc, name):
        self.sem = nc.alloc_semaphore(name)
        self.base = self.n = 0

    def up(self, by=1):
        self.n += by
        return self.sem

    def at(self, k):
        return self.base + k

    def now(self):
        return self.base + self.n

    def close(self):
        self.base += self.n
        self.n = 0


def settle(engine, instruction, signal):
    instruction.then_inc(signal.up(), 1)
    engine.wait_ge(signal.sem, signal.now())


def pieces(width):
    return [(a, min(a + 512, width)) for a in range(0, width, 512)]


class Builder:
    def __init__(self, nc, t, out):
        self.nc, self.t, self.out = nc, t, out
        self.signals = {}
        alloc = lambda name, cols: nc.alloc_sbuf_tensor(name, [P, cols], F32)[:, :]
        self.h = alloc("h", KT * T).rearrange("p (k t) -> p k t", k=KT)
        self.xn = alloc("xn", KT * T)
        self.big = alloc("big", 17664)
        self.ring = alloc("ring", RING * STRIP)
        self.vec = alloc("vec", VEC.n)
        self.base = alloc("base", BASE_COLS)
        self.mods = alloc("mods", DEPTH * 2 * 48).rearrange("p (l s m) -> p l s m", l=DEPTH, s=2)
        self.gains = alloc("gains", DEPTH * 2 * 2 * KT).rearrange("p (l s n k) -> p l s n k", l=DEPTH, s=2, n=2)
        self.small = alloc("small", 128)
        self.work = alloc("work", 10890)
        self.ps = nc.alloc_psum_tensor("ps", [P, 4096], F32)[:, :]
        self.ident = self.base[:, 0:P]
        self.ones = self.base[:, P:2 * P]
        self.group = self.base[:, 2 * P:3 * P]
        self.freq_w = self.base[:, 3 * P:3 * P + 2]
        self.rank = self.base[:, 3 * P + 2:3 * P + 10]
        self.earlier = self.base[:, 3 * P + 10:4 * P + 10]
        self.first_slot = self.base[:, 4 * P + 10:4 * P + 42]
        self.token_number = self.base[:, 4 * P + 42:4 * P + 46]
        self.x = self.h[:, :, 0:S]
        self.issued = 0
        self.freed_at = []
        self.landed = [nc.alloc_semaphore(f"strip_landed_{i}") for i in range(RING)]
        self.done = self.sig("product_done")

    def sig(self, name):
        if name not in self.signals:
            self.signals[name] = Signal(self.nc, name)
        return self.signals[name]

    @contextlib.contextmanager
    def stage(self):
        with self.nc.Block(no_gpsimd_drain=True) as block:
            yield block
        for s in self.signals.values():
            s.close()

    def v(self, name, i=0, n=1):
        a = VEC[name] + i
        return self.vec[:, a:a + n]

    def bank(self, b, width=512, rows=P, first=0):
        return self.ps[first:first + rows, b * 512:b * 512 + width]


    def load_strips(self, sp):
        until = min(len(self.freed_at) + RING, STRIPS)
        for i in range(self.issued, until):
            if i >= RING:
                sp.wait_ge(self.done.sem, self.freed_at[i - RING])
            slot = i % RING
            sp.dma_start(self.ring[:, slot * STRIP:slot * STRIP + WIDTH[i]],
                         self.t["stream"][i, :, 0:WIDTH[i]]).then_inc(self.landed[slot], 16)
        self.issued = until

    def strip(self, pe, i):
        pe.wait_ge(self.landed[i % RING], 16 * (i // RING + 1))
        a = (i % RING) * STRIP
        return self.ring[:, a:a + WIDTH[i]]

    def strips_freed(self, count):
        self.freed_at += [self.done.now()] * count


    def load(self, items):
        landed = self.sig("inputs_landed")
        with self.stage() as block:
            @block.scalar
            def _(act):
                for dst, src in items:
                    act.dma_start(dst, src).then_inc(landed.up(16), 16)
                act.wait_ge(landed.sem, landed.now())

    def norm(self, dst, src, kt, width, segments, tmp, load=()):
        squared, summed, rooted = self.sig("squared"), self.sig("summed"), self.sig("rooted")
        scaled, shifted, vstep = self.sig("scaled"), self.sig("shifted"), self.sig("vector_step")
        landed = self.sig("inputs_landed")
        sq = [tmp[:, i * width:(i + 1) * width] for i in range(2)]
        rstd = tmp[:, 2 * width:3 * width]
        mean = self.ps[:, 0:width]
        with self.stage() as block:
            @block.scalar
            def _(act):
                for a, b in load:
                    act.dma_start(a, b).then_inc(landed.up(16), 16)
                for k in range(kt):
                    if k >= 2:
                        act.wait_ge(summed.sem, summed.at(k - 1))
                    act.activation(sq[k % 2], src(k), ACT.Square).then_inc(squared.up(), 1)
                act.wait_ge(summed.sem, summed.at(kt))
                act.activation(rstd, mean, ACT.Sqrt, scale=1.0 / (kt * P), bias=EPS).then_inc(rooted.up(), 1)
                done = 0
                for k in range(kt):
                    for a, b, gain, shift in segments:
                        done += 1
                        if shift is not None:
                            act.wait_ge(scaled.sem, scaled.at(done))
                            act.activation(dst(k)[:, a:b], dst(k)[:, a:b], ACT.Identity, bias=shift(k)).then_inc(shifted.up(), 1)
                if load:
                    act.wait_ge(landed.sem, landed.now())

            @block.tensor
            def _(pe):
                for k in range(kt):
                    pe.wait_ge(squared.sem, squared.at(k + 1))
                    for a, b in pieces(width):
                        mm = pe.matmul(mean[:, a:b], self.ones, sq[k % 2][:, a:b], start=k == 0, stop=k == kt - 1)
                    mm.then_inc(summed.up(), 1)

            @block.vector
            def _(dve):
                dve.wait_ge(rooted.sem, rooted.at(1))
                settle(dve, dve.reciprocal(rstd, rstd), vstep)
                for k in range(kt):
                    for a, b, gain, shift in segments:
                        dve.scalar_tensor_tensor(out=dst(k)[:, a:b], in0=src(k)[:, a:b], scalar=gain(k), in1=rstd[:, a:b],
                                                 op0=ALU.mult, op1=ALU.mult).then_inc(scaled.up(), 1)

    def project(self, units, strips, finish, banks_each=1, act_every=0):
        first = len(self.freed_at)
        done, taken_v, taken_a = self.done, self.sig("taken_by_vector"), self.sig("taken_by_scalar")
        slots = 8 // banks_each
        on_act = [act_every and i % act_every == act_every - 1 for i in range(len(units))]

        def freed(pe, i):
            j = i - slots
            if j >= 0:
                if on_act[j]:
                    pe.wait_ge(taken_a.sem, taken_a.at(sum(on_act[:j + 1])))
                else:
                    pe.wait_ge(taken_v.sem, taken_v.at(j + 1 - sum(on_act[:j + 1])))

        def place(i):
            rows0, rows, width = units[i][2]
            a = (i % slots) * banks_each * 512
            return self.ps[rows0:rows0 + rows, a:a + width]

        with self.stage() as block:
            @block.tensor
            def _(pe):
                for i, (need, pairs, _) in enumerate(units):
                    freed(pe, i)
                    w = [self.strip(pe, first + s) for s in need]
                    out = place(i)
                    for (a, b), terms in pairs(w):
                        for j, (lhs, rhs) in enumerate(terms):
                            mm = pe.matmul(out[:, a:b], lhs, rhs, start=j == 0, stop=j == len(terms) - 1)
                    mm.then_inc(done.up(), 1)
                    upto = strips if i == len(units) - 1 else min(units[i + 1][0])
                    self.strips_freed(first + upto - len(self.freed_at))

            @block.sync
            def _(sp):
                self.load_strips(sp)

            @block.vector
            def _(dve):
                for i in range(len(units)):
                    if not on_act[i]:
                        dve.wait_ge(done.sem, done.at(i + 1))
                        finish(dve, i, place(i)).then_inc(taken_v.up(), 1)

            @block.scalar
            def _(act):
                for i in range(len(units)):
                    if on_act[i]:
                        act.wait_ge(done.sem, done.at(i + 1))
                        finish(act, i, place(i)).then_inc(taken_a.up(), 1)

    def attention(self, heads, nq, width, depth, q, k, bias, v, outs, scale, tmp):
        nk = width // P
        sbanks = (width + 511) // 512
        scored, tk, biased = self.sig("scored"), self.sig("max_taken"), self.sig("biased")
        exped, normed, turned = self.sig("exponentials"), self.sig("normalised"), self.sig("turned")
        copied, valued, stored = self.sig("turned_copied"), self.sig("valued"), self.sig("stored")
        vstep, bias_in = self.sig("vector_step"), self.sig("bias_landed")
        n_out = len(outs(0))
        pbuf = [tmp[:, i * width:(i + 1) * width] for i in range(2)]
        at = 2 * width
        pt = [tmp[:, at + i * nk * nq * P:at + (i + 1) * nk * nq * P].rearrange("p (k q) -> p k q", k=nk) for i in range(2)]
        at += 2 * nk * nq * P
        gt = [tmp[:, at + i * 960:at + (i + 1) * 960] for i in range(2)]
        stat = self.small[:, 0:16].rearrange("p (a b) -> p a b", a=4)
        units = heads * nq
        spsum = [self.ps[:, i * 1024:i * 1024 + width] for i in range(2)]
        tpsum = self.ps[:, 2048:2048 + width]
        opsum = [self.ps[:, 3072 + i * 512:3072 + (i + 1) * 512] for i in range(2)]
        with self.stage() as block:
            if bias:
                @block.sync
                def _(sp):
                    for h in range(heads):
                        if h >= 2:
                            sp.wait_ge(tk.sem, tk.at((h - 1) * nq))
                        sp.dma_start(gt[h % 2], bias(h)).then_inc(bias_in.up(16), 16)
                        sp.wait_ge(bias_in.sem, bias_in.now())

            @block.tensor
            def _(pe):
                def scores(u):
                    h, i = divmod(u, nq)
                    if u >= 2:
                        pe.wait_ge(exped.sem, exped.at(u - 1))
                    for d in range(depth):
                        for a, b, keys in k(h)[d]:
                            mm = pe.matmul(spsum[u % 2][:, a:b], q(h, i)[d], keys, start=d == 0, stop=d == depth - 1)
                    mm.then_inc(scored.up(), 1)

                def values(h):
                    pe.wait_ge(copied.sem, copied.at((h + 1) * nq))
                    for n in range(n_out):
                        m = h * n_out + n
                        if m >= 2:
                            pe.wait_ge(stored.sem, stored.at(m - 1))
                        dst = outs(h)[n]
                        r0, rows = dst.base_partition(), dst.shape[0]
                        for j in range(nk):
                            mm = pe.matmul(opsum[m % 2][r0:r0 + rows, 0:nq * P], v(h, j, n), pt[h % 2][:, j, :],
                                           start=j == 0, stop=j == nk - 1)
                        mm.then_inc(valued.up(), 1)

                scores(0)
                for u in range(units):
                    if u + 1 < units:
                        scores(u + 1)
                    pe.wait_ge(normed.sem, normed.at(u + 1))
                    if u >= 1:
                        pe.wait_ge(copied.sem, copied.at(u))
                    for j in range(nk):
                        mm = pe.transpose(tpsum[:, j * P:(j + 1) * P], pbuf[u % 2][:, j * P:(j + 1) * P], self.ident)
                    mm.then_inc(turned.up(), 1)
                    if u % nq == 0 and u >= nq:
                        values(u // nq - 1)
                values(heads - 1)

            @block.vector
            def _(dve):
                def top(u):
                    h, i = divmod(u, nq)
                    b = u % 2
                    dve.wait_ge(scored.sem, scored.at(u + 1))
                    src, s = spsum[b], scale
                    if bias:
                        if i == 0:
                            dve.wait_ge(bias_in.sem, bias_in.at(16 * (h + 1)))
                        if u >= 2:
                            dve.wait_ge(turned.sem, turned.at(u - 1))
                        a = (7 - 2 * i) * GRID_W
                        dve.tensor_scalar(pbuf[b][:, 512:width], spsum[b][:, 512:width], scale, None, ALU.mult)
                        settle(dve, dve.scalar_tensor_tensor(out=pbuf[b][:, 0:512], in0=spsum[b][:, 0:512], scalar=scale,
                                                             in1=gt[h % 2][:, a:a + 512], op0=ALU.mult, op1=ALU.add), vstep)
                        src, s = pbuf[b], 1.0
                    settle(dve, dve.reduce_max(stat[:, 0, b:b + 1], src, AX), vstep)
                    dve.tensor_scalar(stat[:, 1, b:b + 1], stat[:, 0, b:b + 1], -s, None, ALU.mult).then_inc(tk.up(), 1)

                def normalise(u):
                    b = u % 2
                    dve.wait_ge(exped.sem, exped.at(u + 1))
                    settle(dve, dve.reciprocal(stat[:, 3, b:b + 1], stat[:, 2, b:b + 1]), vstep)
                    dve.tensor_scalar(pbuf[b], pbuf[b], stat[:, 3, b:b + 1], None, ALU.mult).then_inc(normed.up(), 1)

                def store(h):
                    for n in range(n_out):
                        m = h * n_out + n
                        dve.wait_ge(valued.sem, valued.at(m + 1))
                        dst = outs(h)[n]
                        r0, rows = dst.base_partition(), dst.shape[0]
                        dve.tensor_copy(dst, opsum[m % 2][r0:r0 + rows, 0:nq * P]).then_inc(stored.up(), 1)

                top(0)
                for u in range(units):
                    if u + 1 < units:
                        top(u + 1)
                    normalise(u)
                    if u % nq == min(1, nq - 1) and u >= nq:
                        store(u // nq - 1)
                store(heads - 1)

            @block.scalar
            def _(act):
                for u in range(units):
                    b = u % 2
                    act.wait_ge(tk.sem, tk.at(u + 1))
                    if not bias and u >= 2:
                        act.wait_ge(turned.sem, turned.at(u - 1))
                    src, s = (pbuf[b], 1.0) if bias else (spsum[b], scale)
                    act.activation(pbuf[b], src, ACT.Exp, bias=stat[:, 1, b:b + 1], scale=s,
                                   accum_out=stat[:, 2, b:b + 1]).then_inc(exped.up(), 1)
                    if u >= 1:
                        self._turn_copy(act, u - 1, nq, nk, turned, copied, valued, n_out, pt, tpsum)
                self._turn_copy(act, units - 1, nq, nk, turned, copied, valued, n_out, pt, tpsum)

    def _turn_copy(self, act, u, nq, nk, turned, copied, valued, n_out, pt, tpsum):
        h, i = divmod(u, nq)
        if i == 0 and h >= 2:
            act.wait_ge(valued.sem, valued.at((h - 1) * n_out))
        act.wait_ge(turned.sem, turned.at(u + 1))
        act.activation(pt[h % 2][:, :, i * P:(i + 1) * P], tpsum.rearrange("p (k q) -> p k q", k=nk), ACT.Copy).then_inc(copied.up(), 1)


    def start(self):
        landed, done = self.sig("inputs_landed"), self.sig("conditioned")
        self.cond = self.small[:, 16:32]
        with self.stage() as block:
            @block.sync
            def _(sp):
                self.load_strips(sp)

            @block.scalar
            def _(act):
                for dst, src in ((self.vec, self.t["vectors"]), (self.base, self.t["base"]), (self.h, self.t["tokens"])):
                    act.dma_start(dst, src).then_inc(landed.up(16), 16)
                act.wait_ge(landed.sem, landed.now())
                act.activation(self.cond, self.v("c", 0, 16), ACT.Silu).then_inc(done.up(), 1)
                act.wait_ge(done.sem, done.now())

    def modulation(self):
        rows = self.big[0:2, 0:DEPTH * 6 * D]
        cond = self.cond.rearrange("p (k s) -> p k s", s=2)
        units = []
        for c in range(DEPTH * 12):
            def pairs(w, c=c):
                return [((0, 512), [(cond[:, k, :], w[k // 4][:, (k % 4) * 512:(k % 4 + 1) * 512]) for k in range(KT)])]
            units.append(([2 * c, 2 * c + 1], pairs, (0, 2, 512)))

        def finish(eng, i, ps):
            return eng.tensor_copy(rows[:, i * 512:(i + 1) * 512], ps)

        self.project(units, DEPTH * 24, finish)
        turned, vstep = self.sig("turned"), self.sig("vector_step")
        n = DEPTH * 48
        ps = self.ps[:, 0:2 * n].rearrange("p (l m s) -> p l m s", l=DEPTH, s=2)
        with self.stage() as block:
            @block.tensor
            def _(pe):
                for j in range(n):
                    mm = pe.transpose(self.ps[:, 2 * j:2 * j + 2], rows[:, j * P:(j + 1) * P], self.ident[0:2, 0:2])
                mm.then_inc(turned.up(), 1)

            @block.vector
            def _(dve):
                dve.wait_ge(turned.sem, turned.at(1))
                for l in range(DEPTH):
                    for s in range(2):
                        settle(dve, dve.tensor_tensor(self.mods[:, l, s, :], ps[:, l, :, s], self.v(("b_mod", l), 0, 48), ALU.add), vstep)
                        for which, name, m in ((0, "norm1_g", 1), (1, "norm2_g", 4)):
                            dve.scalar_tensor_tensor(out=self.gains[:, l, s, which, :], in0=self.mods[:, l, s, m * KT:(m + 1) * KT],
                                                     scalar=1.0, in1=self.v((name, l), 0, KT), op0=ALU.add, op1=ALU.mult)

    def segments(self, l, which, need_ctx=True):
        shift = 0 if which == 0 else 3
        def seg(a, b, s):
            return (a, b, lambda k: self.gains[:, l, s, which, k:k + 1],
                    lambda k: self.mods[:, l, s, shift * KT + k:shift * KT + k + 1])
        return [seg(0, S, 0)] + ([seg(S, T, 1)] if need_ctx else [])

    def input_projection(self, l, need_ctx):
        xn = self.xn.rearrange("p (k t) -> p k t", k=KT)
        px = self.big[:, 0:NPX * T].rearrange("p (n t) -> p n t", n=NPX)
        pv = self.big[:, NPX * T:NPX * T + 6 * 768].rearrange("p (n c) -> p n c", n=6)
        self.px, self.pv = px, pv
        units, dst = [], []
        for m in range(NPX):
            width = T if need_ctx or NAK <= m < RQ or RK <= m < GATE else S
            def pairs(w, m=m, width=width):
                ws = w[0].rearrange("p (k c) -> p k c", k=KT)
                o = (m % 2) * P
                return [((a, b), [(ws[:, k, o:o + P], xn[:, k, a:b]) for k in range(KT)]) for a, b in pieces(width)]
            units.append(([m // 2], pairs, (0, P, width)))
            dst.append(px[:, m, 0:width])
        for c in range(3):
            for n in range(6):
                def pairs(w, n=n):
                    ws = w[0].rearrange("p (k c) -> p k c", k=KT)
                    return [((0, 256), [(xn[:, k, n * P:(n + 1) * P], ws[:, k, :]) for k in range(KT)])]
                units.append(([9 + c], pairs, (0, P, 256)))
                dst.append(pv[:, n, c * 256:(c + 1) * 256])
        def finish(eng, i, ps):
            if eng is self.nc.scalar:
                return eng.activation(dst[i], ps, ACT.Copy)
            return eng.tensor_copy(dst[i], ps)

        self.project(units, 12, finish, banks_each=2)

    def pooling(self, l, need_ctx):
        px, y = self.px, self.xn.rearrange("p (k t) -> p k t", k=KT)
        w = self.work
        inv = w[:, 0:2 * T].rearrange("p (n t) -> p n t", n=2)
        lead, gap = 8, 16
        width = lead + S + gap + CTX + lead
        buf = [[w[:, 2 * T + (5 * n + j) * width:2 * T + (5 * n + j + 1) * width] for j in range(5)] for n in range(2)]
        runs = [(0, S, lead), (S, T, lead + S + gap)] if need_ctx else [(0, S, lead)]
        landed, vstep, ready = self.sig("inputs_landed"), self.sig("vector_step"), self.sig("pooled")
        done = self.sig("product_done")
        with self.stage() as block:
            @block.sync
            def _(sp):
                sp.dma_start(inv, self.t["pool"].rearrange("p (n t) -> p n t", n=2)).then_inc(landed.up(16), 16)

            @block.vector
            def _(dve):
                dve.wait_ge(landed.sem, landed.at(16))
                for n in range(2):
                    settle(dve, dve.memset(buf[n][0], 0.0), vstep)
                    for a, b, o in runs:
                        settle(dve, dve.tensor_copy(buf[n][0][:, o:o + b - a], px[:, n, a:b]), vstep)
                    lo, hi = 1, width
                    settle(dve, dve.tensor_tensor(buf[n][1][:, 1:width], buf[n][0][:, 0:width - 1], buf[n][0][:, 1:width], ALU.add), vstep)
                    for level in range(2 + 2 * n):
                        dst = buf[n][(level + 1) % 4]
                        if level > 0:
                            src, half = buf[n][level % 4], 2 ** (level - 1)
                            settle(dve, dve.tensor_tensor(dst[:, lo + half:hi - half], src[:, lo:hi - 2 * half],
                                                          src[:, lo + 2 * half:hi], ALU.add), vstep)
                            lo, hi = lo + half, hi - half
                        group = level - 2 * n
                        if group >= 0:
                            r = slice(64 * group, 64 * group + 64)
                            for a, b, o in runs:
                                settle(dve, dve.tensor_tensor(buf[n][4][r, a:b], dst[r, o:o + b - a], inv[r, n, a:b], ALU.mult), vstep)
                    for a, b, o in runs:
                        dve.tensor_tensor(buf[n][4][:, a:b], buf[n][4][:, a:b], px[:, n, a:b], ALU.subtract).then_inc(ready.up(), 1)
                for n in range(2):
                    dve.wait_ge(done.sem, done.at(n + 1))
                    for a, b, o in runs:
                        dve.tensor_scalar(y[:, n, a:b], self.ps[:, n * 1024 + a:n * 1024 + b], self.v(("pool_scale", l), n), None, ALU.mult)

            @block.tensor
            def _(pe):
                for n in range(2):
                    pe.wait_ge(ready.sem, ready.at(len(runs) * (n + 1)))
                    for half in range(2):
                        r = slice(64 * half, 64 * half + 64)
                        for a, b, o in runs:
                            mm = pe.matmul(self.ps[r, n * 1024 + a:n * 1024 + b], self.v(("pool_w", l), 64 * n, 64)[r, :],
                                           buf[n][4][r, a:b], start=True, stop=True)
                    mm.then_inc(done.up(), 1)

    def rotate(self):
        px = self.px
        cos, sin, swap = self.work[:, 0:S], self.work[:, S:2 * S], self.work[:, 2 * S:2 * S + P]
        tmp = [self.work[:, 1152 + i * S:1152 + (i + 1) * S] for i in range(2)]
        tiles = [RQ, RQ + 1, RQ + 2, RK, RK + 1, RK + 2]
        self._rotate([px[:, m, 0:S] for m in tiles], 0, P, cos, sin, swap, tmp, self.t["rope"], self.work[:, 0:1152])

    def _rotate(self, tiles, row0, rows, cos, sin, swap, tmp, table, table_at):
        r = slice(row0, row0 + rows)
        landed, vstep, done = self.sig("inputs_landed"), self.sig("vector_step"), self.sig("product_done")
        with self.stage() as block:
            @block.sync
            def _(sp):
                sp.dma_start(table_at, table).then_inc(landed.up(16), 16)

            @block.tensor
            def _(pe):
                pe.wait_ge(landed.sem, landed.at(16))
                for i, t in enumerate(tiles):
                    pe.matmul(self.ps[r, i % 8 * 512:i % 8 * 512 + S], swap[r, r], t, start=True, stop=True).then_inc(done.up(), 1)

            @block.vector
            def _(dve):
                dve.wait_ge(landed.sem, landed.at(16))
                for i, t in enumerate(tiles):
                    dve.wait_ge(done.sem, done.at(i + 1))
                    dve.tensor_tensor(tmp[i % 2][r, :], self.ps[r, i % 8 * 512:i % 8 * 512 + S], sin[r, :], ALU.mult)
                    settle(dve, dve.tensor_tensor(t, t, cos[r, :], ALU.mult), vstep)
                    settle(dve, dve.tensor_tensor(t, t, tmp[i % 2][r, :], ALU.add), vstep)

    def neighbourhood(self, l):
        px, pv, y = self.px, self.pv, self.xn.rearrange("p (k t) -> p k t", k=KT)
        def rows(h):
            return slice(64 * (h % 2), 64 * (h % 2) + 64)
        self.attention(
            HEADS, 4, T, 1,
            q=lambda h, i: [px[rows(h), NAQ + h // 2, i * P:(i + 1) * P]],
            k=lambda h: [[(a, b, px[rows(h), NAK + h // 2, a:b]) for a, b in pieces(T)]],
            bias=lambda h: self.t["bias"][l * HEADS + h],
            v=lambda h, j, n: pv[:, j, h * 64:(h + 1) * 64],
            outs=lambda h: [y[rows(h), 2 + h // 2, 0:S]],
            scale=HEAD ** -0.5, tmp=self.work)

    def context_attention(self):
        px, pv, y = self.px, self.pv, self.xn.rearrange("p (k t) -> p k t", k=KT)
        def rows(h):
            return slice(64 * (h % 2), 64 * (h % 2) + 64)
        self.attention(
            HEADS, 2, CTX, 1,
            q=lambda h, i: [px[rows(h), NAQ + h // 2, S + i * P:S + (i + 1) * P]],
            k=lambda h: [[(0, CTX, px[rows(h), NAK + h // 2, S:T])]],
            bias=None,
            v=lambda h, j, n: pv[:, 4 + j, h * 64:(h + 1) * 64],
            outs=lambda h: [y[rows(h), 2 + h // 2, S:T]],
            scale=HEAD ** -0.5, tmp=self.work)

    def retention(self, l, need_ctx):
        px, pv, y = self.px, self.pv, self.xn.rearrange("p (k t) -> p k t", k=KT)
        w = self.work
        ramps = w[:, 0:3968]
        fwd, bwd, diag = (w[:, i * 896:(i + 1) * 896] for i in range(3))
        cfwd, cbwd = w[:, 2688:3328], w[:, 3328:3968]
        mask = [w[:, 3968 + i * 896:3968 + (i + 1) * 896] for i in range(2)]
        cmask = [w[:, 5760 + i * 640:5760 + (i + 1) * 640] for i in range(2)]
        arg, carg = w[:, 7040:7936], w[:, 7936:8576]
        aw = [w[:, 8576 + i * T:8576 + (i + 1) * T] for i in range(3)]
        qw = T if need_ctx else S
        keys = [(4, qw), (5, qw)] + [(j, S) for j in range(4)]
        n = len(keys)
        landed, vstep, argued = self.sig("inputs_landed"), self.sig("vector_step"), self.sig("argued")
        powered, masked, scored = self.sig("powered"), self.sig("masked"), self.sig("scored")
        weighed, valued, stored = self.sig("weighed"), self.sig("valued"), self.sig("stored")
        astep, carg_done = self.sig("scalar_step"), self.sig("context_powered")
        def rows(h):
            return slice(64 * (h % 2), 64 * (h % 2) + 64)
        sps = [self.ps[:, i * 1024:i * 1024 + T] for i in range(2)]
        yps = [self.ps[:, 2048 + i * 1024:2048 + i * 1024 + T] for i in range(2)]
        with self.stage() as block:
            @block.sync
            def _(sp):
                sp.dma_start(ramps, self.t["ramp"]).then_inc(landed.up(16), 16)

            @block.tensor
            def _(pe):
                def scores(u):
                    h, j = divmod(u, n)
                    tile, width = keys[j]
                    if u >= 2:
                        pe.wait_ge(weighed.sem, weighed.at(u - 1))
                    a0 = tile * P
                    for a, b in pieces(width):
                        mm = pe.matmul(sps[u % 2][:, a:b], px[rows(h), RK + h // 2, a0:a0 + P], px[rows(h), RQ + h // 2, a:b],
                                       start=True, stop=True)
                    mm.then_inc(scored.up(), 1)

                scores(0)
                for u in range(HEADS * n):
                    h, j = divmod(u, n)
                    if u + 1 < HEADS * n:
                        scores(u + 1)
                    if j == 0 and h >= 2:
                        pe.wait_ge(stored.sem, stored.at(h - 1))
                    pe.wait_ge(weighed.sem, weighed.at(u + 1))
                    tile, width = keys[j]
                    for a, b in pieces(width):
                        mm = pe.matmul(yps[h % 2][rows(h), a:b], pv[:, tile, 384 + h * 64:384 + (h + 1) * 64], aw[u % 3][:, a:b],
                                       start=j == 0, stop=j == (n - 1 if a == 0 else 1))
                    mm.then_inc(valued.up(), 1)

            @block.scalar
            def _(act):
                act.wait_ge(landed.sem, landed.at(16))
                for h in range(HEADS):
                    if h >= 2:
                        act.wait_ge(weighed.sem, weighed.at(n * (h - 1)))
                    if h >= 1:
                        act.wait_ge(masked.sem, masked.at(h))
                    act.activation(cmask[h % 2], cfwd, ACT.Exp, scale=self.v(("decay_f", l), h)).then_inc(powered.up(), 1)
                    act.activation(carg, cbwd, ACT.Exp, scale=self.v(("decay_b", l), h)).then_inc(powered.up(), 1)
                    act.wait_ge(argued.sem, argued.at(h + 1))
                    act.activation(mask[h % 2], arg, ACT.Exp).then_inc(powered.up(), 1)

            @block.vector
            def _(dve):
                dve.wait_ge(landed.sem, landed.at(16))

                def masks(h):
                    if h >= 1:
                        dve.wait_ge(powered.sem, powered.at(3 * h))
                    settle(dve, dve.tensor_scalar(arg, fwd, self.v(("decay_f", l), h), None, ALU.mult), vstep)
                    dve.scalar_tensor_tensor(out=arg, in0=bwd, scalar=self.v(("decay_b", l), h), in1=arg,
                                             op0=ALU.mult, op1=ALU.add).then_inc(argued.up(), 1)
                    dve.wait_ge(powered.sem, powered.at(3 * h + 3))
                    dve.tensor_tensor(cmask[h % 2], cmask[h % 2], carg, ALU.add)
                    dve.tensor_tensor(mask[h % 2], mask[h % 2], diag, ALU.add).then_inc(masked.up(), 1)
                    dve.wait_ge(masked.sem, masked.at(h + 1))

                def store(h):
                    dve.wait_ge(valued.sem, valued.at(n * (h + 1)))
                    dve.tensor_copy(y[rows(h), 5 + h // 2, 0:qw], yps[h % 2][rows(h), 0:qw]).then_inc(stored.up(), 1)

                masks(0)
                for u in range(HEADS * n):
                    h, j = divmod(u, n)
                    tile, width = keys[j]
                    dve.wait_ge(scored.sem, scored.at(u + 1))
                    if u >= 3:
                        dve.wait_ge(valued.sem, valued.at(u - 2))
                    if j < 2:
                        m = cmask[h % 2][:, 128 - 128 * j:128 - 128 * j + S]
                    else:
                        m = mask[h % 2][:, 384 - 128 * tile:384 - 128 * tile + S]
                    ins = dve.scalar_tensor_tensor(out=aw[u % 3][:, 0:S], in0=sps[u % 2][:, 0:S], scalar=HEAD ** -0.5, in1=m,
                                                   op0=ALU.mult, op1=ALU.mult)
                    if width > S:
                        m = mask[h % 2][:, 384 - 128 * j:384 - 128 * j + CTX]
                        ins = dve.scalar_tensor_tensor(out=aw[u % 3][:, S:T], in0=sps[u % 2][:, S:T], scalar=HEAD ** -0.5, in1=m,
                                                       op0=ALU.mult, op1=ALU.mult)
                    ins.then_inc(weighed.up(), 1)
                    if j == 3 and h + 1 < HEADS:
                        masks(h + 1)
                    if j == 1 and h >= 1:
                        store(h - 1)
                store(HEADS - 1)

    def retention_output(self, l, need_ctx):
        px, y = self.px, self.xn.rearrange("p (k t) -> p k t", k=KT)
        width = T if need_ctx else S
        w = self.work
        sq = [w[:, i * T:i * T + width] for i in range(3)]
        rstd = [w[:, (3 + i) * T:(3 + i) * T + width] for i in range(3)]
        ga = [w[:, (6 + i) * T:(6 + i) * T + width] for i in range(3)]
        meant, centred, squared = self.sig("summed"), self.sig("centred"), self.sig("squared")
        varied, rooted, vstep, gated = self.sig("varied"), self.sig("rooted"), self.sig("vector_step"), self.sig("gated")
        with self.stage() as block:
            @block.tensor
            def _(pe):
                for i in range(3):
                    for a, b in pieces(width):
                        mm = pe.matmul(self.ps[:, i * 1024 + a:i * 1024 + b], self.group, y[:, 5 + i, a:b], start=True, stop=True)
                    mm.then_inc(meant.up(), 1)
                for i in range(3):
                    pe.wait_ge(squared.sem, squared.at(i + 1))
                    for a, b in pieces(width):
                        mm = pe.matmul(self.ps[:, i * 1024 + a:i * 1024 + b], self.group, sq[i][:, a:b], start=True, stop=True)
                    mm.then_inc(varied.up(), 1)

            @block.scalar
            def _(act):
                for i in range(3):
                    act.activation(ga[i], px[:, GATE + i, 0:width], ACT.Silu).then_inc(gated.up(), 1)
                for i in range(3):
                    act.wait_ge(centred.sem, centred.at(i + 1))
                    act.activation(sq[i], y[:, 5 + i, 0:width], ACT.Square).then_inc(squared.up(), 1)
                for i in range(3):
                    act.wait_ge(varied.sem, varied.at(i + 1))
                    act.activation(rstd[i], self.ps[:, i * 1024:i * 1024 + width], ACT.Sqrt, bias=EPS).then_inc(rooted.up(), 1)

            @block.vector
            def _(dve):
                for i in range(3):
                    dve.wait_ge(meant.sem, meant.at(i + 1))
                    dve.tensor_tensor(y[:, 5 + i, 0:width], y[:, 5 + i, 0:width], self.ps[:, i * 1024:i * 1024 + width],
                                      ALU.subtract).then_inc(centred.up(), 1)
                for i in range(3):
                    t = y[:, 5 + i, 0:width]
                    dve.wait_ge(rooted.sem, rooted.at(i + 1))
                    settle(dve, dve.reciprocal(rstd[i], rstd[i]), vstep)
                    settle(dve, dve.scalar_tensor_tensor(out=t, in0=t, scalar=self.v(("ret_gn_g", l), i), in1=rstd[i],
                                                         op0=ALU.mult, op1=ALU.mult), vstep)
                    dve.wait_ge(gated.sem, gated.at(i + 1))
                    settle(dve, dve.tensor_tensor(t, t, ga[i], ALU.mult), vstep)

    def output_projection(self, src, segments, residual):
        width = segments[-1][1]
        units = []
        for m in range(KT):
            def pairs(w, m=m):
                ws = w[0].rearrange("p (k c) -> p k c", k=KT)
                o = (m % 2) * P
                return [((a, b), [(ws[:, k, o:o + P], src(k)[:, a:b]) for k in range(KT)]) for a, b in pieces(width)]
            units.append(([m // 2], pairs, (0, P, width)))

        def finish(eng, i, ps):
            for a, b, gate in segments:
                if gate is None:
                    ins = eng.tensor_tensor(residual(i)[:, a:b], ps[:, a:b], residual(i)[:, a:b], ALU.add)
                else:
                    ins = eng.scalar_tensor_tensor(out=residual(i)[:, a:b], in0=ps[:, a:b], scalar=gate(i), in1=residual(i)[:, a:b],
                                                   op0=ALU.mult, op1=ALU.add)
            return ins

        self.project(units, 4, finish, banks_each=2)

    def gates(self, l, which, need_ctx):
        def seg(a, b, s):
            return (a, b, lambda k: self.mods[:, l, s, which * KT + k:which * KT + k + 1])
        return [seg(0, S, 0)] + ([seg(S, T, 1)] if need_ctx else [])

    def ffn_up(self, l, need_ctx):
        xn = self.xn.rearrange("p (k t) -> p k t", k=KT)
        width = T if need_ctx else S
        g = self.big[:, 0:FT * width].rearrange("p (m t) -> p m t", m=FT)
        self.g = g
        padded = S + 2 + (CTX + 1 if need_ctx else 0)
        n = padded - 2
        w = self.work
        u = w[:, 0:4 * 772].rearrange("p (b c t) -> p b c t", b=2, c=2)
        cv = w[:, 3088:3088 + 4 * 772].rearrange("p (b c t) -> p b c t", b=2, c=2)
        runs = [(0, S, 1)] + ([(S, T, S + 2)] if need_ctx else [])
        done, copied, convolved = self.sig("product_done"), self.sig("copied"), self.sig("convolved")
        silued, zeroed, vstep, gated = self.sig("silued"), self.sig("zeroed"), self.sig("vector_step"), self.sig("gated")
        first = len(self.freed_at)
        cw = lambda j, t: self.v(("conv_w", l), j * 2 * FT + t)
        with self.stage() as block:
            @block.gpsimd
            def _(pool):
                pool.memset(w[:, 0:4 * 772], 0.0).then_inc(zeroed.up(), 1)

            @block.tensor
            def _(pe):
                for i in range(FT):
                    ws = self.strip(pe, first + i).rearrange("p (k c) -> p k c", k=KT)
                    for c in range(2):
                        if i >= 2:
                            pe.wait_ge(copied.sem, copied.at(2 * (i - 2) + c + 1))
                        out = self.ps[:, (i % 2) * 2048 + c * 1024:(i % 2) * 2048 + c * 1024 + width]
                        for a, b in pieces(width):
                            for k in range(KT):
                                mm = pe.matmul(out[:, a:b], ws[:, k, c * P:(c + 1) * P], xn[:, k, a:b], start=k == 0, stop=k == KT - 1)
                        mm.then_inc(done.up(), 1)
                    self.strips_freed(1)

            @block.sync
            def _(sp):
                self.load_strips(sp)

            @block.scalar
            def _(act):
                act.wait_ge(zeroed.sem, zeroed.at(1))

                def silu(i):
                    act.wait_ge(convolved.sem, convolved.at(2 * i + 1))
                    act.activation(cv[:, i % 2, 0, 0:n], cv[:, i % 2, 0, 0:n], ACT.Silu).then_inc(silued.up(), 1)

                for i in range(FT):
                    for c in range(2):
                        act.wait_ge(done.sem, done.at(2 * i + c + 1))
                        if i >= 2:
                            act.wait_ge(convolved.sem, convolved.at(2 * (i - 2) + c + 1))
                        for a, b, o in runs:
                            ps = self.ps[:, (i % 2) * 2048 + c * 1024 + a:(i % 2) * 2048 + c * 1024 + b]
                            ins = act.activation(u[:, i % 2, c, o:o + b - a], ps, ACT.Copy)
                        ins.then_inc(copied.up(), 1)
                    if i >= 1:
                        silu(i - 1)
                silu(FT - 1)

            @block.vector
            def _(dve):
                def gate(i):
                    dve.wait_ge(silued.sem, silued.at(i + 1))
                    dve.wait_ge(convolved.sem, convolved.at(2 * i + 2))
                    for a, b, o in runs:
                        o -= 1
                        dve.tensor_tensor(g[:, i, a:b], cv[:, i % 2, 0, o:o + b - a], cv[:, i % 2, 1, o:o + b - a], ALU.mult).then_inc(gated.up(), 1)

                for i in range(FT):
                    for c in range(2):
                        t = i + c * FT
                        uu, cc = u[:, i % 2, c, :], cv[:, i % 2, c, 0:n]
                        dve.wait_ge(copied.sem, copied.at(2 * i + c + 1))
                        if i >= 2:
                            dve.wait_ge(gated.sem, gated.at(len(runs) * (i - 1)))
                        settle(dve, dve.tensor_scalar(cc, uu[:, 1:1 + n], cw(1, t), self.v(("conv_b", l), t), ALU.mult, ALU.add), vstep)
                        settle(dve, dve.scalar_tensor_tensor(out=cc, in0=uu[:, 0:n], scalar=cw(0, t), in1=cc, op0=ALU.mult, op1=ALU.add), vstep)
                        dve.scalar_tensor_tensor(out=cc, in0=uu[:, 2:2 + n], scalar=cw(2, t), in1=cc, op0=ALU.mult, op1=ALU.add).then_inc(convolved.up(), 1)
                    if i >= 1:
                        gate(i - 1)
                gate(FT - 1)

    def ffn_down(self, l, need_ctx):
        width = T if need_ctx else S
        g, segments = self.g, self.gates(l, 5, need_ctx)
        units = []
        for m in range(KT):
            def pairs(w):
                ws = [a.rearrange("p (k c) -> p k c", k=FT // 2) for a in w]
                return [((a, b), [(ws[k // 11][:, k % 11, :], g[:, k, a:b]) for k in range(FT)]) for a, b in pieces(width)]
            units.append(([2 * m, 2 * m + 1], pairs, (0, P, width)))

        def finish(eng, i, ps):
            for a, b, gate in segments:
                ins = eng.scalar_tensor_tensor(out=self.h[:, i, a:b], in0=ps[:, a:b], scalar=gate(i), in1=self.h[:, i, a:b],
                                               op0=ALU.mult, op1=ALU.add)
            return ins

        self.project(units, 2 * KT, finish, banks_each=2)

    def layer(self, l):
        need_ctx = l < DEPTH - 1
        xn = self.xn.rearrange("p (k t) -> p k t", k=KT)
        self.norm(lambda k: xn[:, k, :], lambda k: self.h[:, k, :], KT, T, self.segments(l, 0), self.work)
        self.input_projection(l, need_ctx)
        self.pooling(l, need_ctx)
        self.rotate()
        self.neighbourhood(l)
        if need_ctx:
            self.context_attention()
        self.retention(l, need_ctx)
        self.retention_output(l, need_ctx)
        self.output_projection(lambda k: xn[:, k, :], self.gates(l, 2, need_ctx), lambda m: self.h[:, m, :])
        width = T if need_ctx else S
        self.norm(lambda k: xn[:, k, 0:width], lambda k: self.h[:, k, 0:width], KT, width, self.segments(l, 1, need_ctx), self.work)
        self.ffn_up(l, need_ctx)
        self.ffn_down(l, need_ctx)


    def bigs(self, col, n, width):
        return self.big[:, col:col + n * width].rearrange("p (n t) -> p n t", n=n)

    def xns(self, n, width, col=0):
        return self.xn[:, col:col + n * width].rearrange("p (n t) -> p n t", n=n)

    def sine(self, eng, arg, k, vstep):
        two_pi_hi = 6.28125
        two_pi_lo = 2 * math.pi - two_pi_hi
        magic = 1.5 * 2.0 ** 23
        settle(eng, eng.tensor_scalar(k, arg, 1.0 / (2 * math.pi), magic, ALU.mult, ALU.add), vstep)
        settle(eng, eng.tensor_scalar(k, k, magic, None, ALU.subtract), vstep)
        settle(eng, eng.scalar_tensor_tensor(out=arg, in0=k, scalar=-two_pi_hi, in1=arg, op0=ALU.mult, op1=ALU.add), vstep)
        settle(eng, eng.scalar_tensor_tensor(out=arg, in0=k, scalar=-two_pi_lo, in1=arg, op0=ALU.mult, op1=ALU.add), vstep)
        top = float(np.nextafter(np.float32(math.pi), np.float32(0)))
        return eng.tensor_scalar(arg, arg, top, -top, ALU.min, ALU.max)

    def hyena_filters(self):
        taps = self.bigs(0, 4, 4 * S)
        spectra = self.big[:, 8192:8192 + 9216].rearrange("p (o n c) -> p o n c", o=2, n=9)
        self.spectra = spectra
        self.dft = self.work[:, 0:6144].rearrange("p (m k f) -> p m k f", m=3, k=4)
        cos, sin = self.dft[:, 0], self.dft[:, 1]
        feats = self.xn[:, 0:2 * S]
        filt = self.xn[:, 1024:3072]
        decay = self.xn[:, 3072:5120]
        h = [self.work[:, 6144 + i * S:6144 + (i + 1) * S] for i in range(2)]
        k = self.work[:, 7168:7168 + S]
        ex = [self.work[:, 7680 + i * S:7680 + (i + 1) * S] for i in range(2)]
        f = lambda i: self.v("hy_f", i)
        self.load([(feats, self.t["hyena"]), (filt[0:65, :], self.t["filter"]), (decay[0:1, :], self.t["decay"]),
                   (self.work[:, 0:6144], self.t["dft"])])
        done, vstep, ready, sined = self.sig("product_done"), self.sig("vector_step"), self.sig("reduced"), self.sig("sined")
        with self.stage() as block:
            @block.tensor
            def _(pe):
                pe.matmul(self.ps[0:64, 0:S], self.v("w1", 0, 64)[0:33, :], feats[0:33, 0:S], start=True, stop=True).then_inc(done.up(), 1)
                pe.wait_ge(sined.sem, sined.at(2))
                pe.matmul(self.ps[0:64, 512:512 + S], self.v("w2", 0, 64)[0:64, :], h[0][0:64, :], start=True, stop=True).then_inc(done.up(), 1)

            @block.vector
            def _(dve):
                dve.memset(h[1][64:65, :], 1.0)
                for i in range(2):
                    r = slice(0, 64)
                    dve.wait_ge(done.sem, done.at(i + 1))
                    settle(dve, dve.tensor_scalar(h[i][r, :], self.ps[r, i * 512:i * 512 + S], f(i)[r, :], f(2 + i)[r, :], ALU.add, ALU.mult), vstep)
                    self.sine(dve, h[i][r, :], k[r, :], vstep).then_inc(ready.up(), 1)

            @block.scalar
            def _(act):
                act.activation(decay[0:1, :], decay[0:1, :], ACT.Abs).then_inc(sined.up(), 1)
                for i in range(2):
                    act.wait_ge(ready.sem, ready.at(i + 1))
                    act.activation(h[i][0:64, :], h[i][0:64, :], ACT.Sin).then_inc(sined.up(), 1)

        exped, multiplied = self.sig("exponentials"), self.sig("multiplied")
        units = [(t, c) for t in range(4) for c in range(4)]
        with self.stage() as block:
            @block.tensor
            def _(pe):
                for u, (t, c) in enumerate(units):
                    if u >= 4:
                        pe.wait_ge(multiplied.sem, multiplied.at(u - 3))
                    b = 2 * (u % 4)
                    pe.matmul(self.bank(b + 1), feats[0:1, S + t * P:S + (t + 1) * P], decay[0:1, c * S:(c + 1) * S], start=True, stop=True)
                    pe.matmul(self.bank(b), h[1][0:65, t * P:(t + 1) * P], filt[0:65, c * S:(c + 1) * S], start=True, stop=True).then_inc(done.up(), 1)

            @block.scalar
            def _(act):
                for u, (t, c) in enumerate(units):
                    act.wait_ge(done.sem, done.at(u + 1))
                    if u >= 2:
                        act.wait_ge(multiplied.sem, multiplied.at(u - 1))
                    act.activation(ex[u % 2], self.bank(2 * (u % 4) + 1), ACT.Exp).then_inc(exped.up(), 1)

            @block.vector
            def _(dve):
                for u, (t, c) in enumerate(units):
                    dve.wait_ge(exped.sem, exped.at(u + 1))
                    dve.tensor_tensor(taps[:, t, c * S:(c + 1) * S], self.bank(2 * (u % 4)), ex[u % 2], ALU.mult).then_inc(multiplied.up(), 1)

        combined, taken = self.sig("combined"), self.sig("taken_by_vector")
        with self.stage() as block:
            @block.vector
            def _(dve):
                for o in range(2):
                    settle(dve, dve.memset(taps[0:1, 0, (2 * o + 1) * S:(2 * o + 2) * S], 0.0), vstep)
                    for t in range(4):
                        fw, bw = taps[:, t, 2 * o * S:(2 * o + 1) * S], taps[:, t, (2 * o + 1) * S:(2 * o + 2) * S]
                        settle(dve, dve.tensor_tensor(fw, fw, bw, ALU.add), vstep)
                        dve.scalar_tensor_tensor(out=bw, in0=bw, scalar=-2.0, in1=fw, op0=ALU.mult, op1=ALU.add).then_inc(combined.up(), 1)
                for o in range(2):
                    for n in range(9):
                        u = 9 * o + n
                        dve.wait_ge(done.sem, done.at(u + 1))
                        first = 0 if n % 4 == 0 else 1
                        if n == 0:
                            settle(dve, dve.tensor_scalar(spectra[:, o, 8, :], self.bank(u % 8), self.freq_w[:, 0:1], None, ALU.mult), vstep)
                        if n == 4:
                            settle(dve, dve.tensor_scalar(spectra[:, o, n, :], self.bank(u % 8), self.freq_w[:, first:first + 1], None, ALU.mult), vstep)
                            ins = dve.memset(spectra[0:1, o, 4, :], 0.0)
                        elif n < 8:
                            ins = dve.tensor_scalar(spectra[:, o, n, :], self.bank(u % 8), self.freq_w[:, first:first + 1], None, ALU.mult)
                        else:
                            ins = dve.tensor_scalar(spectra[0:1, o, 8, :], self.bank(u % 8)[0:1, :], self.freq_w[0:1, 0:1], None, ALU.mult)
                        ins.then_inc(taken.up(), 1)

            @block.tensor
            def _(pe):
                for o in range(2):
                    pe.wait_ge(combined.sem, combined.at(4 * (o + 1)))
                    for n in range(9):
                        u = 9 * o + n
                        if u >= 8:
                            pe.wait_ge(taken.sem, taken.at(u - 7))
                        table, half, m = (cos, 0, n) if n < 4 else (sin, 1, n - 4)
                        for t in range(4):
                            if n < 8:
                                lhs, out = table[:, t, m * P:(m + 1) * P], self.bank(u % 8)
                            else:
                                lhs, out, half = sin[:, t, 0:1], self.bank(u % 8)[0:1, :], 0
                            mm = pe.matmul(out, lhs, taps[:, t, (2 * o + half) * S:(2 * o + half + 1) * S], start=t == 0, stop=t == 3)
                        mm.then_inc(done.up(), 1)

    def second_projection(self):
        xn = self.xns(KT, S)
        p2 = self.bigs(0, 16, S)
        self.p2 = p2
        units = []
        for m in range(16):
            s = m // 2 if m < 2 else (1 if m < 4 else 2 + (m - 4) // 2)
            def pairs(w, m=m, s=s):
                ws = w[0].rearrange("p (k c) -> p k c", k=KT)
                o, n = (128, 32) if m == MKR else ((m % 2) * P if m != MKV else 0, P)
                return [((0, S), [(ws[:, k, o:o + n], xn[:, k, :]) for k in range(KT)])]
            units.append(([0 if m < 2 else s], pairs, (64, 32, S) if m == MKR else (0, P, S)))

        def finish(eng, i, ps):
            dst = p2[64:96, i, :] if i == MKR else p2[:, i, :]
            return eng.tensor_copy(dst, ps)

        self.project(units, 8, finish)

    def hyena(self):
        p2, u = self.p2, self.xns(4, 3 * S)
        free = self.big[:, 2048:8192]
        cos, sin, sint = self.dft[:, 0], self.dft[:, 1], self.dft[:, 2]
        cv = [self.work[:, 6144 + i * S:6144 + (i + 1) * S] for i in range(2)]
        done, vstep, conv, turned = self.sig("product_done"), self.sig("vector_step"), self.sig("convolved"), self.sig("turned")
        copied = self.sig("copied")
        with self.stage() as block:
            @block.vector
            def _(dve):
                for i in range(12):
                    src, c = p2[:, HY + i, :], cv[i % 2]
                    if i >= 2:
                        dve.wait_ge(turned.sem, turned.at(i - 1))
                    settle(dve, dve.tensor_scalar(c, src, self.v("hy_cw", 12 + i), self.v("hy_cb", i), ALU.mult, ALU.add), vstep)
                    settle(dve, dve.scalar_tensor_tensor(out=c[:, 1:S], in0=src[:, 0:S - 1], scalar=self.v("hy_cw", i), in1=c[:, 1:S],
                                                         op0=ALU.mult, op1=ALU.add), vstep)
                    dve.scalar_tensor_tensor(out=c[:, 0:S - 1], in0=src[:, 1:S], scalar=self.v("hy_cw", 24 + i), in1=c[:, 0:S - 1],
                                             op0=ALU.mult, op1=ALU.add).then_inc(conv.up(), 1)

            @block.tensor
            def _(pe):
                for i in range(12):
                    pe.wait_ge(conv.sem, conv.at(i + 1))
                    if i >= 4:
                        pe.wait_ge(copied.sem, copied.at(i - 3))
                    for t in range(4):
                        mm = pe.transpose(self.bank(i % 4)[:, t * P:(t + 1) * P], cv[i % 2][:, t * P:(t + 1) * P], self.ident)
                    mm.then_inc(turned.up(), 1)

            @block.scalar
            def _(act):
                for i in range(12):
                    act.wait_ge(turned.sem, turned.at(i + 1))
                    act.activation(u[:, :, i * P:(i + 1) * P], self.bank(i % 4).rearrange("p (t c) -> p t c", t=4), ACT.Copy).then_inc(copied.up(), 1)

        y = self.bigs(2048, 8, S)
        tmp = [self.work[:, 6144 + i * S:6144 + (i + 1) * S] for i in range(4)]
        skip = self.work[:, 8192:9216]
        self.load([(skip, self.t["skip"])])
        z = [u[:, t, 2 * S:3 * S] for t in range(4)]
        taken, filtered, gated = self.sig("taken_by_vector"), self.sig("filtered"), self.sig("gated")
        for o in range(2):
            sp = self.spectra[:, o]
            with self.stage() as block:
                @block.tensor
                def _(pe):
                    for m in range(4):
                        for half, table in enumerate((cos, sin)):
                            for t in range(4):
                                mm = pe.matmul(self.bank(2 * m + half), table[:, t, m * P:(m + 1) * P], z[t], start=t == 0, stop=t == 3)
                            mm.then_inc(done.up(), 1)
                    for t in range(4):
                        pe.wait_ge(filtered.sem, filtered.at(4))
                        for m in range(4):
                            pe.matmul(self.bank(t), cos[:, m, t * P:(t + 1) * P], y[:, m, :], start=m == 0, stop=False)
                            mm = pe.matmul(self.bank(t), sint[:, m, t * P:(t + 1) * P], y[:, 4 + m, :], start=False, stop=m == 3)
                        mm.then_inc(done.up(), 1)

                @block.vector
                def _(dve):
                    for m in range(4):
                        dve.wait_ge(done.sem, done.at(2 * m + 2))
                        re, im = self.bank(2 * m), self.bank(2 * m + 1)
                        kc, ks, kd = sp[:, m, :], sp[:, 4 + m, :], sp[:, 8 if m == 0 else m, :]
                        a, b = tmp[2 * (m % 2)], tmp[2 * (m % 2) + 1]
                        dve.tensor_tensor(y[:, m, :], re, kc, ALU.mult)
                        dve.tensor_tensor(a, im, ks, ALU.mult)
                        dve.tensor_tensor(y[:, 4 + m, :], re, ks, ALU.mult)
                        settle(dve, dve.tensor_tensor(b, im, kd, ALU.mult), vstep)
                        settle(dve, dve.tensor_tensor(y[:, m, :], y[:, m, :], a, ALU.subtract), vstep)
                        dve.tensor_tensor(y[:, 4 + m, :], y[:, 4 + m, :], b, ALU.add).then_inc(filtered.up(), 1)
                    for t in range(4):
                        if t >= 2:
                            dve.wait_ge(gated.sem, gated.at(t - 1))
                        settle(dve, dve.tensor_tensor(tmp[t % 2], z[t], skip[:, o * S:(o + 1) * S], ALU.mult), vstep)
                        dve.wait_ge(done.sem, done.at(9 + t))
                        settle(dve, dve.tensor_tensor(tmp[t % 2], self.bank(t), tmp[t % 2], ALU.add), vstep)
                        dve.tensor_tensor(z[t], tmp[t % 2], u[:, t, o * S:(o + 1) * S], ALU.mult).then_inc(gated.up(), 1)

        self.mix = self.bigs(8192, 8, S)
        squared, rooted, normed = self.sig("squared"), self.sig("rooted"), self.sig("normalised")
        ss, rs = self.small[:, 0:4], self.small[:, 4:8]
        with self.stage() as block:
            @block.scalar
            def _(act):
                for t in range(4):
                    act.activation(tmp[t], z[t], ACT.Square, accum_out=ss[:, t:t + 1]).then_inc(squared.up(), 1)
                act.wait_ge(squared.sem, squared.at(4))
                act.activation(rs, ss, ACT.Sqrt, scale=1.0 / S, bias=EPS).then_inc(rooted.up(), 1)

            @block.vector
            def _(dve):
                dve.wait_ge(rooted.sem, rooted.at(1))
                settle(dve, dve.reciprocal(rs, rs), vstep)
                for t in range(4):
                    dve.tensor_scalar(z[t], z[t], rs[:, t:t + 1], None, ALU.mult).then_inc(normed.up(), 1)
                for i in range(4):
                    dve.wait_ge(turned.sem, turned.at(i + 1))
                    dve.tensor_scalar(self.mix[:, 4 + i, :], self.bank(i), self.v("hyout_g", i), None, ALU.mult)

            @block.tensor
            def _(pe):
                pe.wait_ge(normed.sem, normed.at(4))
                for i in range(4):
                    for t in range(4):
                        mm = pe.transpose(self.bank(i)[:, t * P:(t + 1) * P], z[t][:, i * P:(i + 1) * P], self.ident)
                    mm.then_inc(turned.up(), 1)

    def latent_attention(self):
        p2, mix = self.p2, self.mix
        whole = lambda gain: [(0, S, gain, None)]
        self.norm(lambda k: p2[:, MQ + k, :], lambda k: p2[:, MQ + k, :], 2, S, whole(lambda k: self.v("q_g", k)), self.work)
        self.norm(lambda k: p2[:, MKV, :], lambda k: p2[:, MKV, :], 1, S, whole(lambda k: self.v("kv_g")), self.work)
        q = self.bigs(12288, MLA_HEADS, S)
        kk = self.xns(MLA_HEADS, S)
        v = self.xns(4, S, 4096)
        units, dst = [], []
        for h in range(MLA_HEADS):
            def pairs(w, h=h):
                ws = w[0].rearrange("p (k c) -> p k c", k=2)
                return [((0, S), [(ws[:, k, h * 96:(h + 1) * 96], p2[:, MQ + k, :]) for k in range(2)])]
            units.append(([0], pairs, (0, 96, S)))
            dst.append(q[0:96, h, :])
        for h in range(MLA_HEADS):
            units.append(([1], lambda w, h=h: [((0, S), [(w[0][:, h * 64:(h + 1) * 64], p2[:, MKV, :])])], (0, 64, S)))
            dst.append(kk[0:64, h, :])
        for t in range(4):
            units.append(([1], lambda w, t=t: [((0, S), [(p2[:, MKV, t * P:(t + 1) * P], w[0][:, 512:1024])])], (0, P, S)))
            dst.append(v[:, t, :])

        def finish(eng, i, ps):
            if eng is self.nc.scalar:
                return eng.activation(dst[i], ps, ACT.Copy)
            return eng.tensor_copy(dst[i], ps)

        self.project(units, 2, finish)
        w = self.work
        tables = (w[:, 0:S], w[:, S:2 * S], w[:, 2 * S:2 * S + P])
        tmp = [w[:, 1152 + i * S:1152 + (i + 1) * S] for i in range(2)]
        self._rotate([q[0:96, h, :] for h in range(MLA_HEADS)], 0, 96, *tables, tmp, self.t["rope96"], w[:, 0:1152])
        self._rotate([p2[64:96, MKR, :]], 64, 32, *tables, tmp, self.t["rope96"], w[:, 0:1152])
        with self.stage() as block:
            @block.vector
            def _(dve):
                for h in range(MLA_HEADS):
                    dve.tensor_copy(kk[64:96, h, :], p2[64:96, MKR, :])
        def rows(h):
            return slice(64 * (h % 2), 64 * (h % 2) + 64)
        self.attention(
            MLA_HEADS, 4, S, 1,
            q=lambda h, i: [q[0:96, h, i * P:(i + 1) * P]],
            k=lambda h: [[(0, S, kk[0:96, h, :])]],
            bias=None,
            v=lambda h, j, n: v[:, j, h * 64:(h + 1) * 64],
            outs=lambda h: [mix[rows(h), h // 2, :]],
            scale=96 ** -0.5, tmp=self.work)
        self.norm(lambda k: mix[:, k, :], lambda k: mix[:, k, :], 4, S, whole(lambda k: self.v("attn_g", k)), self.work)

    def memory_attention(self):
        xn = self.xns(KT, S)
        self.norm(lambda k: xn[:, k, :], lambda k: self.x[:, k, :], KT, S, [(0, S, lambda k: self.v("cross_g", k), None)], self.work,
                  load=[(self.big[:, 0:2048].rearrange("p (k t) -> p k t", k=KT), self.t["memory"])])
        mem, hm = self.bigs(0, KT, 256), self.bigs(2048, KT, 256)
        self.norm(lambda k: hm[:, k, :], lambda k: mem[:, k, :], KT, 256, [(0, 256, lambda k: self.v("mem_g", k), None)], self.work)
        keys, v, q, o = self.bigs(4096, KT, 256), self.bigs(6144, 2, D), self.bigs(8192, KT, S), self.bigs(12288, KT, S)
        units, dst = [], []

        def feature(strip, m, src, width):
            def pairs(w):
                ws = w[0].rearrange("p (k c) -> p k c", k=KT)
                return [((0, width), [(ws[:, k, (m % 2) * P:(m % 2 + 1) * P], src[:, k, :]) for k in range(KT)])]
            units.append(([strip + m // 2], pairs, (0, P, width)))

        for m in range(KT):
            feature(0, m, hm, 256)
            dst.append(keys[:, m, :])
        for c in range(4):
            for t in range(2):
                def pairs(w, t=t):
                    ws = w[0].rearrange("p (k c) -> p k c", k=KT)
                    return [((0, 256), [(hm[:, k, t * P:(t + 1) * P], ws[:, k, :]) for k in range(KT)])]
                units.append(([4 + c], pairs, (0, P, 256)))
                dst.append(v[:, t, c * 256:(c + 1) * 256])
        for m in range(KT):
            feature(8, m, xn, S)
            dst.append(q[:, m, :])
        self.project(units, 12, lambda eng, i, ps: eng.tensor_copy(dst[i], ps))
        self.attention(
            MEM_HEADS, 4, 256, 2,
            q=lambda h, i: [q[:, 2 * h + d, i * P:(i + 1) * P] for d in range(2)],
            k=lambda h: [[(0, 256, keys[:, 2 * h + d, :])] for d in range(2)],
            bias=None,
            v=lambda h, j, n: v[:, j, h * 256 + n * P:h * 256 + (n + 1) * P],
            outs=lambda h: [o[:, 2 * h + n, :] for n in range(2)],
            scale=1.0 / 16, tmp=self.work)
        self.output_projection(lambda k: o[:, k, :], [(0, S, None)], lambda m: self.x[:, m, :])

    def route(self):
        xn = self.xns(KT, S)
        w = self.work[:, 9600:9888].rearrange("p (k c) -> p k c", k=KT)
        tokens = self.work[:, 0:4 * D].rearrange("p (t c) -> p t c", t=4)
        tmp = self.work[:, 4 * D:9088]
        at = [0]

        def take(*dims):
            n = int(np.prod(dims))
            a = tmp[:, at[0]:at[0] + n]
            at[0] += n
            return a.rearrange("p (a b) -> p a b", a=dims[0]) if len(dims) > 1 else a

        logits = take(4, 36)
        one_g, ex, picked = take(4, 4), take(4, 4), take(4, 32)
        e_in, one_1, one_2, rest, weight = take(4, 8), take(4, 8), take(4, 8), take(4, 8), take(4, 8)
        comb, chosen_1, chosen_2, chosen, position = take(4, 32), take(4, 32), take(4, 32), take(4, 32), take(4, 32)
        top, total, v1, v2, p1, p2, m = (take(4) for _ in range(7))
        pos, crowd = take(4), take(4)
        self.share = self.small[:, 64:72]
        self.slot_of = self.small[:, 72:80].bitcast(mybir.dt.uint32)
        numbers = self.small[:, 80:84].bitcast(mybir.dt.uint32)
        zeros = self.small[:, 84:100].bitcast(mybir.dt.uint32)
        self.token_of = self.small[:, 100:116].bitcast(mybir.dt.uint32)
        self.crowded = self.small[:, 116:117].bitcast(mybir.dt.int32)
        self.norm(lambda k: xn[:, k, :], lambda k: self.x[:, k, :], KT, S, [(0, S, lambda k: self.v("ffn_g", k), None)], self.work,
                  load=[(w, self.t["route"])])
        done, vstep, exped, ready = self.sig("product_done"), self.sig("vector_step"), self.sig("exponentials"), self.sig("argued")
        turned, copied, stored = self.sig("turned"), self.sig("copied"), self.sig("outputs_stored")
        comb_t = self.work[:, 9088:9600]
        self.comb_dram = self.nc.dram_tensor("combine", [EXPERTS, S], F32, kind="Internal").ap()
        self.tokens_dram = self.nc.dram_tensor("token_rows", [S, D], F32, kind="Internal").ap()
        self.table_dram = self.nc.dram_tensor("slot_table", [EXPERTS * SLOTS, 1], mybir.dt.uint32, kind="Internal").ap()
        chose, ranked, token_copied = self.sig("combined"), self.sig("valued"), self.sig("gated")
        cleared, zeroed, located = self.sig("table_cleared"), self.sig("zeroed"), self.sig("squared")
        wide = lambda a, n: a.unsqueeze(2).to_broadcast([P, 4, n])
        rank = lambda n: self.rank[:, 8 - n:8].unsqueeze(1).to_broadcast([P, 4, n])
        with self.stage() as block:
            @block.tensor
            def _(pe):
                for t in range(4):
                    for k in range(KT):
                        mm = pe.matmul(self.ps[:, t * 36:(t + 1) * 36], xn[:, k, t * P:(t + 1) * P], w[:, k, :], start=k == 0, stop=k == KT - 1)
                mm.then_inc(done.up(), 1)
                for t in range(4):
                    if t >= 2:
                        pe.wait_ge(token_copied.sem, token_copied.at(t - 1))
                    for k in range(KT):
                        mm = pe.transpose(self.ps[:, 2048 + (t % 2) * 1024 + k * P:2048 + (t % 2) * 1024 + (k + 1) * P],
                                          xn[:, k, t * P:(t + 1) * P], self.ident)
                    mm.then_inc(turned.up(), 1)
                pe.wait_ge(chose.sem, chose.at(1))
                for t in range(5):
                    for j in range(min(t + 1, 4)):
                        mm = pe.matmul(self.ps[:, 1024 + t * 32:1024 + (t + 1) * 32], self.earlier if j == t else self.ones,
                                       chosen[:, j, :], start=j == 0, stop=j == min(t, 3))
                mm.then_inc(ranked.up(), 1)
                pe.wait_ge(ready.sem, ready.at(3))
                for t in range(4):
                    mm = pe.transpose(self.ps[0:32, 512 + t * P:512 + (t + 1) * P], comb[:, t, :], self.ident)
                mm.then_inc(turned.up(), 1)

            @block.scalar
            def _(act):
                for t in range(4):
                    act.wait_ge(turned.sem, turned.at(t + 1))
                    act.activation(tokens[:, t, :], self.ps[:, 2048 + (t % 2) * 1024:3072 + (t % 2) * 1024], ACT.Copy).then_inc(token_copied.up(), 1)
                act.wait_ge(ready.sem, ready.at(1))
                act.activation(ex, ex, ACT.Exp).then_inc(exped.up(), 1)
                act.wait_ge(ready.sem, ready.at(2))
                act.activation(p2, p2, ACT.Exp).then_inc(exped.up(), 1)

            @block.vector
            def _(dve):
                def do(ins):
                    settle(dve, ins, vstep)

                def first_best(hot, values, best, n):
                    do(dve.tensor_tensor(hot, values, wide(best, n), ALU.is_equal))
                    do(dve.tensor_tensor(hot, hot, rank(n), ALU.mult))
                    do(dve.reduce_max(m, hot, AX))
                    do(dve.tensor_tensor(hot, hot, wide(m, n), ALU.is_equal))

                dve.wait_ge(done.sem, done.at(1))
                do(dve.tensor_tensor(logits.rearrange("p a b -> p (a b)"), self.ps[:, 0:144], self.v("route_b", 0, 144), ALU.add))
                g, e = logits[:, :, 0:4], logits[:, :, 4:36]
                do(dve.reduce_max(top, g, AX))
                dve.tensor_tensor(ex, g, wide(top, 4), ALU.subtract).then_inc(ready.up(), 1)
                first_best(one_g, g, top, 4)
                for i in range(GROUPS):
                    do(dve.tensor_tensor(picked[:, :, i * 8:(i + 1) * 8], e[:, :, i * 8:(i + 1) * 8], one_g[:, :, i:i + 1].to_broadcast([P, 4, 8]), ALU.mult))
                do(dve.tensor_tensor(e_in, picked[:, :, 0:8], picked[:, :, 8:16], ALU.add))
                do(dve.tensor_tensor(e_in, e_in, picked[:, :, 16:24], ALU.add))
                do(dve.tensor_tensor(e_in, e_in, picked[:, :, 24:32], ALU.add))
                do(dve.reduce_max(v1, e_in, AX))
                first_best(one_1, e_in, v1, 8)
                do(dve.scalar_tensor_tensor(out=rest, in0=one_1, scalar=-3.0e38, in1=e_in, op0=ALU.mult, op1=ALU.add))
                do(dve.reduce_max(v2, rest, AX))
                first_best(one_2, rest, v2, 8)
                dve.tensor_tensor(p2, v2, v1, ALU.subtract).then_inc(ready.up(), 1)
                dve.wait_ge(exped.sem, exped.at(2))
                do(dve.reduce_sum(total, ex, AX))
                do(dve.tensor_scalar(p1, p2, 1.0, None, ALU.add))
                do(dve.tensor_tensor(p1, p1, total, ALU.mult))
                do(dve.reciprocal(p1, p1))
                do(dve.tensor_tensor(p2, p2, p1, ALU.mult))
                for i in range(GROUPS):
                    r = slice(i * 8, (i + 1) * 8)
                    hot = one_g[:, :, i:i + 1].to_broadcast([P, 4, 8])
                    do(dve.tensor_tensor(chosen_1[:, :, r], one_1, hot, ALU.mult))
                    do(dve.tensor_tensor(chosen_2[:, :, r], one_2, hot, ALU.mult))
                dve.tensor_tensor(chosen, chosen_1, chosen_2, ALU.add).then_inc(chose.up(), 1)
                do(dve.tensor_copy(numbers, self.token_number))
                dve.wait_ge(ranked.sem, ranked.at(1))
                do(dve.tensor_tensor(position, self.ps[:, 1024:1152].rearrange("p (t e) -> p t e", t=4),
                                     self.first_slot.unsqueeze(1).to_broadcast([P, 4, 32]), ALU.add))
                for i, c in enumerate((chosen_1, chosen_2)):
                    do(dve.tensor_tensor(c, c, position, ALU.mult))
                    do(dve.reduce_sum(pos, c, AX))
                    do(dve.tensor_copy(self.slot_of[:, i * 4:(i + 1) * 4], pos))
                do(dve.reduce_max(crowd[:, 0:1], self.ps[:, 1152:1184], AX))
                do(dve.tensor_scalar(crowd[:, 1:2], crowd[:, 0:1], float(SLOTS), None, ALU.is_gt))
                do(dve.tensor_copy(self.crowded, crowd[:, 1:2]))
                do(dve.tensor_copy(self.share[:, 0:4], p1))
                do(dve.tensor_copy(self.share[:, 4:8], p2))
                do(dve.tensor_tensor(one_1, one_1, wide(p1, 8), ALU.mult))
                do(dve.tensor_tensor(one_2, one_2, wide(p2, 8), ALU.mult))
                do(dve.tensor_tensor(weight, one_1, one_2, ALU.add))
                for i in range(GROUPS):
                    ins = dve.tensor_tensor(comb[:, :, i * 8:(i + 1) * 8], weight, one_g[:, :, i:i + 1].to_broadcast([P, 4, 8]), ALU.mult)
                    if i < GROUPS - 1:
                        do(ins)
                ins.then_inc(ready.up(), 1)
                dve.wait_ge(turned.sem, turned.at(5))
                dve.tensor_copy(comb_t[0:32, :], self.ps[0:32, 512:1024]).then_inc(copied.up(), 1)

            @block.gpsimd
            def _(pool):
                pool.memset(zeros, 0).then_inc(zeroed.up(), 1)
                pool.wait_ge(zeroed.sem, zeroed.at(1))
                pool.dma_start(self.table_dram.rearrange("(p c) o -> p (c o)", p=P), zeros).then_inc(cleared.up(16), 16)
                pool.wait_ge(cleared.sem, cleared.at(16))

            @block.sync
            def _(sp):
                sp.wait_ge(token_copied.sem, token_copied.at(4))
                sp.dma_start(self.tokens_dram.rearrange("(t p) c -> p t c", p=P), tokens).then_inc(stored.up(16), 16)
                sp.wait_ge(copied.sem, copied.at(1))
                sp.dma_start(self.comb_dram, comb_t[0:32, :]).then_inc(stored.up(16), 16)
                sp.wait_ge(stored.sem, stored.at(32))

    def experts(self):
        sparse, dense = SparseExperts(self), DenseExperts(self)

        def flag(engine):
            return engine.value_load(self.crowded[0:1, 0:1], min_val=0, max_val=1)

        with self.stage() as block:
            @block.sync
            def _(sp):
                with sp.If(flag(sp) == 0):
                    sparse.sync(sp)
                with sp.Else():
                    dense.sync(sp)

            @block.tensor
            def _(pe):
                with pe.If(flag(pe) == 0):
                    sparse.tensor(pe)
                with pe.Else():
                    dense.tensor(pe)

            @block.scalar
            def _(act):
                with act.If(flag(act) == 0):
                    sparse.scalar(act)
                with act.Else():
                    dense.scalar(act)

            @block.vector
            def _(dve):
                with dve.If(flag(dve) == 0):
                    sparse.vector(dve)
                with dve.Else():
                    dense.vector(dve)

            @block.gpsimd
            def _(pool):
                with pool.If(flag(pool) == 0):
                    sparse.gpsimd(pool)
                with pool.Else():
                    dense.gpsimd(pool)

    def finish(self):
        rows = self.big[:, 0:8192].rearrange("p (e t c) -> p e t c", e=2, t=4)
        y = self.xn[:, 0:4 * D].rearrange("p (t c) -> p t c", t=4)
        gain, sq = self.work[:, 0:D], self.work[:, D:2 * D]
        ss, rs = self.small[:, 0:4], self.small[:, 4:8]
        turned, summed, squared, rooted = self.sig("turned"), self.sig("summed"), self.sig("squared"), self.sig("rooted")
        vstep, ready, stored, landed = self.sig("vector_step"), self.sig("normalised"), self.sig("outputs_stored"), self.sig("inputs_landed")
        ps = [self.ps[:, t * D:(t + 1) * D] for t in range(4)]
        with self.stage() as block:
            @block.tensor
            def _(pe):
                for t in range(4):
                    for k in range(KT):
                        mm = pe.transpose(ps[t][:, k * P:(k + 1) * P], self.x[:, k, t * P:(t + 1) * P], self.ident)
                    mm.then_inc(turned.up(), 1)

            @block.vector
            def _(dve):
                for t in range(4):
                    dve.wait_ge(turned.sem, turned.at(t + 1))
                    settle(dve, dve.scalar_tensor_tensor(out=y[:, t, :], in0=rows[:, 0, t, :], scalar=self.share[:, t:t + 1], in1=ps[t],
                                                         op0=ALU.mult, op1=ALU.add), vstep)
                    dve.scalar_tensor_tensor(out=y[:, t, :], in0=rows[:, 1, t, :], scalar=self.share[:, 4 + t:5 + t], in1=y[:, t, :],
                                             op0=ALU.mult, op1=ALU.add).then_inc(summed.up(), 1)
                dve.wait_ge(rooted.sem, rooted.at(1))
                dve.wait_ge(landed.sem, landed.at(16))
                settle(dve, dve.reciprocal(rs, rs), vstep)
                for t in range(4):
                    dve.scalar_tensor_tensor(out=y[:, t, :], in0=y[:, t, :], scalar=rs[:, t:t + 1], in1=gain,
                                             op0=ALU.mult, op1=ALU.mult).then_inc(ready.up(), 1)

            @block.scalar
            def _(act):
                for t in range(4):
                    act.wait_ge(summed.sem, summed.at(t + 1))
                    if t >= 1:
                        act.wait_ge(squared.sem, squared.at(t))
                    act.activation(sq, y[:, t, :], ACT.Square, accum_out=ss[:, t:t + 1]).then_inc(squared.up(), 1)
                act.wait_ge(squared.sem, squared.at(4))
                act.activation(rs, ss, ACT.Sqrt, scale=1.0 / D, bias=EPS).then_inc(rooted.up(), 1)

            @block.sync
            def _(sp):
                sp.dma_start(gain, self.t["last_gain"]).then_inc(landed.up(16), 16)
                for t in range(4):
                    sp.wait_ge(ready.sem, ready.at(t + 1))
                    sp.dma_start(self.out[t * P:(t + 1) * P, :], y[:, t, :]).then_inc(stored.up(16), 16)
                sp.wait_ge(stored.sem, stored.at(64))

    def second(self):
        xn = self.xns(KT, S)
        whole = lambda name: [(0, S, lambda k: self.v(name, k), None)]
        stream = lambda k: self.x[:, k, :]
        self.norm(stream, stream, KT, S, whole("final_g"), self.work)
        self.hyena_filters()
        self.norm(lambda k: xn[:, k, :], stream, KT, S, whole("mix_g"), self.work[:, 6144:])
        self.second_projection()
        self.hyena()
        self.latent_attention()
        self.output_projection(lambda k: self.mix[:, k, :], [(0, S, None)], stream)
        self.memory_attention()
        self.route()
        self.experts()
        self.finish()


class DenseExperts:

    turns = EXPERTS // 2

    def __init__(self, b):
        self.b, nc = b, b.nc
        self.xn = b.xns(KT, S)
        big = b.big
        self.gu = [big[:, e * 6144:e * 6144 + 4096].rearrange("p (k c) -> p k c", k=KT) for e in range(2)]
        self.dn = [big[:, e * 6144 + 4096:(e + 1) * 6144].rearrange("p (k c) -> p k c", k=2) for e in range(2)]
        self.comb = [big[:, 12288 + i * S:12288 + (i + 1) * S] for i in range(2)]
        self.act_t = [big[:, 13312 + i * S:13312 + (i + 1) * S] for i in range(2)]
        self.hidden = [b.work[:, i * S:(i + 1) * S] for i in range(4)]
        self.gu_landed = [nc.alloc_semaphore(f"dense_gate_up_landed_{i}") for i in range(2)]
        self.dn_landed = [nc.alloc_semaphore(f"dense_down_landed_{i}") for i in range(2)]
        self.comb_landed = [nc.alloc_semaphore(f"combine_landed_{i}") for i in range(2)]
        self.cleared = nc.alloc_semaphore("dense_shares_cleared")
        (self.up_done, self.silued, self.hidden_done, self.down_done, self.added, self.weighed) = (
            nc.alloc_semaphore("dense_" + n) for n in ("up_done", "silu_done", "hidden_done", "down_done", "added", "silu_weighed"))

    def sync(self, sp):
        t = self.b.t["experts"]

        def load_gu(it, e):
            sp.dma_start(self.gu[e].rearrange("p k c -> p (k c)"), t[bass.ds(it * 2 + e, 1), :, 0:4096].rearrange("a p c -> (a p) c"))\
                .then_inc(self.gu_landed[e], 16)

        def load_dn(it, e):
            sp.dma_start(self.dn[e].rearrange("p k c -> p (k c)"), t[bass.ds(it * 2 + e, 1), :, 4096:6144].rearrange("a p c -> (a p) c"))\
                .then_inc(self.dn_landed[e], 16)

        def load_comb(it, e):
            sp.dma_start(self.comb[e], self.b.comb_dram[bass.ds(it * 2 + e, 1), :].to_broadcast([P, S])).then_inc(self.comb_landed[e], 16)

        for e in range(2):
            load_gu(0, e)
            load_comb(0, e)
            load_dn(0, e)
        with sp.Fori(1, self.turns) as it:
            for e in range(2):
                sp.wait_ge(self.up_done, it * 8 - 4 + 4 * e)
                load_gu(it, e)
                sp.wait_ge(self.hidden_done, it * 4 - 2 + 2 * e)
                load_comb(it, e)
            sp.wait_ge(self.down_done, it * 8)
            for e in range(2):
                load_dn(it, e)

    def tensor(self, pe):
        b = self.b
        with pe.Fori(0, self.turns) as it:
            for e in range(2):
                pe.wait_ge(self.gu_landed[e], it * 16 + 16)
                for m in range(2):
                    for j in range(2):
                        if e == 1:
                            pe.wait_ge(self.hidden_done, it * 4 + m + 1)
                        c = 256 * j + m * P
                        for k in range(KT):
                            mm = pe.matmul(b.bank(2 * m + j), self.gu[e][:, k, c:c + P], self.xn[:, k, :], start=k == 0, stop=k == KT - 1)
                        mm.then_inc(self.up_done, 1)
            for half in range(2):
                for e in range(2):
                    if half == 0:
                        pe.wait_ge(self.dn_landed[e], it * 16 + 16)
                        pe.wait_ge(self.hidden_done, it * 4 + 2 + 2 * e)
                    for d in range(4):
                        if e == 0 and half == 1:
                            pe.wait_ge(self.added, it * 8 + d + 1)
                        c = (4 * half + d) * P
                        for k in range(2):
                            mm = pe.matmul(b.bank(4 + d), self.dn[e][:, k, c:c + P], self.hidden[2 * e + k], start=e == 0 and k == 0, stop=e == 1 and k == 1)
                        if e == 1:
                            mm.then_inc(self.down_done, 1)

    def scalar(self, act):
        with act.Fori(0, self.turns) as it:
            for e in range(2):
                for m in range(2):
                    act.wait_ge(self.up_done, it * 8 + 4 * e + 2 * m + 1)
                    if e == 1:
                        act.wait_ge(self.hidden_done, it * 4 + m + 1)
                    act.activation(self.act_t[m], self.b.bank(2 * m), ACT.Silu).then_inc(self.silued, 1)

    def vector(self, dve):
        b = self.b
        with dve.Fori(0, self.turns) as it:
            for e in range(2):
                dve.wait_ge(self.comb_landed[e], it * 16 + 16)
                for m in range(2):
                    i = 2 * e + m
                    dve.wait_ge(self.silued, it * 4 + i + 1)
                    dve.tensor_tensor(self.act_t[m], self.act_t[m], self.comb[e], ALU.mult).then_inc(self.weighed, 1)
                    dve.wait_ge(self.weighed, it * 4 + i + 1)
                    dve.wait_ge(self.up_done, it * 8 + 4 * e + 2 * m + 2)
                    dve.tensor_tensor(self.hidden[i], b.bank(2 * m + 1), self.act_t[m], ALU.mult).then_inc(self.hidden_done, 1)
            for d in range(8):
                dve.wait_ge(self.down_done, it * 8 + d + 1)
                dve.tensor_tensor(b.x[:, d, :], b.bank(4 + d % 4), b.x[:, d, :], ALU.add).then_inc(self.added, 1)

    def gpsimd(self, pool):
        pool.wait_ge(self.down_done, self.turns * 8)
        pool.memset(self.b.big[:, 0:8192], 0.0).then_inc(self.cleared, 1)
        pool.wait_ge(self.cleared, 1)


class SparseExperts:

    turns = EXPERTS // 4

    def __init__(self, b):
        self.b, nc = b, b.nc
        big, ring, w = b.big, b.ring, b.work
        gu = [big[:, i * 4096:(i + 1) * 4096] for i in range(3)] + [ring[:, 0:4096]]
        dn = [big[:, 12288:14336], big[:, 14336:16384], ring[:, 4096:6144], ring[:, 6144:8192]]
        self.gu_at, self.dn_at = gu, dn
        self.gu = [a.rearrange("p (k c) -> p k c", k=KT) for a in gu]
        self.dn = [a.rearrange("p (k c) -> p k c", k=2) for a in dn]
        self.rows = [ring[:, 8192:9216], ring[:, 9216:10240]]
        self.rows_t = w[:, 0:D].rearrange("p (k s) -> p k s", k=KT)
        self.silu_t, self.hidden = w[:, D:D + 256], w[:, D + 256:D + 512]
        self.hidden_t = w[:, D + 512:D + 768].rearrange("p (k s) -> p k s", k=2)
        self.result = [w[:, 2048:3072], w[:, 3072:4096]]
        self.out_dram = nc.dram_tensor("expert_rows", [EXPERTS * SLOTS, D], F32, kind="Internal").ap()
        self.gu_landed = [nc.alloc_semaphore(f"gate_up_landed_{i}") for i in range(4)]
        self.dn_landed = [nc.alloc_semaphore(f"down_landed_{i}") for i in range(4)]
        self.gathered = [nc.alloc_semaphore(f"rows_gathered_{i}") for i in range(2)]
        self.stored = [nc.alloc_semaphore(f"rows_stored_{i}") for i in range(2)]
        (self.rows_turned, self.rows_copied, self.up_done, self.silued, self.hidden_done, self.hidden_turned,
         self.hidden_copied, self.down_done, self.result_done, self.placed, self.table_read,
         self.shares_landed) = (nc.alloc_semaphore("sparse_" + n) for n in (
             "rows_turned", "rows_copied", "up_done", "silu_done", "hidden_done", "hidden_turned", "hidden_copied",
             "down_done", "result_done", "placed", "table_read", "shares_landed"))

    def sync(self, sp):
        t = self.b.t["experts"]

        def load(it, i, part):
            src = t[bass.ds(it * 4 + i, 1), :, 0:4096] if part == 0 else t[bass.ds(it * 4 + i, 1), :, 4096:6144]
            dst, landed = ((self.gu_at, self.gu_landed), (self.dn_at, self.dn_landed))[part]
            sp.dma_start(dst[i], src.rearrange("a p c -> (a p) c")).then_inc(landed[i], 16)

        for pair in range(2):
            for part in range(2):
                for e in range(2):
                    load(0, 2 * pair + e, part)
        with sp.Fori(1, self.turns) as it:
            for pair in range(2):
                for part, used in enumerate((self.up_done, self.down_done)):
                    sp.wait_ge(used, it * 2 + pair - 1)
                    for e in range(2):
                        load(it, 2 * pair + e, part)

    def tensor(self, pe):
        b = self.b
        with pe.Fori(0, self.turns) as it:
            for pair in range(2):
                n = it * 2 + pair + 1
                pe.wait_ge(self.gathered[pair], it * 16 + 16)
                for k in range(KT):
                    mm = pe.transpose(b.ps[:, k * P:(k + 1) * P], self.rows[pair][:, k * P:(k + 1) * P], b.ident)
                mm.then_inc(self.rows_turned, 1)
                pe.wait_ge(self.rows_copied, n)
                for e in range(2):
                    pe.wait_ge(self.gu_landed[2 * pair + e], it * 16 + 16)
                for k in range(KT):
                    for e in range(2):
                        r = slice(64 * e, 64 * e + 64)
                        mm = pe.matmul(b.bank(2)[r, :], self.rows_t[:, k, r], self.gu[2 * pair + e][:, k, :], start=k == 0, stop=k == KT - 1)
                mm.then_inc(self.up_done, 1)
                pe.wait_ge(self.hidden_done, n)
                for k in range(2):
                    mm = pe.transpose(b.bank(3)[:, k * P:(k + 1) * P], self.hidden[:, k * P:(k + 1) * P], b.ident)
                mm.then_inc(self.hidden_turned, 1)
                pe.wait_ge(self.hidden_copied, n)
                for e in range(2):
                    pe.wait_ge(self.dn_landed[2 * pair + e], it * 16 + 16)
                for half in range(2):
                    for k in range(2):
                        for e in range(2):
                            r = slice(64 * e, 64 * e + 64)
                            mm = pe.matmul(b.bank(4 + half)[r, :], self.hidden_t[:, k, r], self.dn[2 * pair + e][:, k, half * S:(half + 1) * S],
                                           start=k == 0, stop=k == 1)
                mm.then_inc(self.down_done, 1)

    def scalar(self, act):
        b = self.b
        with act.Fori(0, self.turns) as it:
            for pair in range(2):
                n = it * 2 + pair + 1
                act.wait_ge(self.rows_turned, n)
                act.activation(self.rows_t.rearrange("p k s -> p (k s)"), b.ps[:, 0:D], ACT.Copy).then_inc(self.rows_copied, 1)
                act.wait_ge(self.up_done, n)
                act.activation(self.silu_t, b.bank(2)[:, 0:256], ACT.Silu).then_inc(self.silued, 1)

    def vector(self, dve):
        b = self.b

        def turn(it, pair, first):
            n = it * 2 + pair + 1
            dve.wait_ge(self.silued, n)
            dve.tensor_tensor(self.hidden, b.bank(2)[:, 256:512], self.silu_t, ALU.mult).then_inc(self.hidden_done, 1)
            dve.wait_ge(self.hidden_turned, n)
            dve.tensor_copy(self.hidden_t.rearrange("p k s -> p (k s)"), b.bank(3)[:, 0:256]).then_inc(self.hidden_copied, 1)
            dve.wait_ge(self.down_done, n)
            if not first:
                dve.wait_ge(self.stored[pair], it * 16)
            dve.tensor_copy(self.result[pair], b.ps[:, 2048:3072]).then_inc(self.result_done, 1)

        for pair in range(2):
            turn(0, pair, True)
        with dve.Fori(1, self.turns) as it:
            for pair in range(2):
                turn(it, pair, False)

    def gpsimd(self, pool):
        b = self.b
        numbers = b.small[:, 80:84].bitcast(mybir.dt.uint32)
        for i in range(8):
            pool.indirect_dma_start(b.table_dram, bass.IndirectOffsetOnAxis(ap=b.slot_of[:, i:i + 1], axis=0),
                                    numbers[:, i % 4:i % 4 + 1], None).then_inc(self.placed, 16)
        pool.wait_ge(self.placed, 128)
        pool.dma_start(b.token_of, b.table_dram.rearrange("(c p) o -> p (c o)", p=P), allow_slow_non_contiguous=True).then_inc(self.table_read, 16)
        pool.wait_ge(self.table_read, 16)

        pairs = 2 * self.turns
        for n in range(pairs + 1):
            if n < pairs:
                if n >= 2:
                    pool.wait_ge(self.rows_turned, n - 1)
                    pool.wait_ge(self.gathered[n % 2], 16 * (n // 2))
                pool.indirect_dma_start(self.rows[n % 2], None, b.tokens_dram,
                                        bass.IndirectOffsetOnAxis(ap=b.token_of[:, n:n + 1], axis=0)).then_inc(self.gathered[n % 2], 16)
            if n >= 1:
                pool.wait_ge(self.result_done, n)
                pool.dma_start(self.out_dram[(n - 1) * P:n * P, :], self.result[(n - 1) % 2]).then_inc(self.stored[(n - 1) % 2], 16)
        for pair in range(2):
            pool.wait_ge(self.stored[pair], 16 * self.turns)
        for i in range(8):
            pool.indirect_dma_start(b.big[:, i * D:(i + 1) * D], None, self.out_dram,
                                    bass.IndirectOffsetOnAxis(ap=b.slot_of[:, i:i + 1], axis=0)).then_inc(self.shares_landed, 16)
        pool.wait_ge(self.shares_landed, 128)


def build(nc, tables):
    t = {}
    for name, a in tables.items():
        t[name[3:]] = nc.dram_tensor(name, a.shape, F32, kind="ExternalInput").ap()
    out = nc.dram_tensor("out", [S, D], F32, kind="ExternalOutput").ap()
    b = Builder(nc, t, out)
    b.start()
    b.modulation()
    for l in range(DEPTH):
        b.layer(l)
    b.second()


def kernel(**inputs):
    import concourse.bacc as bacc
    from concourse.bass_utils import run_bass_kernel_spmd

    tables = lay_out(inputs)
    nc = bacc.Bacc("TRN2", target_bir_lowering=False, num_devices=1)
    build(nc, tables)
    r = run_bass_kernel_spmd(nc, [tables], core_ids=[0])
    got = r.results[0]["out"]
    return got.reshape(1, S, D)
```

```python
import contextlib
import math

import numpy as np

import concourse.bass as bass
from concourse import mybir
from concourse.alu_op_type import AluOpType as ALU

F32 = mybir.dt.float32
F32R = mybir.dt.float32r
ACT = mybir.ActivationFunctionType
AX = mybir.AxisListType.X

P = 128
D = 1024
KT = D // P
S = 512
CTX = 256
T = S + CTX
DEPTH = 2
GRID_W = 64
NEG_INF = -1e30
EPS = 1e-6
HEAD = 64
HEADS = 6
WINDOWS = (2, 4, 8, 16)
D_FF = 2816
FT = D_FF // P
STRIP = 2048
RING = 3
MLA_HEADS = 8
MEM_HEADS = 4
EXPERTS = 32
GROUPS = 4
SLOTS = 64
PER_GROUP = EXPERTS // GROUPS
NFFT = 2 * S
MOD_FIRST = 2 * D // 256
MOD_STRIPS = DEPTH * 6 * D // 256

POOL, NAQ, NAK, RQ, RK, GATE, NPX = 0, 2, 5, 8, 11, 14, 17
MQ, MKV, MKR, HY = 0, 2, 3, 4




def strip_plan():
    plan = []
    r = np.arange
    off = np.cumsum([0, 256, 384, 384, 384, 384, 384, 384, 384])
    feature = np.concatenate([r(off[i], off[i + 1]) for i in (0, 1, 2, 4, 5, 7)])
    token = np.concatenate([r(off[3], off[4]), r(off[6], off[7])])
    modulation = [(("w_mod", l), r(D), r(c, c + 256)) for l in range(DEPTH) for c in range(0, 6 * D, 256)]
    plan += modulation[:MOD_FIRST]
    for l in range(DEPTH):
        for c in range(0, NPX * P, 256):
            plan.append((("w_in", l), r(D), feature[c:c + 256]))
        for c in range(0, 768, 256):
            plan.append((("w_in", l), r(D), token[c:c + 256]))
        if l == 0:
            plan += modulation[MOD_FIRST:]
        for c in range(0, D, 256):
            plan.append((("w_out", l), r(D), r(c, c + 256)))
        for m in range(FT):
            plan.append((("w_up", l), r(D), np.concatenate([r(m * P, m * P + P), D_FF + r(m * P, m * P + P)])))
        for c in range(0, D, P):
            for half in range(2):
                plan.append((("w_down", l), r(half * 1408, half * 1408 + 1408), r(c, c + P)))
    plan.append((("w_in_2", 0), r(D), r(0, 256)))
    plan.append((("w_in_2", 0), r(D), r(256, 416)))
    for c in range(0, 1536, 256):
        plan.append((("w_in_2", 0), r(D), 416 + r(c, c + 256)))
    plan.append((("w_uq_2", 0), r(256), r(768)))
    nope = np.concatenate([h * 128 + r(64) for h in range(MLA_HEADS)])
    plan.append((("w_ukv_2", 0), r(128), np.concatenate([nope, nope + 64])))
    for name, cols in (("w_out_2", D), ("w_mkv_2", 2 * D), ("w_mq_2", D), ("w_mo_2", D)):
        for c in range(0, cols, 256):
            plan.append(((name, 0), r(D), r(c, c + 256)))
    return plan


PLAN = strip_plan()
STRIPS = len(PLAN)
WIDTH = [len(rows) // P * len(cols) for _, rows, cols in PLAN]


def pack_strip(matrix, rows, cols):
    a = matrix[rows][:, cols]
    a = a.reshape(len(rows) // P, P, len(cols)).transpose(1, 0, 2).reshape(P, -1)
    return a


class Columns:

    def __init__(self):
        self.at, self.n = {}, 0

    def add(self, name, count):
        self.at[name] = self.n
        self.n += count

    def __getitem__(self, name):
        return self.at[name]


VEC = Columns()
for _l in range(DEPTH):
    for _name, _count in (("b_mod", 48), ("norm1_g", KT), ("norm2_g", KT), ("conv_w", 6 * FT), ("conv_b", 2 * FT),
                          ("pool_scale", 2), ("ret_gn_g", 3), ("decay_f", HEADS), ("decay_b", HEADS), ("pool_w", 128)):
        VEC.add((_name, _l), _count)
for _name, _count in (("c", 2 * KT), ("final_g", KT), ("mix_g", KT), ("q_g", 2), ("kv_g", 1), ("hy_cw", 36),
                      ("hy_cb", 12), ("attn_g", 4), ("hyout_g", 4), ("cross_g", KT), ("mem_g", KT), ("ffn_g", KT),
                      ("last_g", KT), ("hy_f", 4), ("w1", 64), ("w2", 64), ("route_b", 4 * 36)):
    VEC.add(_name, _count)


def tiles_of(v):
    return np.reshape(v, (-1, P)).T


def pack_vectors(x):
    out = np.zeros((P, VEC.n), np.float32)

    def put(name, a):
        out[:a.shape[0], VEC[name]:VEC[name] + a.shape[1]] = a

    for l in range(DEPTH):
        for name in ("b_mod", "norm1_g", "norm2_g", "conv_b", "pool_scale", "ret_gn_g"):
            put((name, l), tiles_of(x[name][l]))
        put(("conv_w", l), tiles_of(x["conv_w"][l]))
        put(("decay_f", l), np.broadcast_to(x["ret_decay_fwd"][l], (P, HEADS)))
        put(("decay_b", l), np.broadcast_to(x["ret_decay_bwd"][l], (P, HEADS)))
        w = x["pool_w"][l].reshape(2, 2, 64, 64)
        put(("pool_w", l), w.transpose(1, 2, 0, 3).reshape(P, 128))
    put("c", np.stack([tiles_of(x["c"][0]), tiles_of(x["c_ctx"])], axis=2).reshape(P, 2 * KT))
    for name, key in (("final_g", "final_g"), ("mix_g", "mix_norm_g_2"), ("q_g", "q_norm_g_2"),
                      ("kv_g", "kv_norm_g_2"), ("hy_cw", "hy_conv_w_2"), ("hy_cb", "hy_conv_b_2"),
                      ("attn_g", "attn_out_g_2"), ("hyout_g", "hy_out_g_2"), ("cross_g", "cross_norm_g_2"),
                      ("mem_g", "mem_norm_g_2"), ("ffn_g", "ffn_norm_g_2"), ("last_g", "final_norm_g_2")):
        put(name, tiles_of(x[key]))
    put("hy_f", np.stack([x["hy_b1_2"][0], x["hy_b2_2"][0], x["hy_freq_2"][0, 0], x["hy_freq_2"][0, 1]], axis=1))
    put("w1", x["hy_w1_2"][0])
    put("w2", x["hy_w2_2"][0])
    bias = np.concatenate([x["b_route_group_2"][0], x["b_route_expert_2"][0]])
    put("route_b", np.broadcast_to(np.tile(bias, 4), (P, 144)))
    return out


def constants():
    f = np.float64
    p = np.arange(P)[:, None]
    t = np.arange(S)[None, :]
    out = {}
    inv = np.zeros((P, 2, T), f)
    for g, w in enumerate(WINDOWS):
        for a, n in ((0, S), (S, CTX)):
            i = np.arange(n)
            inv[64 * (g % 2):64 * (g % 2) + 64, g // 2, a:a + n] = 1.0 / (np.clip(i - w // 2 + w, 0, n) - np.clip(i - w // 2, 0, n))
    out["pool"] = inv.reshape(P, -1)
    freq = 10000.0 ** (-np.arange(16) / 16.0)
    freq = freq.astype(np.float32)
    pos = np.arange(S)
    ang = np.stack([(pos // GRID_W).astype(np.float32)[None, :] * freq[:, None],
                    (pos % GRID_W).astype(np.float32)[None, :] * freq[:, None]]).astype(np.float32)
    within = np.arange(P) % 64
    axis, i = within // 32, within % 16
    a = ang[axis, i]
    swap = np.zeros((P, P), f)
    for q in range(P):
        first = q % 32 < 16
        swap[q + 16 if first else q - 16, q] = -1.0 if first else 1.0
    out["rope"] = np.concatenate([np.cos(a), np.sin(a), swap], axis=1)
    x = np.arange(896)[None, :] - 384 - p
    y = np.arange(896)[None, :] - 128 - p
    out["ramp"] = np.concatenate([np.maximum(x, 0), np.maximum(-x, 0), (x == 0), 256 + y[:, :640], 512 - y[:, :640]], axis=1)
    ang = (pos.astype(np.float32)[None, :] * freq[:, None]).astype(np.float32)
    ang = ang[np.arange(32) % 16]
    c96 = np.ones((P, S), f)
    s96 = np.zeros((P, S), f)
    c96[64:96], s96[64:96] = np.cos(ang), np.sin(ang)
    swap = np.zeros((P, P), f)
    for q in range(64, 96):
        first = q < 80
        swap[q + 16 if first else q - 16, q] = -1.0 if first else 1.0
    out["rope96"] = np.concatenate([c96, s96, swap], axis=1)
    n, k = np.arange(S)[:, None], np.arange(S)[None, :]
    cos = np.cos(2 * np.pi * (n * k % NFFT) / NFFT)
    sin = np.sin(2 * np.pi * (n * k % NFFT) / NFFT)
    sin[:, 0] = 1.0 - 2.0 * (np.arange(S) % 2)
    def tiled(m):
        return m.reshape(4, P, S).transpose(1, 0, 2).reshape(P, 4 * S)
    out["dft"] = np.concatenate([tiled(cos), tiled(sin), tiled(sin.T)], axis=1)
    tt = np.arange(S).astype(np.float32)
    t01 = tt / np.float32(S)
    bands = np.linspace(1e-4, 15, 16, dtype=np.float32)
    ang = (np.float32(2.0 * math.pi) * tt[:, None] * bands[None, :] / np.float32(S)).astype(np.float32)
    z = np.concatenate([t01[:, None], np.cos(ang), -np.sin(ang)], axis=1).T
    feats = np.zeros((P, 2 * S), f)
    feats[:33, :S] = z
    feats[0, S:] = -t01
    out["hyena"] = feats
    group = np.zeros((P, P))
    group[:64, :64] = group[64:, 64:] = 1.0 / 64
    w = np.full((P, 2), 2.0 / NFFT)
    w[0, 0] = 1.0 / NFFT
    rank = np.broadcast_to(np.arange(8, 0, -1)[None, :], (P, 8))
    earlier = p < np.arange(P)[None, :]
    slot = np.broadcast_to(SLOTS * np.arange(EXPERTS)[None, :], (P, EXPERTS))
    groups = (p % 32 == np.arange(2)[None, :]).astype(f)
    out["base"] = np.concatenate([np.eye(P), np.ones((P, P)), group, w, rank, earlier, slot, p + P * np.arange(4)[None, :], groups], axis=1)
    return {k: np.ascontiguousarray(v.astype(np.float32)) for k, v in out.items()}


BASE_COLS = 4 * P + 48


def pack_bias(rpb):
    qc = np.arange(GRID_W)
    start = np.clip(qc - 8, 0, GRID_W - 16)
    kc = np.arange(GRID_W)
    valid = (kc[None, :] >= start[:, None]) & (kc[None, :] < start[:, None] + 16)
    dc = np.clip(kc[None, :] - qc[:, None] + 15, 0, 30)
    out = np.full((DEPTH, HEADS, 2, GRID_W, 15, GRID_W), NEG_INF, np.float32)
    for a in range(2):
        for s in range(1, 15):
            picked = rpb[:, :, s - a][:, :, dc]
            out[:, :, a, :, s, :] = np.where(valid, picked, np.float32(NEG_INF))
    return out.reshape(DEPTH * HEADS, P, 15 * GRID_W)


def lay_out(x):
    x = {k: np.asarray(v) for k, v in x.items()}
    out = dict(constants())
    stream = np.zeros((STRIPS, P, STRIP), np.float32)
    for i, ((name, l), rows, cols) in enumerate(PLAN):
        stream[i, :, :WIDTH[i]] = pack_strip(x[name][l], rows, cols)
    out["stream"] = stream
    experts = np.empty((EXPERTS, P, 3 * STRIP), np.float32)
    both = np.concatenate([x[name][0].reshape(EXPERTS, KT, P, 256) for name in ("w_gate_2", "w_up_2")], axis=3)
    experts[:, :, :2 * STRIP] = both.transpose(0, 2, 1, 3).reshape(EXPERTS, P, 2 * STRIP)
    experts[:, :, 2 * STRIP:] = x["w_down_2"][0].reshape(EXPERTS, 2, P, D).transpose(0, 2, 1, 3).reshape(EXPERTS, P, STRIP)
    out["experts"] = experts
    out["last_gain"] = np.broadcast_to(x["final_norm_g_2"], (P, D))
    out["vectors"] = pack_vectors(x)
    out["bias"] = pack_bias(x["na_rpb"])
    out["tokens"] = np.concatenate([x["x"][0].T.reshape(KT, P, S), x["ctx"][0].T.reshape(KT, P, CTX)], axis=2).transpose(1, 0, 2)
    out["memory"] = x["mem_2"][0].T.reshape(KT, P, 256).transpose(1, 0, 2)
    route = np.concatenate([x["w_route_group_2"][0], x["w_route_expert_2"][0]], axis=1)
    out["route"] = route.reshape(KT, P, 36).transpose(1, 0, 2)
    out["filter"] = np.concatenate([x["hy_w3_2"][0], x["hy_b3_2"]], axis=0)
    out["decay"] = x["hy_decay_2"]
    out["skip"] = np.broadcast_to(x["hy_skip_2"].reshape(1, 2 * S), (P, 2 * S))
    return {"in_" + k: np.ascontiguousarray(v) for k, v in out.items()}




class Signal:

    def __init__(self, nc, name):
        self.sem = nc.alloc_semaphore(name)
        self.base = self.n = 0

    def up(self, by=1):
        self.n += by
        return self.sem

    def at(self, k):
        return self.base + k

    def now(self):
        return self.base + self.n

    def close(self):
        self.base += self.n
        self.n = 0


def settle(engine, instruction, signal):
    instruction.then_inc(signal.up(), 1)
    engine.wait_ge(signal.sem, signal.now())


class Unit:

    def __init__(self, need, weight, tiles, partitions, width, rows=None):
        self.need, self.weight, self.tiles, self.rows = need, weight, tiles, rows
        self.partitions, self.width = partitions, width


def tiles_in(width, *areas):
    return [a[:, i * width:(i + 1) * width] for a in areas for i in range(a.shape[1] // width)]


def pieces(width):
    return [(a, min(a + 512, width)) for a in range(0, width, 512)]


def halves(m):
    o = (m % 2) * P
    return lambda w, j: w[0].rearrange("p (k c) -> p k c", k=KT)[:, j, o:o + P]


class ModulationProducts:

    def __init__(self, b, first, count, bank, partial):
        self.b, self.first, self.count, self.partial = b, first, count, partial
        self.partial_ps, self.sums_ps = bank[:, 0:256], bank[:, 256:512]
        self.copied, self.summed = b.sig("partial_copied"), b.sig("partial_summed")
        self.ends = []

    def products(self, pe, n):
        b = self.b
        strip = b.strip(pe, len(b.freed_at))
        if n >= 1:
            self.sum(pe, n - 1)
        for half in range(2):
            for g in range(4):
                k = 2 * g + half
                mm = pe.matmul(self.partial_ps[32 * g:32 * g + 32, :], b.cond[:, k, :], strip[:, k * 256:(k + 1) * 256],
                               start=half == 0, stop=half == 1)
        mm.then_inc(b.done.up(), 1)
        b.strips_freed(1)
        self.ends.append(b.done.now())

    def copy(self, act, n):
        act.wait_ge(self.b.done.sem, self.ends[n])
        if n >= 2:
            act.wait_ge(self.summed.sem, self.summed.at(n - 1))
        act.activation(self.partial[n % 2], self.partial_ps, ACT.Copy).then_inc(self.copied.up(), 1)

    def sum(self, pe, n):
        pe.wait_ge(self.copied.sem, self.copied.at(n + 1))
        for t in range(2):
            c = 2 * (2 * n + t)
            mm = pe.matmul(self.sums_ps[:, c:c + 2], self.partial[n % 2][:, t * P:(t + 1) * P], self.b.sum_groups, start=True, stop=True)
        mm.then_inc(self.summed.up(), 1)

    def finish(self, dve):
        b, vstep = self.b, self.b.sig("vector_step")
        dve.wait_ge(self.summed.sem, self.summed.at(self.count))
        ps = self.sums_ps[:, 0:4 * self.count].rearrange("p (m s) -> p m s", s=2)
        for l in range(DEPTH):
            a = max(2 * self.first, l * 48)
            z = min(2 * (self.first + self.count), (l + 1) * 48)
            for s in range(2):
                if a < z:
                    settle(dve, dve.tensor_tensor(b.mods[:, l, s, a - l * 48:z - l * 48], ps[:, a - 2 * self.first:z - 2 * self.first, s],
                                                  b.v(("b_mod", l), a - l * 48, z - a), ALU.add), vstep)
                for which, name, m in ((0, "norm1_g", 1), (1, "norm2_g", 4)):
                    if a <= l * 48 + m * KT < z:
                        dve.scalar_tensor_tensor(out=b.gains[:, l, s, which, :], in0=b.mods[:, l, s, m * KT:(m + 1) * KT],
                                                 scalar=1.0, in1=b.v((name, l), 0, KT), op0=ALU.add, op1=ALU.mult)


class Builder:
    def __init__(self, nc, t, out):
        self.nc, self.t, self.out = nc, t, out
        self.signals = {}
        self.twins = {}

        def alloc(name, cols, twin=False):
            at = (nc.sbuf_base + 31) // 32 * 32
            area = nc.alloc_sbuf_tensor(name, [P, cols], F32)[:, :]
            if twin:
                assert nc.sbuf_base == at + 4 * cols
                self.twins[name] = nc.alloc_sbuf_tensor_at(name + "_rounded", [P, cols], F32R, offset=at)[:, :]
            return area

        self.h = alloc("h", KT * T).rearrange("p (k t) -> p k t", k=KT)
        self.xn = alloc("xn", KT * T, twin=True)
        self.big = alloc("big", 17664, twin=True)
        self.ring = alloc("ring", (RING + 2) * STRIP, twin=True)
        self.high = [self.ring[:, (RING + i) * STRIP:(RING + i + 1) * STRIP] for i in range(2)]
        self.vec = alloc("vec", VEC.n)
        self.base = alloc("base", BASE_COLS)
        self.mods = alloc("mods", DEPTH * 2 * 48).rearrange("p (l s m) -> p l s m", l=DEPTH, s=2)
        self.gains = alloc("gains", DEPTH * 2 * 2 * KT).rearrange("p (l s n k) -> p l s n k", l=DEPTH, s=2, n=2)
        self.small = alloc("small", 128)
        self.work = alloc("work", 10888, twin=True)
        self.ps = nc.alloc_psum_tensor("ps", [P, 4096], F32)[:, :]
        self.ident = self.base[:, 0:P]
        self.ones = self.base[:, P:2 * P]
        self.group = self.base[:, 2 * P:3 * P]
        self.freq_w = self.base[:, 3 * P:3 * P + 2]
        self.rank = self.base[:, 3 * P + 2:3 * P + 10]
        self.earlier = self.base[:, 3 * P + 10:4 * P + 10]
        self.first_slot = self.base[:, 4 * P + 10:4 * P + 42]
        self.token_number = self.base[:, 4 * P + 42:4 * P + 46]
        self.sum_groups = self.base[:, 4 * P + 46:4 * P + 48]
        self.cond = self.work[:, 10632:10888].rearrange("p (k s) -> p k s", k=KT)
        self.x = self.h[:, :, 0:S]
        self.issued = 0
        self.ahead = 0
        self.freed_at = []
        self.landed = [nc.alloc_semaphore(f"strip_landed_{i}") for i in range(RING)]
        self.done = self.sig("product_done")

    def sig(self, name):
        if name not in self.signals:
            self.signals[name] = Signal(self.nc, name)
        return self.signals[name]

    @contextlib.contextmanager
    def stage(self):
        with self.nc.Block(no_gpsimd_drain=True) as block:
            yield block
        for s in self.signals.values():
            s.close()

    def v(self, name, i=0, n=1):
        a = VEC[name] + i
        return self.vec[:, a:a + n]

    def bank(self, b, width=512, rows=P, first=0):
        return self.ps[first:first + rows, b * 512:b * 512 + width]


    def load_strips(self, sp):
        until = min(len(self.freed_at) + RING, STRIPS)
        for i in range(self.issued, until):
            if i >= RING:
                sp.wait_ge(self.done.sem, self.freed_at[i - RING])
            slot = i % RING
            sp.dma_start(self.ring[:, slot * STRIP:slot * STRIP + WIDTH[i]],
                         self.t["stream"][i, :, 0:WIDTH[i]]).then_inc(self.landed[slot], 16)
        self.issued = until

    def strip(self, pe, i):
        pe.wait_ge(self.landed[i % RING], 16 * (i // RING + 1))
        a = (i % RING) * STRIP
        return self.ring[:, a:a + WIDTH[i]]


    def rounded(self, area):
        return self.twins[area.tensor.name][:, area.offset:area.offset + area.shape[1]]

    def split_high(self, act, value, high):
        return act.activation(self.rounded(high), value, ACT.Copy)

    def split_ahead(self, halves):
        i, tiled = len(self.freed_at), lambda a: a.rearrange("p (k c) -> p k c", k=KT)
        views = []
        for j in range(2):
            n = i if halves else i + j
            value = self.ring[:, n % RING * STRIP:n % RING * STRIP + WIDTH[n]]
            low = self.rounded(value)
            if halves:
                value, low = (tiled(a)[:, :, j * P:(j + 1) * P] for a in (value, low))
                high = tiled(self.rounded(self.high[0][:, j * 1024:(j + 1) * 1024]))
            else:
                high = self.rounded(self.high[n % 2][:, 0:WIDTH[n]])
            views.append((n, value, low, high))
        self.ahead = 2
        return views

    def split_low(self, dve, value, high):
        return dve.tensor_tensor(self.rounded(value), value, self.rounded(high).bitcast(F32), ALU.subtract)

    def strips_freed(self, count):
        self.freed_at += [self.done.now()] * count


    def load(self, items):
        landed = self.sig("inputs_landed")
        with self.stage() as block:
            @block.scalar
            def _(act):
                for dst, src in items:
                    act.dma_start(dst, src).then_inc(landed.up(16), 16)
                act.wait_ge(landed.sem, landed.now())

    def norm(self, dst, src, kt, width, segments, tmp, load=(), ahead=None):
        strip_high, strip_low = self.sig("strip_high"), self.sig("strip_low")
        views = self.split_ahead(ahead == "halves") if ahead else []
        squared, summed, rooted = self.sig("squared"), self.sig("summed"), self.sig("rooted")
        scaled, shifted, vstep = self.sig("scaled"), self.sig("shifted"), self.sig("vector_step")
        landed = self.sig("inputs_landed")
        pair = min(kt, 2)
        sq = [tmp[:, i * width:(i + 1) * width] for i in range(4)]
        rstd = tmp[:, 4 * width:5 * width]
        mean = self.ps[:, 0:width]
        paired = self.sig("squares_paired")
        with self.stage() as block:
            @block.scalar
            def _(act):
                for a, b in load:
                    act.dma_start(a, b).then_inc(landed.up(16), 16)
                act.activation(self.small[:, 124:125], self.ones[:, 0:1], ACT.Sqrt)
                for k in range(kt):
                    if k >= 4:
                        act.wait_ge(summed.sem, summed.at(k // 2 - 1))
                    act.activation(sq[k % 4], src(k), ACT.Square).then_inc(squared.up(), 1)
                    if k == min(3, kt - 1):
                        for n, value, low, high in views:
                            self.strip(act, n)
                            act.activation(high, value, ACT.Copy).then_inc(strip_high.up(), 1)
                act.wait_ge(summed.sem, summed.at(kt // pair))
                act.activation(rstd, mean, ACT.Sqrt, scale=1.0 / (kt * P), bias=EPS).then_inc(rooted.up(), 1)
                done = 0
                for k in range(kt):
                    for a, b, gain, shift in segments:
                        done += 1
                        if shift is not None:
                            act.wait_ge(scaled.sem, scaled.at(done))
                            act.activation(dst(k)[:, a:b], dst(k)[:, a:b], ACT.Identity, bias=shift(k)).then_inc(shifted.up(), 1)
                if load:
                    act.wait_ge(landed.sem, landed.now())

            @block.tensor
            def _(pe):
                for j in range(kt // pair):
                    before = paired if pair == 2 else squared
                    pe.wait_ge(before.sem, before.at(j + 1))
                    for a, b in pieces(width):
                        mm = pe.matmul(mean[:, a:b], self.ones, sq[2 * j % 4][:, a:b], start=j == 0, stop=j == kt // pair - 1)
                    mm.then_inc(summed.up(), 1)

            @block.vector
            def _(dve):
                if pair == 2:
                    for j in range(kt // 2):
                        dve.wait_ge(squared.sem, squared.at(2 * j + 2))
                        x = sq[2 * j % 4]
                        dve.tensor_tensor(x, x, sq[2 * j % 4 + 1], ALU.add).then_inc(paired.up(), 1)
                for j, (n, value, low, high) in enumerate(views):
                    dve.wait_ge(strip_high.sem, strip_high.at(j + 1))
                    dve.tensor_tensor(low, value, high.bitcast(F32), ALU.subtract).then_inc(strip_low.up(), 1)
                dve.wait_ge(rooted.sem, rooted.at(1))
                settle(dve, dve.reciprocal(rstd, rstd), vstep)
                for k in range(kt):
                    for a, b, gain, shift in segments:
                        dve.scalar_tensor_tensor(out=dst(k)[:, a:b], in0=src(k)[:, a:b], scalar=gain(k), in1=rstd[:, a:b],
                                                 op0=ALU.mult, op1=ALU.mult).then_inc(scaled.up(), 1)

    def project(self, units, strips, finish, sources, banks_each=1):
        first = len(self.freed_at)
        done, taken = self.done, self.sig("taken_by_vector")
        tile_high, tile_low = self.sig("tile_high"), self.sig("tile_low")
        strip_high, strip_low = self.sig("strip_high"), self.sig("strip_low")
        slots = 8 // banks_each
        ahead, self.ahead = self.ahead, 0
        last_unit = {s: i for i, u in enumerate(units) for s in u.need}
        ends = []

        def place(i):
            a = (i % slots) * banks_each * 512
            return self.ps[0:units[i].partitions, a:a + units[i].width]

        def parts(strips_of_unit):
            slot = [self.ring[:, (first + s) % RING * STRIP:(first + s) % RING * STRIP + WIDTH[first + s]] for s in strips_of_unit]
            low_w = [self.rounded(a) for a in slot]
            high_w = [self.rounded(self.high[(first + s) % 2][:, 0:WIDTH[first + s]]) for s in strips_of_unit]
            low_x, high_x = ([self.rounded(t[part]) for t in sources] for part in (0, 1))
            return [(high_w, low_x), (high_w, high_x), (low_w, high_x)]

        def split_order(split_strip, split_tile, take):
            if not ahead:
                split_strip(0)
            for k in range(len(sources)):
                split_tile(k)
            following = max(1, ahead)
            for i in range(len(units)):
                while following < strips and (following < 2 or self.freed_at[first + following - 2] < ends[i]):
                    split_strip(following)
                    following += 1
                take(i)

        with self.stage() as block:
            @block.tensor
            def _(pe):
                seen_strips, seen_tiles = 0, 0
                for i, u in enumerate(units):
                    if i >= slots:
                        pe.wait_ge(taken.sem, taken.at(i - slots + 1))
                    out, terms = place(i), len(u.tiles)
                    passes = parts(u.need)
                    for j, tile in enumerate(u.tiles):
                        mine = j * len(u.need) // terms
                        if u.need[mine] >= seen_strips:
                            seen_strips += 1
                            if seen_strips > ahead:
                                pe.wait_ge(strip_low.sem, strip_low.at(seen_strips - ahead))
                        if tile >= seen_tiles:
                            seen_tiles = tile + 1
                            pe.wait_ge(tile_low.sem, tile_low.at(seen_tiles))
                        for n, (w, x) in enumerate(passes):
                            weight = u.weight(w, j)
                            for a, b in pieces(u.width):
                                lhs, rhs = (weight, x[tile][:, a:b]) if u.rows is None else (x[tile][:, u.rows], weight)
                                mm = pe.matmul(out[:, a:b], lhs, rhs, start=j == 0 and n == 0, stop=j == terms - 1 and n == len(passes) - 1)
                        if j == terms - 1 or (j + 1) * len(u.need) // terms != mine:
                            mm.then_inc(done.up(), 1)
                            if last_unit[u.need[mine]] == i:
                                self.strips_freed(1)
                    ends.append(done.now())

            @block.sync
            def _(sp):
                self.load_strips(sp)

            @block.vector
            def _(dve):
                def take(i):
                    dve.wait_ge(done.sem, ends[i])
                    finish(dve, i, place(i)).then_inc(taken.up(), 1)

                def split_strip(s):
                    n, i = WIDTH[first + s], first + s
                    dve.wait_ge(strip_high.sem, strip_high.at(s + 1 - ahead))
                    self.split_low(dve, self.ring[:, i % RING * STRIP:i % RING * STRIP + n], self.high[i % 2][:, 0:n]).then_inc(strip_low.up(), 1)

                def split_tile(k):
                    dve.wait_ge(tile_high.sem, tile_high.at(k + 1))
                    self.split_low(dve, *sources[k]).then_inc(tile_low.up(), 1)

                split_order(split_strip, split_tile, take)

            @block.scalar
            def _(act):
                def split_strip(s):
                    if s >= 2:
                        act.wait_ge(done.sem, self.freed_at[first + s - 2])
                    self.split_high(act, self.strip(act, first + s), self.high[(first + s) % 2][:, 0:WIDTH[first + s]]).then_inc(strip_high.up(), 1)

                def split_tile(k):
                    self.split_high(act, *sources[k]).then_inc(tile_high.up(), 1)

                split_order(split_strip, split_tile, lambda i: None)

    def attention(self, heads, nq, width, depth, q, k, bias, v, outs, scale, tmp, modulation=None):
        nk = width // P
        scored, tk = self.sig("scored"), self.sig("max_taken")
        exped, normed, turned = self.sig("exponentials"), self.sig("normalised"), self.sig("turned")
        copied, valued, stored = self.sig("turned_copied"), self.sig("valued"), self.sig("stored")
        vstep, bias_in = self.sig("vector_step"), self.sig("bias_landed")
        n_out = len(outs(0))
        pbuf = [tmp[:, i * width:(i + 1) * width] for i in range(3)]
        at = 3 * width
        pt = [tmp[:, at + i * nk * nq * P:at + (i + 1) * nk * nq * P].rearrange("p (k q) -> p k q", k=nk) for i in range(2)]
        at += 2 * nk * nq * P
        gt = [tmp[:, at + i * 960:at + (i + 1) * 960] for i in range(2)]
        stat = self.small[:, 0:16].rearrange("p (a b) -> p a b", a=4)
        units = heads * nq
        score_buffers, room = (2, 1024) if width > 512 else (4, 512)
        spsum = [self.ps[:, i * room:i * room + width] for i in range(score_buffers)]
        tpsum = self.ps[:, 2048:2048 + width]
        opsum = [self.bank(6 + i) for i in range(1 if modulation else 2)]
        share = [range(u * modulation.count // units, (u + 1) * modulation.count // units) if modulation else () for u in range(units)]
        with self.stage() as block:
            @block.tensor
            def _(pe):
                def scores(u):
                    h, i = divmod(u, nq)
                    if u >= score_buffers:
                        before = tk if bias else exped
                        pe.wait_ge(before.sem, before.at(u - score_buffers + 1))
                    for d in range(depth):
                        for a, b, keys in k(h)[d]:
                            mm = pe.matmul(spsum[u % score_buffers][:, a:b], q(h, i)[d], keys, start=d == 0, stop=d == depth - 1)
                    mm.then_inc(scored.up(), 1)

                def values(h):
                    pe.wait_ge(copied.sem, copied.at((h + 1) * nq))
                    for n in range(n_out):
                        m = h * n_out + n
                        if m >= len(opsum):
                            pe.wait_ge(stored.sem, stored.at(m - len(opsum) + 1))
                        dst = outs(h)[n]
                        r0, rows = dst.base_partition(), dst.shape[0]
                        for j in range(nk):
                            mm = pe.matmul(opsum[m % len(opsum)][r0:r0 + rows, 0:nq * P], v(h, j, n), pt[h % 2][:, j, :],
                                           start=j == 0, stop=j == nk - 1)
                        mm.then_inc(valued.up(), 1)

                scores(0)
                scores(1)
                for u in range(units):
                    if u + 2 < units:
                        scores(u + 2)
                    for n in share[u][0:1]:
                        modulation.products(pe, n)
                    pe.wait_ge(normed.sem, normed.at(u + 1))
                    if u >= 1:
                        pe.wait_ge(copied.sem, copied.at(u))
                    for j in range(nk):
                        mm = pe.transpose(tpsum[:, j * P:(j + 1) * P], pbuf[u % 3][:, j * P:(j + 1) * P], self.ident)
                    mm.then_inc(turned.up(), 1)
                    if u % nq == 0 and u >= nq:
                        values(u // nq - 1)
                    for n in share[u][1:2]:
                        modulation.products(pe, n)
                if modulation:
                    modulation.sum(pe, modulation.count - 1)
                values(heads - 1)

            if bias:
                @block.gpsimd
                def _(pool):
                    for h in range(heads):
                        if h >= 2:
                            pool.wait_ge(tk.sem, tk.at((h - 1) * nq))
                        pool.dma_start(gt[h % 2], bias(h)).then_inc(bias_in.up(16), 16)
                        pool.wait_ge(bias_in.sem, bias_in.now())

            @block.sync
            def _(sp):
                self.load_strips(sp)

            @block.vector
            def _(dve):
                def top(u):
                    h, i = divmod(u, nq)
                    b = u % 4
                    dve.wait_ge(scored.sem, scored.at(u + 1))
                    src, s = spsum[u % score_buffers], scale
                    if bias:
                        if i == 0:
                            dve.wait_ge(bias_in.sem, bias_in.at(16 * (h + 1)))
                        if u >= 3:
                            dve.wait_ge(turned.sem, turned.at(u - 2))
                        a = (7 - 2 * i) * GRID_W
                        dve.tensor_scalar(pbuf[u % 3][:, 512:width], src[:, 512:width], scale, None, ALU.mult)
                        settle(dve, dve.scalar_tensor_tensor(out=pbuf[u % 3][:, 0:512], in0=src[:, 0:512], scalar=scale,
                                                             in1=gt[h % 2][:, a:a + 512], op0=ALU.mult, op1=ALU.add), vstep)
                        src, s = pbuf[u % 3], 1.0
                    settle(dve, dve.reduce_max(stat[:, 0, b:b + 1], src, AX), vstep)
                    dve.tensor_scalar(stat[:, 1, b:b + 1], stat[:, 0, b:b + 1], -s, None, ALU.mult).then_inc(tk.up(), 1)

                def normalise(u):
                    b = u % 4
                    dve.wait_ge(exped.sem, exped.at(u + 1))
                    settle(dve, dve.reciprocal(stat[:, 3, b:b + 1], stat[:, 2, b:b + 1]), vstep)
                    dve.tensor_scalar(pbuf[u % 3], pbuf[u % 3], stat[:, 3, b:b + 1], None, ALU.mult).then_inc(normed.up(), 1)

                def store(h):
                    for n in range(n_out):
                        m = h * n_out + n
                        dve.wait_ge(valued.sem, valued.at(m + 1))
                        dst = outs(h)[n]
                        r0, rows = dst.base_partition(), dst.shape[0]
                        dve.tensor_copy(dst, opsum[m % len(opsum)][r0:r0 + rows, 0:nq * P]).then_inc(stored.up(), 1)

                top(0)
                top(1)
                for u in range(units):
                    normalise(u)
                    if u + 2 < units:
                        top(u + 2)
                    if u % nq == min(1, nq - 1) and u >= nq:
                        store(u // nq - 1)
                store(heads - 1)
                if modulation:
                    modulation.finish(dve)

            @block.scalar
            def _(act):
                def exponentials(u):
                    b = u % 4
                    act.wait_ge(tk.sem, tk.at(u + 1))
                    if not bias and u >= 3:
                        act.wait_ge(turned.sem, turned.at(u - 2))
                    src, s = (pbuf[u % 3], 1.0) if bias else (spsum[u % score_buffers], scale)
                    act.activation(pbuf[u % 3], src, ACT.Exp, bias=stat[:, 1, b:b + 1], scale=s,
                                   accum_out=stat[:, 2, b:b + 1]).then_inc(exped.up(), 1)

                exponentials(0)
                exponentials(1)
                for u in range(units):
                    for n in share[u][0:1]:
                        modulation.copy(act, n)
                    self._turn_copy(act, u, nq, nk, turned, copied, valued, n_out, pt, tpsum)
                    if u + 2 < units:
                        exponentials(u + 2)
                    for n in share[u][1:2]:
                        modulation.copy(act, n)

    def _turn_copy(self, act, u, nq, nk, turned, copied, valued, n_out, pt, tpsum):
        h, i = divmod(u, nq)
        if i == 0 and h >= 2:
            act.wait_ge(valued.sem, valued.at((h - 1) * n_out))
        act.wait_ge(turned.sem, turned.at(u + 1))
        act.activation(pt[h % 2][:, :, i * P:(i + 1) * P], tpsum.rearrange("p (k q) -> p k q", k=nk), ACT.Copy).then_inc(copied.up(), 1)


    def start(self):
        landed, done = self.sig("inputs_landed"), self.sig("conditioned")
        zeroed = self.sig("zeroed")
        with self.stage() as block:
            @block.sync
            def _(sp):
                self.load_strips(sp)

            @block.scalar
            def _(act):
                for dst, src in ((self.vec, self.t["vectors"]), (self.base, self.t["base"])):
                    act.dma_start(dst, src).then_inc(landed.up(16), 16)
                act.dma_start(self.h, self.t["tokens"]).then_inc(self.sig("tokens_landed").up(16), 16)
                act.wait_ge(landed.sem, landed.now())
                act.wait_ge(zeroed.sem, zeroed.at(1))
                act.activation(self.cond[:, :, 0:2], self.v("c", 0, 16).rearrange("p (k s) -> p k s", s=2), ACT.Silu).then_inc(done.up(), 1)
                act.wait_ge(done.sem, done.now())

            @block.vector
            def _(dve):
                dve.memset(self.cond, 0.0).then_inc(zeroed.up(), 1)

    def modulation(self):
        work = ModulationProducts(self, 0, MOD_FIRST, self.bank(0), tiles_in(256, self.work[:, 0:512]))
        with self.stage() as block:
            @block.tensor
            def _(pe):
                for n in range(MOD_FIRST):
                    work.products(pe, n)
                work.sum(pe, MOD_FIRST - 1)

            @block.sync
            def _(sp):
                self.load_strips(sp)

            @block.scalar
            def _(act):
                for n in range(MOD_FIRST):
                    work.copy(act, n)
                act.wait_ge(self.sig("tokens_landed").sem, 16)

            @block.vector
            def _(dve):
                work.finish(dve)

    def segments(self, l, which, need_ctx=True):
        shift = 0 if which == 0 else 3
        def seg(a, b, s):
            return (a, b, lambda k: self.gains[:, l, s, which, k:k + 1],
                    lambda k: self.mods[:, l, s, shift * KT + k:shift * KT + k + 1])
        return [seg(0, S, 0)] + ([seg(S, T, 1)] if need_ctx else [])

    def input_projection(self, l, need_ctx):
        xn = self.xn.rearrange("p (k t) -> p k t", k=KT)
        px = self.big[:, 0:NPX * T].rearrange("p (n t) -> p n t", n=NPX)
        pv = self.big[:, NPX * T:NPX * T + 6 * 768].rearrange("p (n c) -> p n c", n=6)
        self.px, self.pv = px, pv
        units, dst = [], []
        for m in range(NPX):
            width = T if need_ctx or NAK <= m < RQ or RK <= m < GATE else S
            units.append(Unit([m // 2], halves(m), range(KT), P, width))
            dst.append(px[:, m, 0:width])
        for c in range(3):
            for n in range(6):
                units.append(Unit([9 + c], lambda w, j: w[0].rearrange("p (k c) -> p k c", k=KT)[:, j, :], range(KT), P, 256,
                                  slice(n * P, (n + 1) * P)))
                dst.append(pv[:, n, c * 256:(c + 1) * 256])
        def finish(eng, i, ps):
            if eng is self.nc.scalar:
                return eng.activation(dst[i], ps, ACT.Copy)
            return eng.tensor_copy(dst[i], ps)

        self.project(units, 12, finish, banks_each=2, sources=[(xn[:, k, :], self.work[:, k * T:(k + 1) * T]) for k in range(KT)])

    def pooling(self, l, need_ctx):
        px, y = self.px, self.xn.rearrange("p (k t) -> p k t", k=KT)
        w = self.work
        inv = w[:, 0:2 * T].rearrange("p (n t) -> p n t", n=2)
        lead, gap = 8, 16
        self.rope_table, table_landed = self.xn[:, 5 * T:5 * T + 1152], self.sig("table_landed")
        width = lead + S + gap + CTX + lead
        buf = [[w[:, 2 * T + (5 * n + j) * width:2 * T + (5 * n + j + 1) * width] for j in range(5)] for n in range(2)]
        runs = [(0, S, lead), (S, T, lead + S + gap)] if need_ctx else [(0, S, lead)]
        landed, vstep, ready = self.sig("inputs_landed"), self.sig("vector_step"), self.sig("pooled")
        done = self.sig("product_done")
        with self.stage() as block:
            @block.sync
            def _(sp):
                sp.dma_start(inv, self.t["pool"].rearrange("p (n t) -> p n t", n=2)).then_inc(landed.up(16), 16)
                sp.dma_start(self.rope_table, self.t["rope"]).then_inc(table_landed.up(16), 16)
                sp.wait_ge(table_landed.sem, table_landed.now())

            @block.vector
            def _(dve):
                dve.wait_ge(landed.sem, landed.at(16))
                for n in range(2):
                    settle(dve, dve.memset(buf[n][0], 0.0), vstep)
                    for a, b, o in runs:
                        settle(dve, dve.tensor_copy(buf[n][0][:, o:o + b - a], px[:, n, a:b]), vstep)
                    lo, hi = 1, width
                    settle(dve, dve.tensor_tensor(buf[n][1][:, 1:width], buf[n][0][:, 0:width - 1], buf[n][0][:, 1:width], ALU.add), vstep)
                    for level in range(2 + 2 * n):
                        dst = buf[n][(level + 1) % 4]
                        if level > 0:
                            src, half = buf[n][level % 4], 2 ** (level - 1)
                            settle(dve, dve.tensor_tensor(dst[:, lo + half:hi - half], src[:, lo:hi - 2 * half],
                                                          src[:, lo + 2 * half:hi], ALU.add), vstep)
                            lo, hi = lo + half, hi - half
                        group = level - 2 * n
                        if group >= 0:
                            r = slice(64 * group, 64 * group + 64)
                            for a, b, o in runs:
                                settle(dve, dve.tensor_tensor(buf[n][4][r, a:b], dst[r, o:o + b - a], inv[r, n, a:b], ALU.mult), vstep)
                    for a, b, o in runs:
                        dve.tensor_tensor(buf[n][4][:, a:b], buf[n][4][:, a:b], px[:, n, a:b], ALU.subtract).then_inc(ready.up(), 1)
                for n in range(2):
                    dve.wait_ge(done.sem, done.at(n + 1))
                    for a, b, o in runs:
                        dve.tensor_scalar(y[:, n, a:b], self.ps[:, n * 1024 + a:n * 1024 + b], self.v(("pool_scale", l), n), None, ALU.mult)

            @block.tensor
            def _(pe):
                for n in range(2):
                    pe.wait_ge(ready.sem, ready.at(len(runs) * (n + 1)))
                    for half in range(2):
                        r = slice(64 * half, 64 * half + 64)
                        for a, b, o in runs:
                            mm = pe.matmul(self.ps[r, n * 1024 + a:n * 1024 + b], self.v(("pool_w", l), 64 * n, 64)[r, :],
                                           buf[n][4][r, a:b], start=True, stop=True)
                    mm.then_inc(done.up(), 1)

    def rotate(self):
        px = self.px
        tmp = [self.work[:, i * S:(i + 1) * S] for i in range(2)]
        tiles = [RQ, RQ + 1, RQ + 2, RK, RK + 1, RK + 2]
        self._rotate([px[:, m, 0:S] for m in tiles], P, self.rope_table, tmp)

    def _rotate(self, tiles, rows, table, tmp):
        r = slice(0, rows)
        cos, sin, swap = table[:, 0:S], table[:, S:2 * S], table[:, 2 * S:2 * S + P]
        vstep, done, turned = self.sig("vector_step"), self.sig("product_done"), self.sig("rotated")
        with self.stage() as block:
            @block.tensor
            def _(pe):
                for i, t in enumerate(tiles):
                    if i >= 8:
                        pe.wait_ge(turned.sem, turned.at(i - 7))
                    pe.matmul(self.ps[r, i % 8 * 512:i % 8 * 512 + S], swap[r, r], t, start=True, stop=True).then_inc(done.up(), 1)

            @block.vector
            def _(dve):
                for i, t in enumerate(tiles):
                    dve.wait_ge(done.sem, done.at(i + 1))
                    dve.tensor_tensor(tmp[i % 2][r, :], self.ps[r, i % 8 * 512:i % 8 * 512 + S], sin[r, :], ALU.mult).then_inc(turned.up(), 1)
                    settle(dve, dve.tensor_tensor(t, t, cos[r, :], ALU.mult), vstep)
                    settle(dve, dve.tensor_tensor(t, t, tmp[i % 2][r, :], ALU.add), vstep)

    def neighbourhood(self, l):
        px, pv, y = self.px, self.pv, self.xn.rearrange("p (k t) -> p k t", k=KT)
        def rows(h):
            return slice(64 * (h % 2), 64 * (h % 2) + 64)
        modulation = None
        if l == 0:
            modulation = ModulationProducts(self, MOD_FIRST, MOD_STRIPS - MOD_FIRST, self.bank(7), tiles_in(256, self.xn[:, 5 * T:5 * T + 512]))
        self.attention(
            HEADS, 4, T, 1,
            q=lambda h, i: [px[rows(h), NAQ + h // 2, i * P:(i + 1) * P]],
            k=lambda h: [[(a, b, px[rows(h), NAK + h // 2, a:b]) for a, b in pieces(T)]],
            bias=lambda h: self.t["bias"][l * HEADS + h],
            v=lambda h, j, n: pv[:, j, h * 64:(h + 1) * 64],
            outs=lambda h: [y[rows(h), 2 + h // 2, 0:S]],
            scale=HEAD ** -0.5, tmp=self.work, modulation=modulation)

    def context_attention(self):
        px, pv, y = self.px, self.pv, self.xn.rearrange("p (k t) -> p k t", k=KT)
        def rows(h):
            return slice(64 * (h % 2), 64 * (h % 2) + 64)
        self.attention(
            HEADS, 2, CTX, 1,
            q=lambda h, i: [px[rows(h), NAQ + h // 2, S + i * P:S + (i + 1) * P]],
            k=lambda h: [[(0, CTX, px[rows(h), NAK + h // 2, S:T])]],
            bias=None,
            v=lambda h, j, n: pv[:, 4 + j, h * 64:(h + 1) * 64],
            outs=lambda h: [y[rows(h), 2 + h // 2, S:T]],
            scale=HEAD ** -0.5, tmp=self.work)

    def retention(self, l, need_ctx):
        px, pv, y = self.px, self.pv, self.xn.rearrange("p (k t) -> p k t", k=KT)
        w = self.work
        ramps = w[:, 0:3968]
        fwd, bwd, diag = (w[:, i * 896:(i + 1) * 896] for i in range(3))
        cfwd, cbwd = w[:, 2688:3328], w[:, 3328:3968]
        mask = [w[:, 3968 + i * 896:3968 + (i + 1) * 896] for i in range(2)]
        cmask = [w[:, 5760 + i * 640:5760 + (i + 1) * 640] for i in range(2)]
        arg, carg = w[:, 7040:7936], w[:, 7936:8576]
        aw = [w[:, 8576 + i * T:8576 + (i + 1) * T] for i in range(3)]
        qw = T if need_ctx else S
        keys = [(4, qw), (5, qw)] + [(j, S) for j in range(4)]
        n = len(keys)
        landed, vstep, argued = self.sig("inputs_landed"), self.sig("vector_step"), self.sig("argued")
        powered, masked, scored = self.sig("powered"), self.sig("masked"), self.sig("scored")
        weighed, valued, stored = self.sig("weighed"), self.sig("valued"), self.sig("stored")
        astep, carg_done = self.sig("scalar_step"), self.sig("context_powered")
        def rows(h):
            return slice(64 * (h % 2), 64 * (h % 2) + 64)
        sps = [self.ps[:, i * 1024:i * 1024 + T] for i in range(2)]
        yps = [self.ps[:, 2048 + i * 1024:2048 + i * 1024 + T] for i in range(2)]
        with self.stage() as block:
            @block.sync
            def _(sp):
                sp.dma_start(ramps, self.t["ramp"]).then_inc(landed.up(16), 16)

            @block.tensor
            def _(pe):
                def scores(u):
                    h, j = divmod(u, n)
                    tile, width = keys[j]
                    if u >= 2:
                        pe.wait_ge(weighed.sem, weighed.at(u - 1))
                    a0 = tile * P
                    for a, b in pieces(width):
                        mm = pe.matmul(sps[u % 2][:, a:b], px[rows(h), RK + h // 2, a0:a0 + P], px[rows(h), RQ + h // 2, a:b],
                                       start=True, stop=True)
                    mm.then_inc(scored.up(), 1)

                scores(0)
                for u in range(HEADS * n):
                    h, j = divmod(u, n)
                    if u + 1 < HEADS * n:
                        scores(u + 1)
                    if j == 0 and h >= 2:
                        pe.wait_ge(stored.sem, stored.at(h - 1))
                    pe.wait_ge(weighed.sem, weighed.at(u + 1))
                    tile, width = keys[j]
                    for a, b in pieces(width):
                        mm = pe.matmul(yps[h % 2][rows(h), a:b], pv[:, tile, 384 + h * 64:384 + (h + 1) * 64], aw[u % 3][:, a:b],
                                       start=j == 0, stop=j == (n - 1 if a == 0 else 1))
                    mm.then_inc(valued.up(), 1)

            @block.scalar
            def _(act):
                act.wait_ge(landed.sem, landed.at(16))
                for h in range(HEADS):
                    if h >= 2:
                        act.wait_ge(weighed.sem, weighed.at(n * (h - 1)))
                    if h >= 1:
                        act.wait_ge(masked.sem, masked.at(h))
                    act.activation(cmask[h % 2], cfwd, ACT.Exp, scale=self.v(("decay_f", l), h)).then_inc(powered.up(), 1)
                    act.activation(carg, cbwd, ACT.Exp, scale=self.v(("decay_b", l), h)).then_inc(powered.up(), 1)
                    act.wait_ge(argued.sem, argued.at(h + 1))
                    act.activation(mask[h % 2], arg, ACT.Exp).then_inc(powered.up(), 1)

            @block.vector
            def _(dve):
                dve.wait_ge(landed.sem, landed.at(16))

                def masks(h):
                    if h >= 1:
                        dve.wait_ge(powered.sem, powered.at(3 * h))
                    settle(dve, dve.tensor_scalar(arg, fwd, self.v(("decay_f", l), h), None, ALU.mult), vstep)
                    dve.scalar_tensor_tensor(out=arg, in0=bwd, scalar=self.v(("decay_b", l), h), in1=arg,
                                             op0=ALU.mult, op1=ALU.add).then_inc(argued.up(), 1)
                    dve.wait_ge(powered.sem, powered.at(3 * h + 3))
                    dve.tensor_tensor(cmask[h % 2], cmask[h % 2], carg, ALU.add)
                    dve.tensor_tensor(mask[h % 2], mask[h % 2], diag, ALU.add).then_inc(masked.up(), 1)
                    dve.wait_ge(masked.sem, masked.at(h + 1))

                def store(h):
                    dve.wait_ge(valued.sem, valued.at(n * (h + 1)))
                    dve.tensor_copy(y[rows(h), 5 + h // 2, 0:qw], yps[h % 2][rows(h), 0:qw]).then_inc(stored.up(), 1)

                masks(0)
                for u in range(HEADS * n):
                    h, j = divmod(u, n)
                    tile, width = keys[j]
                    dve.wait_ge(scored.sem, scored.at(u + 1))
                    if u >= 3:
                        dve.wait_ge(valued.sem, valued.at(u - 2))
                    if j < 2:
                        m = cmask[h % 2][:, 128 - 128 * j:128 - 128 * j + S]
                    else:
                        m = mask[h % 2][:, 384 - 128 * tile:384 - 128 * tile + S]
                    ins = dve.scalar_tensor_tensor(out=aw[u % 3][:, 0:S], in0=sps[u % 2][:, 0:S], scalar=HEAD ** -0.5, in1=m,
                                                   op0=ALU.mult, op1=ALU.mult)
                    if width > S:
                        m = mask[h % 2][:, 384 - 128 * j:384 - 128 * j + CTX]
                        ins = dve.scalar_tensor_tensor(out=aw[u % 3][:, S:T], in0=sps[u % 2][:, S:T], scalar=HEAD ** -0.5, in1=m,
                                                       op0=ALU.mult, op1=ALU.mult)
                    ins.then_inc(weighed.up(), 1)
                    if j == 3 and h + 1 < HEADS:
                        masks(h + 1)
                    if j == 1 and h >= 1:
                        store(h - 1)
                store(HEADS - 1)

    def retention_output(self, l, need_ctx):
        px, y = self.px, self.xn.rearrange("p (k t) -> p k t", k=KT)
        width = T if need_ctx else S
        w = self.work
        sq = [w[:, i * T:i * T + width] for i in range(3)]
        rstd = [w[:, (3 + i) * T:(3 + i) * T + width] for i in range(3)]
        ga = [w[:, (6 + i) * T:(6 + i) * T + width] for i in range(3)]
        meant, centred, squared = self.sig("summed"), self.sig("centred"), self.sig("squared")
        varied, rooted, vstep, gated = self.sig("varied"), self.sig("rooted"), self.sig("vector_step"), self.sig("gated")
        with self.stage() as block:
            @block.tensor
            def _(pe):
                for i in range(3):
                    for a, b in pieces(width):
                        mm = pe.matmul(self.ps[:, i * 1024 + a:i * 1024 + b], self.group, y[:, 5 + i, a:b], start=True, stop=True)
                    mm.then_inc(meant.up(), 1)
                for i in range(3):
                    pe.wait_ge(squared.sem, squared.at(i + 1))
                    for a, b in pieces(width):
                        mm = pe.matmul(self.ps[:, i * 1024 + a:i * 1024 + b], self.group, sq[i][:, a:b], start=True, stop=True)
                    mm.then_inc(varied.up(), 1)

            @block.scalar
            def _(act):
                for i in range(3):
                    act.activation(ga[i], px[:, GATE + i, 0:width], ACT.Silu).then_inc(gated.up(), 1)
                for i in range(3):
                    act.wait_ge(centred.sem, centred.at(i + 1))
                    act.activation(sq[i], y[:, 5 + i, 0:width], ACT.Square).then_inc(squared.up(), 1)
                for i in range(3):
                    act.wait_ge(varied.sem, varied.at(i + 1))
                    act.activation(rstd[i], self.ps[:, i * 1024:i * 1024 + width], ACT.Sqrt, bias=EPS).then_inc(rooted.up(), 1)

            @block.vector
            def _(dve):
                for i in range(3):
                    dve.wait_ge(meant.sem, meant.at(i + 1))
                    dve.tensor_tensor(y[:, 5 + i, 0:width], y[:, 5 + i, 0:width], self.ps[:, i * 1024:i * 1024 + width],
                                      ALU.subtract).then_inc(centred.up(), 1)
                for i in range(3):
                    t = y[:, 5 + i, 0:width]
                    dve.wait_ge(rooted.sem, rooted.at(i + 1))
                    settle(dve, dve.reciprocal(rstd[i], rstd[i]), vstep)
                    settle(dve, dve.scalar_tensor_tensor(out=t, in0=t, scalar=self.v(("ret_gn_g", l), i), in1=rstd[i],
                                                         op0=ALU.mult, op1=ALU.mult), vstep)
                    dve.wait_ge(gated.sem, gated.at(i + 1))
                    settle(dve, dve.tensor_tensor(t, t, ga[i], ALU.mult), vstep)

    def output_projection(self, src, segments, residual):
        width = segments[-1][1]
        units = [Unit([m // 2], halves(m), range(KT), P, width) for m in range(KT)]

        def finish(eng, i, ps):
            for a, b, gate in segments:
                if gate is None:
                    ins = eng.tensor_tensor(residual(i)[:, a:b], ps[:, a:b], residual(i)[:, a:b], ALU.add)
                else:
                    ins = eng.scalar_tensor_tensor(out=residual(i)[:, a:b], in0=ps[:, a:b], scalar=gate(i), in1=residual(i)[:, a:b],
                                                   op0=ALU.mult, op1=ALU.add)
            return ins

        self.project(units, 4, finish, banks_each=2, sources=[(src(k)[:, 0:width], self.work[:, k * width:(k + 1) * width]) for k in range(KT)])

    def gates(self, l, which, need_ctx):
        def seg(a, b, s):
            return (a, b, lambda k: self.mods[:, l, s, which * KT + k:which * KT + k + 1])
        return [seg(0, S, 0)] + ([seg(S, T, 1)] if need_ctx else [])

    def ffn_up(self, l, need_ctx):
        xn = self.xn.rearrange("p (k t) -> p k t", k=KT)
        width = T if need_ctx else S
        g = self.big[:, 0:FT * width].rearrange("p (m t) -> p m t", m=FT)
        self.g = g
        self.ahead = 0
        padded = S + 2 + (CTX + 1 if need_ctx else 0)
        n = padded - 2
        w = self.work
        u = w[:, 0:4 * 772].rearrange("p (b c t) -> p b c t", b=2, c=2)
        cv = w[:, 3088:3088 + 4 * 772].rearrange("p (b c t) -> p b c t", b=2, c=2)
        runs = [(0, S, 1)] + ([(S, T, S + 2)] if need_ctx else [])
        done, copied, convolved = self.sig("product_done"), self.sig("copied"), self.sig("convolved")
        silued, zeroed, vstep, gated = self.sig("silued"), self.sig("zeroed"), self.sig("vector_step"), self.sig("gated")
        tile_high, tile_low = self.sig("tile_high"), self.sig("tile_low")
        strip_high, strip_low = self.sig("strip_high"), self.sig("strip_low")
        sources = [(xn[:, k, 0:width], room) for k, room in
                   zip(range(KT), tiles_in(width, self.big[:, FT * width:], w[:, 6176:], self.ring[:, 8192:]))]
        low_x, high_x = ([self.rounded(s[part]) for s in sources] for part in (0, 1))
        tiled = lambda a: a.rearrange("p (k c) -> p k c", k=KT)
        high_w = [tiled(self.rounded(self.high[0][:, c * 1024:(c + 1) * 1024])) for c in range(2)]
        first = len(self.freed_at)

        def half(i, c):
            a = (first + i) % RING * STRIP
            slot = self.ring[:, a:a + STRIP]
            return [tiled(view)[:, :, c * P:(c + 1) * P] for view in (slot, self.rounded(slot))]

        cw = lambda j, t: self.v(("conv_w", l), j * 2 * FT + t)
        with self.stage() as block:
            @block.gpsimd
            def _(pool):
                pool.memset(w[:, 0:4 * 772], 0.0).then_inc(zeroed.up(), 1)

            @block.tensor
            def _(pe):
                for i in range(FT):
                    for c in range(2):
                        if i >= 2:
                            pe.wait_ge(copied.sem, copied.at(2 * (i - 2) + c + 1))
                        if i >= 1:
                            pe.wait_ge(strip_low.sem, strip_low.at(2 * i + c - 1))
                        out = self.ps[:, (i % 2) * 2048 + c * 1024:(i % 2) * 2048 + c * 1024 + width]
                        high, low = high_w[c], half(i, c)[1]
                        for k in range(KT):
                            if i == 0 and c == 0:
                                pe.wait_ge(tile_low.sem, tile_low.at(k + 1))
                            for n, (ws, x) in enumerate(((high, low_x), (high, high_x), (low, high_x))):
                                for a, b in pieces(width):
                                    mm = pe.matmul(out[:, a:b], ws[:, k, :], x[k][:, a:b], start=k == 0 and n == 0, stop=k == KT - 1 and n == 2)
                        mm.then_inc(done.up(), 1)
                    self.strips_freed(1)

            @block.sync
            def _(sp):
                self.load_strips(sp)

            @block.scalar
            def _(act):
                act.wait_ge(zeroed.sem, zeroed.at(1))

                def high(i, c):
                    self.strip(act, first + i)
                    act.wait_ge(done.sem, done.at(2 * (i - 1) + c + 1))
                    act.activation(high_w[c], half(i, c)[0], ACT.Copy).then_inc(strip_high.up(), 1)

                def silu(i):
                    act.wait_ge(convolved.sem, convolved.at(2 * i + 1))
                    act.activation(cv[:, i % 2, 0, 0:n], cv[:, i % 2, 0, 0:n], ACT.Silu).then_inc(silued.up(), 1)

                for tile, room in sources:
                    self.split_high(act, tile, room).then_inc(tile_high.up(), 1)
                for i in range(FT):
                    for c in range(2):
                        act.wait_ge(done.sem, done.at(2 * i + c + 1))
                        if i >= 2:
                            act.wait_ge(convolved.sem, convolved.at(2 * (i - 2) + c + 1))
                        for a, b, o in runs:
                            ps = self.ps[:, (i % 2) * 2048 + c * 1024 + a:(i % 2) * 2048 + c * 1024 + b]
                            ins = act.activation(u[:, i % 2, c, o:o + b - a], ps, ACT.Copy)
                        ins.then_inc(copied.up(), 1)
                        if i + 1 < FT:
                            high(i + 1, c)
                    if i >= 1:
                        silu(i - 1)
                silu(FT - 1)

            @block.vector
            def _(dve):
                def low(i, c):
                    dve.wait_ge(strip_high.sem, strip_high.at(2 * i + c - 1))
                    value, low_part = half(i, c)
                    dve.tensor_tensor(low_part, value, high_w[c].bitcast(F32), ALU.subtract).then_inc(strip_low.up(), 1)

                def gate(i):
                    dve.wait_ge(silued.sem, silued.at(i + 1))
                    dve.wait_ge(convolved.sem, convolved.at(2 * i + 2))
                    for a, b, o in runs:
                        o -= 1
                        dve.tensor_tensor(g[:, i, a:b], cv[:, i % 2, 0, o:o + b - a], cv[:, i % 2, 1, o:o + b - a], ALU.mult).then_inc(gated.up(), 1)

                for k in range(KT):
                    dve.wait_ge(tile_high.sem, tile_high.at(k + 1))
                    self.split_low(dve, *sources[k]).then_inc(tile_low.up(), 1)
                for i in range(FT):
                    for c in range(2):
                        t = i + c * FT
                        uu, cc = u[:, i % 2, c, :], cv[:, i % 2, c, 0:n]
                        dve.wait_ge(copied.sem, copied.at(2 * i + c + 1))
                        if i >= 2:
                            dve.wait_ge(gated.sem, gated.at(len(runs) * (i - 1)))
                        settle(dve, dve.tensor_scalar(cc, uu[:, 1:1 + n], cw(1, t), self.v(("conv_b", l), t), ALU.mult, ALU.add), vstep)
                        settle(dve, dve.scalar_tensor_tensor(out=cc, in0=uu[:, 0:n], scalar=cw(0, t), in1=cc, op0=ALU.mult, op1=ALU.add), vstep)
                        dve.scalar_tensor_tensor(out=cc, in0=uu[:, 2:2 + n], scalar=cw(2, t), in1=cc, op0=ALU.mult, op1=ALU.add).then_inc(convolved.up(), 1)
                        if i + 1 < FT:
                            low(i + 1, c)
                    if i >= 1:
                        gate(i - 1)
                gate(FT - 1)

    def ffn_down(self, l, need_ctx):
        width = T if need_ctx else S
        g, segments = self.g, self.gates(l, 5, need_ctx)
        units = [Unit([2 * m, 2 * m + 1], lambda w, j: w[j // 11].rearrange("p (k c) -> p k c", k=FT // 2)[:, j % 11, :], range(FT), P, width)
                 for m in range(KT)]

        def finish(eng, i, ps):
            for a, b, gate in segments:
                ins = eng.scalar_tensor_tensor(out=self.h[:, i, a:b], in0=ps[:, a:b], scalar=gate(i), in1=self.h[:, i, a:b],
                                               op0=ALU.mult, op1=ALU.add)
            return ins

        self.project(units, 2 * KT, finish, banks_each=2,
                     sources=[(g[:, k, :], room) for k, room in zip(range(FT), tiles_in(width, self.xn, self.work))])

    def layer(self, l):
        need_ctx = l < DEPTH - 1
        xn = self.xn.rearrange("p (k t) -> p k t", k=KT)
        self.norm(lambda k: xn[:, k, :], lambda k: self.h[:, k, :], KT, T, self.segments(l, 0), self.work, ahead="strips")
        self.input_projection(l, need_ctx)
        self.pooling(l, need_ctx)
        self.rotate()
        self.neighbourhood(l)
        if need_ctx:
            self.context_attention()
        self.retention(l, need_ctx)
        self.retention_output(l, need_ctx)
        self.output_projection(lambda k: xn[:, k, :], self.gates(l, 2, need_ctx), lambda m: self.h[:, m, :])
        width = T if need_ctx else S
        self.norm(lambda k: xn[:, k, 0:width], lambda k: self.h[:, k, 0:width], KT, width, self.segments(l, 1, need_ctx), self.work, ahead="halves")
        self.ffn_up(l, need_ctx)
        self.ffn_down(l, need_ctx)


    def bigs(self, col, n, width):
        return self.big[:, col:col + n * width].rearrange("p (n t) -> p n t", n=n)

    def xns(self, n, width, col=0):
        return self.xn[:, col:col + n * width].rearrange("p (n t) -> p n t", n=n)

    def sine(self, eng, arg, k, vstep):
        two_pi_hi = 6.28125
        two_pi_lo = 2 * math.pi - two_pi_hi
        magic = 1.5 * 2.0 ** 23
        settle(eng, eng.tensor_scalar(k, arg, 1.0 / (2 * math.pi), magic, ALU.mult, ALU.add), vstep)
        settle(eng, eng.tensor_scalar(k, k, magic, None, ALU.subtract), vstep)
        settle(eng, eng.scalar_tensor_tensor(out=arg, in0=k, scalar=-two_pi_hi, in1=arg, op0=ALU.mult, op1=ALU.add), vstep)
        settle(eng, eng.scalar_tensor_tensor(out=arg, in0=k, scalar=-two_pi_lo, in1=arg, op0=ALU.mult, op1=ALU.add), vstep)
        top = float(np.nextafter(np.float32(math.pi), np.float32(0)))
        return eng.tensor_scalar(arg, arg, top, -top, ALU.min, ALU.max)

    def hyena_inputs(self):
        xn = self.xn
        return [(xn[:, 0:2 * S], self.t["hyena"]), (xn[0:65, 1024:3072], self.t["filter"]), (xn[0:1, 3072:5120], self.t["decay"]),
                (self.work[:, 0:6144], self.t["dft"])]

    def hyena_filters(self):
        taps = self.bigs(0, 4, 4 * S)
        spectra = self.big[:, 8192:8192 + 9216].rearrange("p (o n c) -> p o n c", o=2, n=9)
        self.spectra = spectra
        self.dft = self.work[:, 0:6144].rearrange("p (m k f) -> p m k f", m=3, k=4)
        cos, sin = self.dft[:, 0], self.dft[:, 1]
        feats = self.xn[:, 0:2 * S]
        filt = self.xn[:, 1024:3072]
        decay = self.xn[:, 3072:5120]
        h = [self.work[:, 6144 + i * S:6144 + (i + 1) * S] for i in range(2)]
        k = self.work[:, 7168:7168 + S]
        ex = [self.work[:, 7680 + i * S:7680 + (i + 1) * S] for i in range(2)]
        f = lambda i: self.v("hy_f", i)
        done, vstep, ready, sined = self.sig("product_done"), self.sig("vector_step"), self.sig("reduced"), self.sig("sined")
        with self.stage() as block:
            @block.tensor
            def _(pe):
                pe.matmul(self.ps[0:64, 0:S], self.v("w1", 0, 64)[0:33, :], feats[0:33, 0:S], start=True, stop=True).then_inc(done.up(), 1)
                pe.wait_ge(sined.sem, sined.at(2))
                pe.matmul(self.ps[0:64, 512:512 + S], self.v("w2", 0, 64)[0:64, :], h[0][0:64, :], start=True, stop=True).then_inc(done.up(), 1)

            @block.vector
            def _(dve):
                dve.memset(h[1][64:65, :], 1.0)
                for i in range(2):
                    r = slice(0, 64)
                    dve.wait_ge(done.sem, done.at(i + 1))
                    settle(dve, dve.tensor_scalar(h[i][r, :], self.ps[r, i * 512:i * 512 + S], f(i)[r, :], f(2 + i)[r, :], ALU.add, ALU.mult), vstep)
                    self.sine(dve, h[i][r, :], k[r, :], vstep).then_inc(ready.up(), 1)

            @block.scalar
            def _(act):
                act.activation(decay[0:1, :], decay[0:1, :], ACT.Abs).then_inc(sined.up(), 1)
                for i in range(2):
                    act.wait_ge(ready.sem, ready.at(i + 1))
                    act.activation(h[i][0:64, :], h[i][0:64, :], ACT.Sin).then_inc(sined.up(), 1)

        exped, multiplied = self.sig("exponentials"), self.sig("multiplied")
        units = [(t, c) for t in range(4) for c in range(4)]
        with self.stage() as block:
            @block.tensor
            def _(pe):
                for u, (t, c) in enumerate(units):
                    if u >= 4:
                        pe.wait_ge(multiplied.sem, multiplied.at(u - 3))
                    b = 2 * (u % 4)
                    pe.matmul(self.bank(b + 1), feats[0:1, S + t * P:S + (t + 1) * P], decay[0:1, c * S:(c + 1) * S], start=True, stop=True)
                    pe.matmul(self.bank(b), h[1][0:65, t * P:(t + 1) * P], filt[0:65, c * S:(c + 1) * S], start=True, stop=True).then_inc(done.up(), 1)

            @block.scalar
            def _(act):
                for u, (t, c) in enumerate(units):
                    act.wait_ge(done.sem, done.at(u + 1))
                    if u >= 2:
                        act.wait_ge(multiplied.sem, multiplied.at(u - 1))
                    act.activation(ex[u % 2], self.bank(2 * (u % 4) + 1), ACT.Exp).then_inc(exped.up(), 1)

            @block.vector
            def _(dve):
                for u, (t, c) in enumerate(units):
                    dve.wait_ge(exped.sem, exped.at(u + 1))
                    dve.tensor_tensor(taps[:, t, c * S:(c + 1) * S], self.bank(2 * (u % 4)), ex[u % 2], ALU.mult).then_inc(multiplied.up(), 1)

        combined, taken = self.sig("combined"), self.sig("taken_by_vector")
        with self.stage() as block:
            @block.vector
            def _(dve):
                for o in range(2):
                    settle(dve, dve.memset(taps[0:1, 0, (2 * o + 1) * S:(2 * o + 2) * S], 0.0), vstep)
                    for t in range(4):
                        fw, bw = taps[:, t, 2 * o * S:(2 * o + 1) * S], taps[:, t, (2 * o + 1) * S:(2 * o + 2) * S]
                        settle(dve, dve.tensor_tensor(fw, fw, bw, ALU.add), vstep)
                        dve.scalar_tensor_tensor(out=bw, in0=bw, scalar=-2.0, in1=fw, op0=ALU.mult, op1=ALU.add).then_inc(combined.up(), 1)
                for o in range(2):
                    for n in range(9):
                        u = 9 * o + n
                        dve.wait_ge(done.sem, done.at(u + 1))
                        first = 0 if n % 4 == 0 else 1
                        if n == 0:
                            settle(dve, dve.tensor_scalar(spectra[:, o, 8, :], self.bank(u % 8), self.freq_w[:, 0:1], None, ALU.mult), vstep)
                        if n == 4:
                            settle(dve, dve.tensor_scalar(spectra[:, o, n, :], self.bank(u % 8), self.freq_w[:, first:first + 1], None, ALU.mult), vstep)
                            ins = dve.memset(spectra[0:1, o, 4, :], 0.0)
                        elif n < 8:
                            ins = dve.tensor_scalar(spectra[:, o, n, :], self.bank(u % 8), self.freq_w[:, first:first + 1], None, ALU.mult)
                        else:
                            ins = dve.tensor_scalar(spectra[0:1, o, 8, :], self.bank(u % 8)[0:1, :], self.freq_w[0:1, 0:1], None, ALU.mult)
                        ins.then_inc(taken.up(), 1)

            @block.tensor
            def _(pe):
                for o in range(2):
                    pe.wait_ge(combined.sem, combined.at(4 * (o + 1)))
                    for n in range(9):
                        u = 9 * o + n
                        if u >= 8:
                            pe.wait_ge(taken.sem, taken.at(u - 7))
                        table, half, m = (cos, 0, n) if n < 4 else (sin, 1, n - 4)
                        for t in range(4):
                            if n < 8:
                                lhs, out = table[:, t, m * P:(m + 1) * P], self.bank(u % 8)
                            else:
                                lhs, out, half = sin[:, t, 0:1], self.bank(u % 8)[0:1, :], 0
                            mm = pe.matmul(out, lhs, taps[:, t, (2 * o + half) * S:(2 * o + half + 1) * S], start=t == 0, stop=t == 3)
                        mm.then_inc(done.up(), 1)

    def second_projection(self):
        xn = self.xns(KT, S)
        p2 = self.bigs(0, 16, S)
        self.p2 = p2
        units = []
        for m in range(16):
            s = m // 2 if m < 2 else (1 if m < 4 else 2 + (m - 4) // 2)
            o, n = (64, 96) if m == MKR else (0 if m == MKV else (m % 2) * P, P)
            units.append(Unit([s], lambda w, j, o=o, n=n: w[0].rearrange("p (k c) -> p k c", k=KT)[:, j, o:o + n], range(KT), n, S))

        def finish(eng, i, ps):
            n = 96 if i == MKR else P
            return eng.tensor_copy(p2[0:n, i, :], ps)

        self.project(units, 8, finish, sources=[(xn[:, k, :], self.work[:, 6144 + k * S:6144 + (k + 1) * S]) for k in range(KT)])

    def hyena(self):
        p2, u = self.p2, self.xns(4, 3 * S)
        free = self.big[:, 2048:8192]
        cos, sin, sint = self.dft[:, 0], self.dft[:, 1], self.dft[:, 2]
        cv = [self.work[:, 6144 + i * S:6144 + (i + 1) * S] for i in range(2)]
        done, vstep, conv, turned = self.sig("product_done"), self.sig("vector_step"), self.sig("convolved"), self.sig("turned")
        copied = self.sig("copied")
        with self.stage() as block:
            @block.vector
            def _(dve):
                for i in range(12):
                    src, c = p2[:, HY + i, :], cv[i % 2]
                    if i >= 2:
                        dve.wait_ge(turned.sem, turned.at(i - 1))
                    settle(dve, dve.tensor_scalar(c, src, self.v("hy_cw", 12 + i), self.v("hy_cb", i), ALU.mult, ALU.add), vstep)
                    settle(dve, dve.scalar_tensor_tensor(out=c[:, 1:S], in0=src[:, 0:S - 1], scalar=self.v("hy_cw", i), in1=c[:, 1:S],
                                                         op0=ALU.mult, op1=ALU.add), vstep)
                    dve.scalar_tensor_tensor(out=c[:, 0:S - 1], in0=src[:, 1:S], scalar=self.v("hy_cw", 24 + i), in1=c[:, 0:S - 1],
                                             op0=ALU.mult, op1=ALU.add).then_inc(conv.up(), 1)

            @block.tensor
            def _(pe):
                for i in range(12):
                    pe.wait_ge(conv.sem, conv.at(i + 1))
                    if i >= 4:
                        pe.wait_ge(copied.sem, copied.at(i - 3))
                    for t in range(4):
                        mm = pe.transpose(self.bank(i % 4)[:, t * P:(t + 1) * P], cv[i % 2][:, t * P:(t + 1) * P], self.ident)
                    mm.then_inc(turned.up(), 1)

            @block.scalar
            def _(act):
                for i in range(12):
                    act.wait_ge(turned.sem, turned.at(i + 1))
                    act.activation(u[:, :, i * P:(i + 1) * P], self.bank(i % 4).rearrange("p (t c) -> p t c", t=4), ACT.Copy).then_inc(copied.up(), 1)

        y = self.bigs(2048, 8, S)
        tmp = [self.work[:, 6144 + i * S:6144 + (i + 1) * S] for i in range(4)]
        skip = self.work[:, 8192:9216]
        self.load([(skip, self.t["skip"])])
        z = [u[:, t, 2 * S:3 * S] for t in range(4)]
        taken, filtered, gated = self.sig("taken_by_vector"), self.sig("filtered"), self.sig("gated")
        for o in range(2):
            sp = self.spectra[:, o]
            with self.stage() as block:
                @block.tensor
                def _(pe):
                    for m in range(4):
                        for half, table in enumerate((cos, sin)):
                            for t in range(4):
                                mm = pe.matmul(self.bank(2 * m + half), table[:, t, m * P:(m + 1) * P], z[t], start=t == 0, stop=t == 3)
                            mm.then_inc(done.up(), 1)
                    for t in range(4):
                        pe.wait_ge(filtered.sem, filtered.at(4))
                        for m in range(4):
                            pe.matmul(self.bank(t), cos[:, m, t * P:(t + 1) * P], y[:, m, :], start=m == 0, stop=False)
                            mm = pe.matmul(self.bank(t), sint[:, m, t * P:(t + 1) * P], y[:, 4 + m, :], start=False, stop=m == 3)
                        mm.then_inc(done.up(), 1)

                @block.vector
                def _(dve):
                    for m in range(4):
                        dve.wait_ge(done.sem, done.at(2 * m + 2))
                        re, im = self.bank(2 * m), self.bank(2 * m + 1)
                        kc, ks, kd = sp[:, m, :], sp[:, 4 + m, :], sp[:, 8 if m == 0 else m, :]
                        a, b = tmp[2 * (m % 2)], tmp[2 * (m % 2) + 1]
                        dve.tensor_tensor(y[:, m, :], re, kc, ALU.mult)
                        dve.tensor_tensor(a, im, ks, ALU.mult)
                        dve.tensor_tensor(y[:, 4 + m, :], re, ks, ALU.mult)
                        settle(dve, dve.tensor_tensor(b, im, kd, ALU.mult), vstep)
                        settle(dve, dve.tensor_tensor(y[:, m, :], y[:, m, :], a, ALU.subtract), vstep)
                        dve.tensor_tensor(y[:, 4 + m, :], y[:, 4 + m, :], b, ALU.add).then_inc(filtered.up(), 1)
                    for t in range(4):
                        if t >= 2:
                            dve.wait_ge(gated.sem, gated.at(t - 1))
                        settle(dve, dve.tensor_tensor(tmp[t % 2], z[t], skip[:, o * S:(o + 1) * S], ALU.mult), vstep)
                        dve.wait_ge(done.sem, done.at(9 + t))
                        settle(dve, dve.tensor_tensor(tmp[t % 2], self.bank(t), tmp[t % 2], ALU.add), vstep)
                        dve.tensor_tensor(z[t], tmp[t % 2], u[:, t, o * S:(o + 1) * S], ALU.mult).then_inc(gated.up(), 1)

        self.mix = self.bigs(8192, 8, S)
        squared, rooted, normed = self.sig("squared"), self.sig("rooted"), self.sig("normalised")
        ss, rs = self.small[:, 0:4], self.small[:, 4:8]
        with self.stage() as block:
            @block.scalar
            def _(act):
                for t in range(4):
                    act.activation(tmp[t], z[t], ACT.Square, accum_out=ss[:, t:t + 1]).then_inc(squared.up(), 1)
                act.wait_ge(squared.sem, squared.at(4))
                act.activation(rs, ss, ACT.Sqrt, scale=1.0 / S, bias=EPS).then_inc(rooted.up(), 1)

            @block.vector
            def _(dve):
                dve.wait_ge(rooted.sem, rooted.at(1))
                settle(dve, dve.reciprocal(rs, rs), vstep)
                for t in range(4):
                    dve.tensor_scalar(z[t], z[t], rs[:, t:t + 1], None, ALU.mult).then_inc(normed.up(), 1)
                for i in range(4):
                    dve.wait_ge(turned.sem, turned.at(i + 1))
                    dve.tensor_scalar(self.mix[:, 4 + i, :], self.bank(i), self.v("hyout_g", i), None, ALU.mult)

            @block.tensor
            def _(pe):
                pe.wait_ge(normed.sem, normed.at(4))
                for i in range(4):
                    for t in range(4):
                        mm = pe.transpose(self.bank(i)[:, t * P:(t + 1) * P], z[t][:, i * P:(i + 1) * P], self.ident)
                    mm.then_inc(turned.up(), 1)

    def latent_attention(self):
        p2, mix = self.p2, self.mix
        whole = lambda gain: [(0, S, gain, None)]
        self.norm(lambda k: p2[:, MQ + k, :], lambda k: p2[:, MQ + k, :], 2, S, whole(lambda k: self.v("q_g", k)), self.work)
        table = self.work[:, 8192:9344]
        self.norm(lambda k: p2[:, MKV, :], lambda k: p2[:, MKV, :], 1, S, whole(lambda k: self.v("kv_g")), self.work,
                  load=[(table, self.t["rope96"])], ahead="strips")
        q = self.bigs(12288, MLA_HEADS, S)
        kk = self.xns(MLA_HEADS, S)
        v = self.xns(4, S, 4096)
        units, dst = [], []
        for h in range(MLA_HEADS):
            units.append(Unit([0], lambda w, j, h=h: w[0].rearrange("p (k c) -> p k c", k=2)[:, j, h * 96:(h + 1) * 96], [0, 1], 96, S))
            dst.append(q[0:96, h, :])
        for h in range(MLA_HEADS):
            units.append(Unit([1], lambda w, j, h=h: w[0][:, h * 64:(h + 1) * 64], [2], 64, S))
            dst.append(kk[0:64, h, :])
        for t in range(4):
            units.append(Unit([1], lambda w, j: w[0][:, 512:1024], [2], P, S, slice(t * P, (t + 1) * P)))
            dst.append(v[:, t, :])

        def finish(eng, i, ps):
            if eng is self.nc.scalar:
                return eng.activation(dst[i], ps, ACT.Copy)
            return eng.tensor_copy(dst[i], ps)

        self.project(units, 2, finish, sources=[(p2[:, m, :], self.work[:, i * S:(i + 1) * S]) for i, m in enumerate((MQ, MQ + 1, MKV))])
        tmp = [self.work[:, i * S:(i + 1) * S] for i in range(2)]
        self._rotate([q[0:96, h, :] for h in range(MLA_HEADS)] + [p2[0:96, MKR, :]], 96, table, tmp)
        with self.stage() as block:
            @block.vector
            def _(dve):
                for h in range(MLA_HEADS):
                    dve.tensor_copy(kk[64:96, h, :], p2[64:96, MKR, :])
        def rows(h):
            return slice(64 * (h % 2), 64 * (h % 2) + 64)
        self.attention(
            MLA_HEADS, 4, S, 1,
            q=lambda h, i: [q[0:96, h, i * P:(i + 1) * P]],
            k=lambda h: [[(0, S, kk[0:96, h, :])]],
            bias=None,
            v=lambda h, j, n: v[:, j, h * 64:(h + 1) * 64],
            outs=lambda h: [mix[rows(h), h // 2, :]],
            scale=96 ** -0.5, tmp=self.work)
        self.norm(lambda k: mix[:, k, :], lambda k: mix[:, k, :], 4, S, whole(lambda k: self.v("attn_g", k)), self.work, ahead="strips")

    def memory_attention(self):
        xn = self.xns(KT, S)
        self.norm(lambda k: xn[:, k, :], lambda k: self.x[:, k, :], KT, S, [(0, S, lambda k: self.v("cross_g", k), None)], self.work,
                  load=[(self.big[:, 0:2048].rearrange("p (k t) -> p k t", k=KT), self.t["memory"])])
        mem, hm = self.bigs(0, KT, 256), self.bigs(2048, KT, 256)
        self.norm(lambda k: hm[:, k, :], lambda k: mem[:, k, :], KT, 256, [(0, 256, lambda k: self.v("mem_g", k), None)], self.work, ahead="strips")
        keys, v, q, o = self.bigs(4096, KT, 256), self.bigs(6144, 2, D), self.bigs(8192, KT, S), self.bigs(12288, KT, S)
        units, dst = [], []

        for m in range(KT):
            units.append(Unit([m // 2], halves(m), range(KT), P, 256))
            dst.append(keys[:, m, :])
        for c in range(4):
            for t in range(2):
                units.append(Unit([4 + c], lambda w, j: w[0].rearrange("p (k c) -> p k c", k=KT)[:, j, :], range(KT), P, 256,
                                  slice(t * P, (t + 1) * P)))
                dst.append(v[:, t, c * 256:(c + 1) * 256])
        for m in range(KT):
            units.append(Unit([8 + m // 2], halves(m), range(KT, 2 * KT), P, S))
            dst.append(q[:, m, :])
        sources = [(hm[:, k, :], self.work[:, k * 256:(k + 1) * 256]) for k in range(KT)]
        sources += [(xn[:, k, :], self.work[:, 2048 + k * S:2048 + (k + 1) * S]) for k in range(KT)]
        self.project(units, 12, lambda eng, i, ps: eng.tensor_copy(dst[i], ps), sources=sources)
        self.attention(
            MEM_HEADS, 4, 256, 2,
            q=lambda h, i: [q[:, 2 * h + d, i * P:(i + 1) * P] for d in range(2)],
            k=lambda h: [[(0, 256, keys[:, 2 * h + d, :])] for d in range(2)],
            bias=None,
            v=lambda h, j, n: v[:, j, h * 256 + n * P:h * 256 + (n + 1) * P],
            outs=lambda h: [o[:, 2 * h + n, :] for n in range(2)],
            scale=1.0 / 16, tmp=self.work)
        self.output_projection(lambda k: o[:, k, :], [(0, S, None)], lambda m: self.x[:, m, :])

    def route(self):
        xn = self.xns(KT, S)
        w = self.work[:, 9600:9888].rearrange("p (k c) -> p k c", k=KT)
        tokens = self.work[:, 0:4 * D].rearrange("p (t c) -> p t c", t=4)
        tmp = self.work[:, 4 * D:9088]
        at = [0]

        def take(*dims):
            n = int(np.prod(dims))
            a = tmp[:, at[0]:at[0] + n]
            at[0] += n
            return a.rearrange("p (a b) -> p a b", a=dims[0]) if len(dims) > 1 else a

        logits = take(4, 36)
        one_g, ex, picked = take(4, 4), take(4, 4), take(4, 32)
        e_in, one_1, one_2, rest, weight = take(4, 8), take(4, 8), take(4, 8), take(4, 8), take(4, 8)
        comb, chosen_1, chosen_2, chosen, position = take(4, 32), take(4, 32), take(4, 32), take(4, 32), take(4, 32)
        top, total, v1, v2, p1, p2, m = (take(4) for _ in range(7))
        pos, crowd = take(4), take(4)
        self.share = self.small[:, 64:72]
        self.slot_of = self.small[:, 72:80].bitcast(mybir.dt.uint32)
        numbers = self.small[:, 80:84].bitcast(mybir.dt.uint32)
        zeros = self.small[:, 84:100].bitcast(mybir.dt.uint32)
        self.token_of = self.small[:, 100:116].bitcast(mybir.dt.uint32)
        self.crowded = self.small[:, 116:117].bitcast(mybir.dt.int32)
        self.norm(lambda k: xn[:, k, :], lambda k: self.x[:, k, :], KT, S, [(0, S, lambda k: self.v("ffn_g", k), None)], self.work,
                  load=[(w, self.t["route"])])
        self.sparse = SparseExperts(self)
        done, vstep, exped, ready = self.sig("product_done"), self.sig("vector_step"), self.sig("exponentials"), self.sig("argued")
        turned, copied, stored = self.sig("turned"), self.sig("copied"), self.sig("outputs_stored")
        comb_t = self.work[:, 9088:9600]
        self.comb_dram = self.nc.dram_tensor("combine", [EXPERTS, S], F32, kind="Internal").ap()
        self.tokens_dram = self.nc.dram_tensor("token_rows", [S, D], F32, kind="Internal").ap()
        self.table_dram = self.nc.dram_tensor("slot_table", [EXPERTS * SLOTS, 1], mybir.dt.uint32, kind="Internal").ap()
        chose, ranked, token_copied = self.sig("combined"), self.sig("valued"), self.sig("gated")
        cleared, zeroed, located = self.sig("table_cleared"), self.sig("zeroed"), self.sig("squared")
        wide = lambda a, n: a.unsqueeze(2).to_broadcast([P, 4, n])
        rank = lambda n: self.rank[:, 8 - n:8].unsqueeze(1).to_broadcast([P, 4, n])
        with self.stage() as block:
            @block.tensor
            def _(pe):
                for t in range(4):
                    for k in range(KT):
                        mm = pe.matmul(self.ps[:, t * 36:(t + 1) * 36], xn[:, k, t * P:(t + 1) * P], w[:, k, :], start=k == 0, stop=k == KT - 1)
                mm.then_inc(done.up(), 1)
                for t in range(4):
                    if t >= 2:
                        pe.wait_ge(token_copied.sem, token_copied.at(t - 1))
                    for k in range(KT):
                        mm = pe.transpose(self.ps[:, 2048 + (t % 2) * 1024 + k * P:2048 + (t % 2) * 1024 + (k + 1) * P],
                                          xn[:, k, t * P:(t + 1) * P], self.ident)
                    mm.then_inc(turned.up(), 1)
                pe.wait_ge(chose.sem, chose.at(1))
                for t in range(5):
                    for j in range(min(t + 1, 4)):
                        mm = pe.matmul(self.ps[:, 1024 + t * 32:1024 + (t + 1) * 32], self.earlier if j == t else self.ones,
                                       chosen[:, j, :], start=j == 0, stop=j == min(t, 3))
                mm.then_inc(ranked.up(), 1)
                pe.wait_ge(ready.sem, ready.at(3))
                for t in range(4):
                    mm = pe.transpose(self.ps[0:32, 512 + t * P:512 + (t + 1) * P], comb[:, t, :], self.ident)
                mm.then_inc(turned.up(), 1)

            @block.scalar
            def _(act):
                for t in range(4):
                    act.wait_ge(turned.sem, turned.at(t + 1))
                    act.activation(tokens[:, t, :], self.ps[:, 2048 + (t % 2) * 1024:3072 + (t % 2) * 1024], ACT.Copy).then_inc(token_copied.up(), 1)
                act.wait_ge(ready.sem, ready.at(1))
                act.activation(ex, ex, ACT.Exp).then_inc(exped.up(), 1)
                act.wait_ge(ready.sem, ready.at(2))
                act.activation(p2, p2, ACT.Exp).then_inc(exped.up(), 1)

            @block.vector
            def _(dve):
                def do(ins):
                    settle(dve, ins, vstep)

                def first_best(hot, values, best, n):
                    do(dve.tensor_tensor(hot, values, wide(best, n), ALU.is_equal))
                    do(dve.tensor_tensor(hot, hot, rank(n), ALU.mult))
                    do(dve.reduce_max(m, hot, AX))
                    do(dve.tensor_tensor(hot, hot, wide(m, n), ALU.is_equal))

                dve.wait_ge(done.sem, done.at(1))
                do(dve.tensor_tensor(logits.rearrange("p a b -> p (a b)"), self.ps[:, 0:144], self.v("route_b", 0, 144), ALU.add))
                g, e = logits[:, :, 0:4], logits[:, :, 4:36]
                do(dve.reduce_max(top, g, AX))
                dve.tensor_tensor(ex, g, wide(top, 4), ALU.subtract).then_inc(ready.up(), 1)
                first_best(one_g, g, top, 4)
                for i in range(GROUPS):
                    do(dve.tensor_tensor(picked[:, :, i * 8:(i + 1) * 8], e[:, :, i * 8:(i + 1) * 8], one_g[:, :, i:i + 1].to_broadcast([P, 4, 8]), ALU.mult))
                do(dve.tensor_tensor(e_in, picked[:, :, 0:8], picked[:, :, 8:16], ALU.add))
                do(dve.tensor_tensor(e_in, e_in, picked[:, :, 16:24], ALU.add))
                do(dve.tensor_tensor(e_in, e_in, picked[:, :, 24:32], ALU.add))
                do(dve.reduce_max(v1, e_in, AX))
                first_best(one_1, e_in, v1, 8)
                do(dve.scalar_tensor_tensor(out=rest, in0=one_1, scalar=-3.0e38, in1=e_in, op0=ALU.mult, op1=ALU.add))
                do(dve.reduce_max(v2, rest, AX))
                first_best(one_2, rest, v2, 8)
                dve.tensor_tensor(p2, v2, v1, ALU.subtract).then_inc(ready.up(), 1)
                dve.wait_ge(exped.sem, exped.at(2))
                do(dve.reduce_sum(total, ex, AX))
                do(dve.tensor_scalar(p1, p2, 1.0, None, ALU.add))
                do(dve.tensor_tensor(p1, p1, total, ALU.mult))
                do(dve.reciprocal(p1, p1))
                do(dve.tensor_tensor(p2, p2, p1, ALU.mult))
                for i in range(GROUPS):
                    r = slice(i * 8, (i + 1) * 8)
                    hot = one_g[:, :, i:i + 1].to_broadcast([P, 4, 8])
                    do(dve.tensor_tensor(chosen_1[:, :, r], one_1, hot, ALU.mult))
                    do(dve.tensor_tensor(chosen_2[:, :, r], one_2, hot, ALU.mult))
                dve.tensor_tensor(chosen, chosen_1, chosen_2, ALU.add).then_inc(chose.up(), 1)
                do(dve.tensor_copy(numbers, self.token_number))
                dve.wait_ge(ranked.sem, ranked.at(1))
                do(dve.tensor_tensor(position, self.ps[:, 1024:1152].rearrange("p (t e) -> p t e", t=4),
                                     self.first_slot.unsqueeze(1).to_broadcast([P, 4, 32]), ALU.add))
                for i, c in enumerate((chosen_1, chosen_2)):
                    do(dve.tensor_tensor(c, c, position, ALU.mult))
                    do(dve.reduce_sum(pos, c, AX))
                    do(dve.tensor_copy(self.slot_of[:, i * 4:(i + 1) * 4], pos))
                do(dve.reduce_max(crowd[:, 0:1], self.ps[:, 1152:1184], AX))
                do(dve.tensor_scalar(crowd[:, 1:2], crowd[:, 0:1], float(SLOTS), None, ALU.is_gt))
                do(dve.tensor_copy(self.crowded, crowd[:, 1:2]))
                do(dve.tensor_copy(self.share[:, 0:4], p1))
                do(dve.tensor_copy(self.share[:, 4:8], p2))
                do(dve.tensor_tensor(one_1, one_1, wide(p1, 8), ALU.mult))
                do(dve.tensor_tensor(one_2, one_2, wide(p2, 8), ALU.mult))
                do(dve.tensor_tensor(weight, one_1, one_2, ALU.add))
                for i in range(GROUPS):
                    ins = dve.tensor_tensor(comb[:, :, i * 8:(i + 1) * 8], weight, one_g[:, :, i:i + 1].to_broadcast([P, 4, 8]), ALU.mult)
                    if i < GROUPS - 1:
                        do(ins)
                ins.then_inc(ready.up(), 1)
                dve.wait_ge(turned.sem, turned.at(5))
                dve.tensor_copy(comb_t[0:32, :], self.ps[0:32, 512:1024]).then_inc(copied.up(), 1)

            @block.gpsimd
            def _(pool):
                pool.memset(zeros, 0).then_inc(zeroed.up(), 1)
                pool.wait_ge(zeroed.sem, zeroed.at(1))
                pool.dma_start(self.table_dram.rearrange("(p c) o -> p (c o)", p=P), zeros).then_inc(cleared.up(16), 16)
                pool.wait_ge(cleared.sem, cleared.at(16))

            @block.sync
            def _(sp):
                self.sparse.load_first(sp)
                sp.wait_ge(token_copied.sem, token_copied.at(4))
                sp.dma_start(self.tokens_dram.rearrange("(t p) c -> p t c", p=P), tokens).then_inc(stored.up(16), 16)
                sp.wait_ge(copied.sem, copied.at(1))
                sp.dma_start(self.comb_dram, comb_t[0:32, :]).then_inc(stored.up(16), 16)
                sp.wait_ge(stored.sem, stored.at(32))

    def experts(self):
        sparse, dense = self.sparse, DenseExperts(self)

        def flag(engine):
            return engine.value_load(self.crowded[0:1, 0:1], min_val=0, max_val=1)

        with self.stage() as block:
            @block.sync
            def _(sp):
                with sp.If(flag(sp) == 0):
                    sparse.sync(sp)
                with sp.Else():
                    dense.sync(sp)

            @block.tensor
            def _(pe):
                with pe.If(flag(pe) == 0):
                    sparse.tensor(pe)
                with pe.Else():
                    dense.tensor(pe)

            @block.scalar
            def _(act):
                with act.If(flag(act) == 0):
                    sparse.scalar(act)
                with act.Else():
                    dense.scalar(act)

            @block.vector
            def _(dve):
                with dve.If(flag(dve) == 0):
                    sparse.vector(dve)
                with dve.Else():
                    dense.vector(dve)

            @block.gpsimd
            def _(pool):
                with pool.If(flag(pool) == 0):
                    sparse.gpsimd(pool)
                with pool.Else():
                    dense.gpsimd(pool)

    def finish(self):
        rows = self.big[:, 0:8192].rearrange("p (e t c) -> p e t c", e=2, t=4)
        y = self.xn[:, 0:4 * D].rearrange("p (t c) -> p t c", t=4)
        gain, sq = self.work[:, 0:D], self.work[:, D:2 * D]
        ss, rs = self.small[:, 0:4], self.small[:, 4:8]
        turned, summed, squared, rooted = self.sig("turned"), self.sig("summed"), self.sig("squared"), self.sig("rooted")
        vstep, ready, stored, landed = self.sig("vector_step"), self.sig("normalised"), self.sig("outputs_stored"), self.sig("inputs_landed")
        ps = [self.ps[:, t * D:(t + 1) * D] for t in range(4)]
        with self.stage() as block:
            @block.tensor
            def _(pe):
                for t in range(4):
                    for k in range(KT):
                        mm = pe.transpose(ps[t][:, k * P:(k + 1) * P], self.x[:, k, t * P:(t + 1) * P], self.ident)
                    mm.then_inc(turned.up(), 1)

            @block.vector
            def _(dve):
                for t in range(4):
                    dve.wait_ge(turned.sem, turned.at(t + 1))
                    settle(dve, dve.scalar_tensor_tensor(out=y[:, t, :], in0=rows[:, 0, t, :], scalar=self.share[:, t:t + 1], in1=ps[t],
                                                         op0=ALU.mult, op1=ALU.add), vstep)
                    dve.scalar_tensor_tensor(out=y[:, t, :], in0=rows[:, 1, t, :], scalar=self.share[:, 4 + t:5 + t], in1=y[:, t, :],
                                             op0=ALU.mult, op1=ALU.add).then_inc(summed.up(), 1)
                dve.wait_ge(rooted.sem, rooted.at(1))
                dve.wait_ge(landed.sem, landed.at(16))
                settle(dve, dve.reciprocal(rs, rs), vstep)
                for t in range(4):
                    dve.scalar_tensor_tensor(out=y[:, t, :], in0=y[:, t, :], scalar=rs[:, t:t + 1], in1=gain,
                                             op0=ALU.mult, op1=ALU.mult).then_inc(ready.up(), 1)

            @block.scalar
            def _(act):
                for t in range(4):
                    act.wait_ge(summed.sem, summed.at(t + 1))
                    if t >= 1:
                        act.wait_ge(squared.sem, squared.at(t))
                    act.activation(sq, y[:, t, :], ACT.Square, accum_out=ss[:, t:t + 1]).then_inc(squared.up(), 1)
                act.wait_ge(squared.sem, squared.at(4))
                act.activation(rs, ss, ACT.Sqrt, scale=1.0 / D, bias=EPS).then_inc(rooted.up(), 1)

            @block.sync
            def _(sp):
                sp.dma_start(gain, self.t["last_gain"]).then_inc(landed.up(16), 16)
                for t in range(4):
                    sp.wait_ge(ready.sem, ready.at(t + 1))
                    sp.dma_start(self.out[t * P:(t + 1) * P, :], y[:, t, :]).then_inc(stored.up(16), 16)
                sp.wait_ge(stored.sem, stored.at(64))

    def second(self):
        xn = self.xns(KT, S)
        whole = lambda name: [(0, S, lambda k: self.v(name, k), None)]
        stream = lambda k: self.x[:, k, :]
        self.norm(stream, stream, KT, S, whole("final_g"), self.work[:, 6144:], load=self.hyena_inputs())
        self.hyena_filters()
        self.norm(lambda k: xn[:, k, :], stream, KT, S, whole("mix_g"), self.work[:, 6144:], ahead="strips")
        self.second_projection()
        self.hyena()
        self.latent_attention()
        self.output_projection(lambda k: self.mix[:, k, :], [(0, S, None)], stream)
        self.memory_attention()
        self.route()
        self.experts()
        self.finish()


class DenseExperts:

    turns = EXPERTS // 2

    def __init__(self, b):
        self.b, nc = b, b.nc
        self.xn = b.xns(KT, S)
        big = b.big
        self.gu = [big[:, e * 6144:e * 6144 + 4096].rearrange("p (k c) -> p k c", k=KT) for e in range(2)]
        self.dn = [big[:, e * 6144 + 4096:(e + 1) * 6144].rearrange("p (k c) -> p k c", k=2) for e in range(2)]
        self.comb = [big[:, 12288 + i * S:12288 + (i + 1) * S] for i in range(2)]
        self.act_t = [big[:, 13312 + i * S:13312 + (i + 1) * S] for i in range(2)]
        self.hidden = [b.work[:, i * S:(i + 1) * S] for i in range(4)]
        self.gu_landed = [nc.alloc_semaphore(f"dense_gate_up_landed_{i}") for i in range(2)]
        self.dn_landed = [nc.alloc_semaphore(f"dense_down_landed_{i}") for i in range(2)]
        self.comb_landed = [nc.alloc_semaphore(f"combine_landed_{i}") for i in range(2)]
        self.cleared = nc.alloc_semaphore("dense_shares_cleared")
        (self.up_done, self.silued, self.hidden_done, self.down_done, self.added, self.weighed) = (
            nc.alloc_semaphore("dense_" + n) for n in ("up_done", "silu_done", "hidden_done", "down_done", "added", "silu_weighed"))

    def sync(self, sp):
        t = self.b.t["experts"]

        def load_gu(it, e):
            sp.dma_start(self.gu[e].rearrange("p k c -> p (k c)"), t[bass.ds(it * 2 + e, 1), :, 0:4096].rearrange("a p c -> (a p) c"))\
                .then_inc(self.gu_landed[e], 16)

        def load_dn(it, e):
            sp.dma_start(self.dn[e].rearrange("p k c -> p (k c)"), t[bass.ds(it * 2 + e, 1), :, 4096:6144].rearrange("a p c -> (a p) c"))\
                .then_inc(self.dn_landed[e], 16)

        def load_comb(it, e):
            sp.dma_start(self.comb[e], self.b.comb_dram[bass.ds(it * 2 + e, 1), :].to_broadcast([P, S])).then_inc(self.comb_landed[e], 16)

        for landed in self.b.sparse.gu_landed + self.b.sparse.dn_landed:
            sp.wait_ge(landed, 16)
        for e in range(2):
            load_gu(0, e)
            load_comb(0, e)
            load_dn(0, e)
        with sp.Fori(1, self.turns) as it:
            for e in range(2):
                sp.wait_ge(self.up_done, it * 8 - 4 + 4 * e)
                load_gu(it, e)
                sp.wait_ge(self.hidden_done, it * 4 - 2 + 2 * e)
                load_comb(it, e)
            sp.wait_ge(self.down_done, it * 8)
            for e in range(2):
                load_dn(it, e)

    def tensor(self, pe):
        b = self.b
        with pe.Fori(0, self.turns) as it:
            for e in range(2):
                pe.wait_ge(self.gu_landed[e], it * 16 + 16)
                for m in range(2):
                    for j in range(2):
                        if e == 1:
                            pe.wait_ge(self.hidden_done, it * 4 + m + 1)
                        c = 256 * j + m * P
                        for k in range(KT):
                            mm = pe.matmul(b.bank(2 * m + j), self.gu[e][:, k, c:c + P], self.xn[:, k, :], start=k == 0, stop=k == KT - 1)
                        mm.then_inc(self.up_done, 1)
            for half in range(2):
                for e in range(2):
                    if half == 0:
                        pe.wait_ge(self.dn_landed[e], it * 16 + 16)
                        pe.wait_ge(self.hidden_done, it * 4 + 2 + 2 * e)
                    for d in range(4):
                        if e == 0 and half == 1:
                            pe.wait_ge(self.added, it * 8 + d + 1)
                        c = (4 * half + d) * P
                        for k in range(2):
                            mm = pe.matmul(b.bank(4 + d), self.dn[e][:, k, c:c + P], self.hidden[2 * e + k], start=e == 0 and k == 0, stop=e == 1 and k == 1)
                        if e == 1:
                            mm.then_inc(self.down_done, 1)

    def scalar(self, act):
        with act.Fori(0, self.turns) as it:
            for e in range(2):
                for m in range(2):
                    act.wait_ge(self.up_done, it * 8 + 4 * e + 2 * m + 1)
                    if e == 1:
                        act.wait_ge(self.hidden_done, it * 4 + m + 1)
                    act.activation(self.act_t[m], self.b.bank(2 * m), ACT.Silu).then_inc(self.silued, 1)

    def vector(self, dve):
        b = self.b
        with dve.Fori(0, self.turns) as it:
            for e in range(2):
                dve.wait_ge(self.comb_landed[e], it * 16 + 16)
                for m in range(2):
                    i = 2 * e + m
                    dve.wait_ge(self.silued, it * 4 + i + 1)
                    dve.tensor_tensor(self.act_t[m], self.act_t[m], self.comb[e], ALU.mult).then_inc(self.weighed, 1)
                    dve.wait_ge(self.weighed, it * 4 + i + 1)
                    dve.wait_ge(self.up_done, it * 8 + 4 * e + 2 * m + 2)
                    dve.tensor_tensor(self.hidden[i], b.bank(2 * m + 1), self.act_t[m], ALU.mult).then_inc(self.hidden_done, 1)
            for d in range(8):
                dve.wait_ge(self.down_done, it * 8 + d + 1)
                dve.tensor_tensor(b.x[:, d, :], b.bank(4 + d % 4), b.x[:, d, :], ALU.add).then_inc(self.added, 1)

    def gpsimd(self, pool):
        pool.wait_ge(self.down_done, self.turns * 8)
        pool.memset(self.b.big[:, 0:8192], 0.0).then_inc(self.cleared, 1)
        pool.wait_ge(self.cleared, 1)


class SparseExperts:

    turns = EXPERTS // 4

    def __init__(self, b):
        self.b, nc = b, b.nc
        big, ring, w = b.big, b.ring, b.work
        gu = [big[:, i * 4096:(i + 1) * 4096] for i in range(3)] + [ring[:, 0:4096]]
        dn = [big[:, 12288:14336], big[:, 14336:16384], ring[:, 4096:6144], ring[:, 6144:8192]]
        self.gu_at, self.dn_at = gu, dn
        self.gu = [a.rearrange("p (k c) -> p k c", k=KT) for a in gu]
        self.dn = [a.rearrange("p (k c) -> p k c", k=2) for a in dn]
        self.rows = [ring[:, 8192:9216], ring[:, 9216:10240]]
        self.rows_t = w[:, 0:D].rearrange("p (k s) -> p k s", k=KT)
        self.silu_t, self.hidden = w[:, D:D + 256], w[:, D + 256:D + 512]
        self.hidden_t = w[:, D + 512:D + 768].rearrange("p (k s) -> p k s", k=2)
        self.result = [w[:, 2048:3072], w[:, 3072:4096]]
        self.out_dram = nc.dram_tensor("expert_rows", [EXPERTS * SLOTS, D], F32, kind="Internal").ap()
        self.gu_landed = [nc.alloc_semaphore(f"gate_up_landed_{i}") for i in range(4)]
        self.dn_landed = [nc.alloc_semaphore(f"down_landed_{i}") for i in range(4)]
        self.gathered = [nc.alloc_semaphore(f"rows_gathered_{i}") for i in range(2)]
        self.stored = [nc.alloc_semaphore(f"rows_stored_{i}") for i in range(2)]
        (self.rows_turned, self.rows_copied, self.up_done, self.silued, self.hidden_done, self.hidden_turned,
         self.hidden_copied, self.down_done, self.result_done, self.placed, self.table_read,
         self.shares_landed) = (nc.alloc_semaphore("sparse_" + n) for n in (
             "rows_turned", "rows_copied", "up_done", "silu_done", "hidden_done", "hidden_turned", "hidden_copied",
             "down_done", "result_done", "placed", "table_read", "shares_landed"))

    def load(self, sp, it, i, part):
        t = self.b.t["experts"]
        src = t[bass.ds(it * 4 + i, 1), :, 0:4096] if part == 0 else t[bass.ds(it * 4 + i, 1), :, 4096:6144]
        dst, landed = ((self.gu_at, self.gu_landed), (self.dn_at, self.dn_landed))[part]
        sp.dma_start(dst[i], src.rearrange("a p c -> (a p) c")).then_inc(landed[i], 16)

    def load_first(self, sp):
        for pair in range(2):
            for part in range(2):
                for e in range(2):
                    self.load(sp, 0, 2 * pair + e, part)

    def sync(self, sp):
        with sp.Fori(1, self.turns) as it:
            for pair in range(2):
                for part, used in enumerate((self.up_done, self.down_done)):
                    sp.wait_ge(used, it * 2 + pair - 1)
                    for e in range(2):
                        self.load(sp, it, 2 * pair + e, part)

    def tensor(self, pe):
        b = self.b
        with pe.Fori(0, self.turns) as it:
            for pair in range(2):
                n = it * 2 + pair + 1
                pe.wait_ge(self.gathered[pair], it * 16 + 16)
                for k in range(KT):
                    mm = pe.transpose(b.ps[:, k * P:(k + 1) * P], self.rows[pair][:, k * P:(k + 1) * P], b.ident)
                mm.then_inc(self.rows_turned, 1)
                pe.wait_ge(self.rows_copied, n)
                for e in range(2):
                    pe.wait_ge(self.gu_landed[2 * pair + e], it * 16 + 16)
                for k in range(KT):
                    for e in range(2):
                        r = slice(64 * e, 64 * e + 64)
                        mm = pe.matmul(b.bank(2)[r, :], self.rows_t[:, k, r], self.gu[2 * pair + e][:, k, :], start=k == 0, stop=k == KT - 1)
                mm.then_inc(self.up_done, 1)
                pe.wait_ge(self.hidden_done, n)
                for k in range(2):
                    mm = pe.transpose(b.bank(3)[:, k * P:(k + 1) * P], self.hidden[:, k * P:(k + 1) * P], b.ident)
                mm.then_inc(self.hidden_turned, 1)
                pe.wait_ge(self.hidden_copied, n)
                for e in range(2):
                    pe.wait_ge(self.dn_landed[2 * pair + e], it * 16 + 16)
                for half in range(2):
                    for k in range(2):
                        for e in range(2):
                            r = slice(64 * e, 64 * e + 64)
                            mm = pe.matmul(b.bank(4 + half)[r, :], self.hidden_t[:, k, r], self.dn[2 * pair + e][:, k, half * S:(half + 1) * S],
                                           start=k == 0, stop=k == 1)
                mm.then_inc(self.down_done, 1)

    def scalar(self, act):
        b = self.b
        with act.Fori(0, self.turns) as it:
            for pair in range(2):
                n = it * 2 + pair + 1
                act.wait_ge(self.rows_turned, n)
                act.activation(self.rows_t.rearrange("p k s -> p (k s)"), b.ps[:, 0:D], ACT.Copy).then_inc(self.rows_copied, 1)
                act.wait_ge(self.up_done, n)
                act.activation(self.silu_t, b.bank(2)[:, 0:256], ACT.Silu).then_inc(self.silued, 1)

    def vector(self, dve):
        b = self.b

        def turn(it, pair, first):
            n = it * 2 + pair + 1
            dve.wait_ge(self.silued, n)
            dve.tensor_tensor(self.hidden, b.bank(2)[:, 256:512], self.silu_t, ALU.mult).then_inc(self.hidden_done, 1)
            dve.wait_ge(self.hidden_turned, n)
            dve.tensor_copy(self.hidden_t.rearrange("p k s -> p (k s)"), b.bank(3)[:, 0:256]).then_inc(self.hidden_copied, 1)
            dve.wait_ge(self.down_done, n)
            if not first:
                dve.wait_ge(self.stored[pair], it * 16)
            dve.tensor_copy(self.result[pair], b.ps[:, 2048:3072]).then_inc(self.result_done, 1)

        for pair in range(2):
            turn(0, pair, True)
        with dve.Fori(1, self.turns) as it:
            for pair in range(2):
                turn(it, pair, False)

    def gpsimd(self, pool):
        b = self.b
        numbers = b.small[:, 80:84].bitcast(mybir.dt.uint32)
        for i in range(8):
            pool.indirect_dma_start(b.table_dram, bass.IndirectOffsetOnAxis(ap=b.slot_of[:, i:i + 1], axis=0),
                                    numbers[:, i % 4:i % 4 + 1], None).then_inc(self.placed, 16)
        pool.wait_ge(self.placed, 128)
        pool.dma_start(b.token_of, b.table_dram.rearrange("(c p) o -> p (c o)", p=P), allow_slow_non_contiguous=True).then_inc(self.table_read, 16)
        pool.wait_ge(self.table_read, 16)

        pairs = 2 * self.turns
        for n in range(pairs + 1):
            if n < pairs:
                if n >= 2:
                    pool.wait_ge(self.rows_turned, n - 1)
                    pool.wait_ge(self.gathered[n % 2], 16 * (n // 2))
                pool.indirect_dma_start(self.rows[n % 2], None, b.tokens_dram,
                                        bass.IndirectOffsetOnAxis(ap=b.token_of[:, n:n + 1], axis=0)).then_inc(self.gathered[n % 2], 16)
            if n >= 1:
                pool.wait_ge(self.result_done, n)
                pool.dma_start(self.out_dram[(n - 1) * P:n * P, :], self.result[(n - 1) % 2]).then_inc(self.stored[(n - 1) % 2], 16)
        for pair in range(2):
            pool.wait_ge(self.stored[pair], 16 * self.turns)
        for i in range(8):
            pool.indirect_dma_start(b.big[:, i * D:(i + 1) * D], None, self.out_dram,
                                    bass.IndirectOffsetOnAxis(ap=b.slot_of[:, i:i + 1], axis=0)).then_inc(self.shares_landed, 16)
        pool.wait_ge(self.shares_landed, 128)


def build(nc, tables):
    t = {}
    for name, a in tables.items():
        t[name[3:]] = nc.dram_tensor(name, a.shape, F32, kind="ExternalInput").ap()
    out = nc.dram_tensor("out", [S, D], F32, kind="ExternalOutput").ap()
    b = Builder(nc, t, out)
    b.start()
    b.modulation()
    for l in range(DEPTH):
        b.layer(l)
    b.second()


def kernel(**inputs):
    import concourse.bacc as bacc
    from concourse.bass_utils import run_bass_kernel_spmd

    tables = lay_out(inputs)
    nc = bacc.Bacc("TRN2", target_bir_lowering=False, num_devices=1)
    build(nc, tables)
    r = run_bass_kernel_spmd(nc, [tables], core_ids=[0])
    got = r.results[0]["out"]
    return got.reshape(1, S, D)
```
